# Optimizing a Trainium2 kernel written in Bass

```python
import jax, jax.numpy as jnp
from jax import lax
import numpy as np

D_MODEL = 2048
BATCH = 1
SEQ = 256
DEPTH = 1
DEC_BATCH = 1
DEC_SEQ = 32
PAST_LEN = 128

CHUNK = 64
HEAD_DIM = 128
SB_HEADS = 8
SWA_Q_HEADS = 8
SWA_KV_HEADS = 2
SWA_GROUP = SWA_Q_HEADS // SWA_KV_HEADS
WINDOW = 128
WINDOW_CHUNKS = WINDOW // CHUNK
ROPE_THETA = 10000.0
Q_BLOCK = 128
N_GROUPS = 4
EXPERTS_PER_GROUP = 4
N_EXPERTS = N_GROUPS * EXPERTS_PER_GROUP
TOP_K_IN_GROUP = 2
D_EXPERT = 512
RMS_EPS = 1e-6

SB_W = SB_HEADS * HEAD_DIM
SWA_QW = SWA_Q_HEADS * HEAD_DIM
SWA_KVW = SWA_KV_HEADS * HEAD_DIM
GATE_W = 2 * D_MODEL
IN_W = 3 * SB_W + SWA_QW + 2 * SWA_KVW + GATE_W
SPLIT_POINTS = (SB_W, 2 * SB_W, 3 * SB_W, 3 * SB_W + SWA_QW,
                3 * SB_W + SWA_QW + SWA_KVW, 3 * SB_W + SWA_QW + 2 * SWA_KVW)

kernel_name = 'stickbreak_swa_sink_hmoe_stream_step'

def rms_norm(x, g):
    x32 = x.astype(jnp.float32)
    y = x32 * lax.rsqrt(jnp.mean(x32 * x32, axis=-1, keepdims=True) + RMS_EPS)
    return (y * g.astype(jnp.float32)).astype(x.dtype)

def rope(x, pos):
    half = HEAD_DIM // 2
    inv = jnp.power(ROPE_THETA, -jnp.arange(half, dtype=jnp.float32) * (2.0 / HEAD_DIM))
    ang = pos.astype(jnp.float32)[:, None] * inv[None, :]
    cos = jnp.cos(ang)[None, :, None, :]
    sin = jnp.sin(ang)[None, :, None, :]
    x32 = x.astype(jnp.float32)
    x1, x2 = x32[..., :half], x32[..., half:]
    return jnp.concatenate([x1 * cos - x2 * sin, x2 * cos + x1 * sin], axis=-1).astype(x.dtype)

def stick_breaking(q, k, v, q_pos, k_pos):
    z = jnp.einsum('bqhd,bkhd->bhqk', q, k).astype(jnp.float32) * (HEAD_DIM ** -0.5)
    mask = k_pos[None, :] < q_pos[:, None]
    log_keep = jnp.where(mask, jax.nn.log_sigmoid(-z), 0.0)
    later = lax.cumsum(log_keep, axis=3, reverse=True) - log_keep
    a = jnp.where(mask, jnp.exp(jax.nn.log_sigmoid(z) + later), 0.0)
    return jnp.einsum('bhqk,bkhd->bqhd', a.astype(v.dtype), v)

def sb_prompt(q, k, v):
    s = q.shape[1]
    pos = jnp.arange(s, dtype=jnp.int32)
    outs = []
    for start in range(0, s, Q_BLOCK):
        end = start + Q_BLOCK
        outs.append(stick_breaking(q[:, start:end], k[:, :end], v[:, :end],
                                   pos[start:end], pos[:end]))
    return jnp.concatenate(outs, axis=1).reshape(q.shape[0], s, SB_W)

def sink_softmax(z, mask, sink):
    z = jnp.where(mask, z, -jnp.inf)
    m = jnp.maximum(jnp.max(z, axis=-1, keepdims=True), sink)
    e = jnp.exp(z - m)
    return e / (jnp.sum(e, axis=-1, keepdims=True) + jnp.exp(sink - m))

def swa_prompt(q, k, v, sink):
    b, s = q.shape[0], q.shape[1]
    nc = s // CHUNK
    qc = q.reshape(b, nc, CHUNK, SWA_KV_HEADS, SWA_GROUP, HEAD_DIM)
    kc = k.reshape(b, nc, CHUNK, SWA_KV_HEADS, HEAD_DIM)
    vc = v.reshape(b, nc, CHUNK, SWA_KV_HEADS, HEAD_DIM)

    def band(xc):
        parts = [jnp.pad(xc, ((0, 0), (w, 0), (0, 0), (0, 0), (0, 0)))[:, :nc]
                 for w in range(WINDOW_CHUNKS - 1, -1, -1)]
        return jnp.concatenate(parts, axis=2)

    kb, vb = band(kc), band(vc)
    offs = jnp.repeat(jnp.arange(WINDOW_CHUNKS - 1, -1, -1), CHUNK)
    mask = (jnp.arange(nc)[:, None] - offs[None, :]) >= 0
    z = jnp.einsum('bncxgd,bnkxd->bnxgck', qc, kb).astype(jnp.float32) * (HEAD_DIM ** -0.5)
    sink_b = sink.astype(jnp.float32).reshape(SWA_KV_HEADS, SWA_GROUP)[None, None, :, :, None, None]
    p = sink_softmax(z, mask[None, :, None, None, None, :], sink_b)
    o = jnp.einsum('bnxgck,bnkxd->bncxgd', p.astype(v.dtype), vb)
    return o.reshape(b, s, SWA_QW)

def swa_attend(q, k_all, v_all, sink, q_pos, k_pos):
    b, t = q.shape[0], q.shape[1]
    qg = q.reshape(b, t, SWA_KV_HEADS, SWA_GROUP, HEAD_DIM)
    z = jnp.einsum('btxgd,bkxd->bxgtk', qg, k_all).astype(jnp.float32) * (HEAD_DIM ** -0.5)
    dc = q_pos[:, None] // CHUNK - k_pos[None, :] // CHUNK
    mask = (dc >= 0) & (dc < WINDOW_CHUNKS)
    sink_b = sink.astype(jnp.float32).reshape(SWA_KV_HEADS, SWA_GROUP)[None, :, :, None, None]
    p = sink_softmax(z, mask, sink_b)
    o = jnp.einsum('bxgtk,bkxd->btxgd', p.astype(v_all.dtype), v_all)
    return o.reshape(b, t, SWA_QW)

def hier_moe(h, w_rg, b_rg, w_re, b_re, w_e_gate, w_e_up, w_e_down):
    hf = h.reshape(-1, D_MODEL)
    g_prob = jax.nn.softmax((hf @ w_rg).astype(jnp.float32) + b_rg.astype(jnp.float32), axis=-1)
    g_p, g_idx = lax.top_k(g_prob, 1)
    e_logits = ((hf @ w_re).astype(jnp.float32) + b_re.astype(jnp.float32)).reshape(
        -1, N_GROUPS, EXPERTS_PER_GROUP)
    e_in = jnp.take_along_axis(e_logits, g_idx[:, :, None], axis=1)[:, 0]
    e_val, e_idx = lax.top_k(e_in, TOP_K_IN_GROUP)
    e_w = jax.nn.softmax(e_val, axis=-1) * g_p
    expert_id = g_idx * EXPERTS_PER_GROUP + e_idx
    gate = jnp.sum(jax.nn.one_hot(expert_id, N_EXPERTS, dtype=jnp.float32) * e_w[..., None], axis=1)
    y = jnp.zeros(hf.shape, jnp.float32)
    for e in range(N_EXPERTS):
        a = jax.nn.silu(hf @ w_e_gate[e]) * (hf @ w_e_up[e])
        y = y + gate[:, e:e + 1] * (a @ w_e_down[e]).astype(jnp.float32)
    return y.astype(h.dtype).reshape(h.shape)

def mixer_inputs(x, g_mix, w_in):
    b, s = x.shape[0], x.shape[1]
    parts = jnp.split(rms_norm(x, g_mix) @ w_in, SPLIT_POINTS, axis=-1)
    q_sb = parts[0].reshape(b, s, SB_HEADS, HEAD_DIM)
    k_sb = parts[1].reshape(b, s, SB_HEADS, HEAD_DIM)
    v_sb = parts[2].reshape(b, s, SB_HEADS, HEAD_DIM)
    q_sw = parts[3].reshape(b, s, SWA_Q_HEADS, HEAD_DIM)
    k_sw = parts[4].reshape(b, s, SWA_KV_HEADS, HEAD_DIM)
    v_sw = parts[5].reshape(b, s, SWA_KV_HEADS, HEAD_DIM)
    return q_sb, k_sb, v_sb, q_sw, k_sw, v_sw, parts[6]

def merge_and_ffn(x, o_sb, o_sw, gate_pre, lp):
    g = jax.nn.sigmoid(gate_pre + lp['b_gate'])
    g_sb, g_sw = jnp.split(g, 2, axis=-1)
    x = x + (g_sb * (o_sb @ lp['w_sb_o']) + g_sw * (o_sw @ lp['w_swa_o'])) @ lp['w_out']
    return x + hier_moe(rms_norm(x, lp['g_ffn']), lp['w_rg'], lp['b_rg'], lp['w_re'], lp['b_re'],
                        lp['w_e_gate'], lp['w_e_up'], lp['w_e_down'])

def setup_inputs(seed: int = 0) -> dict:
    key = jax.random.key(seed)
    ks = jax.random.split(key, 24)
    f32 = jnp.float32

    def nrm(k, shape, scale):
        return jax.random.normal(k, shape, f32) * scale

    swa_len = min(WINDOW, PAST_LEN)
    return {
        'x_prompt': nrm(ks[0], (BATCH, SEQ, D_MODEL), 1.0),
        'x_sample': nrm(ks[1], (DEC_BATCH, DEC_SEQ, D_MODEL), 1.0),
        'cache_sb_k': nrm(ks[2], (DEPTH, DEC_BATCH, PAST_LEN, SB_HEADS, HEAD_DIM), 1.0),
        'cache_sb_v': nrm(ks[3], (DEPTH, DEC_BATCH, PAST_LEN, SB_HEADS, HEAD_DIM), 1.0),
        'cache_swa_k': nrm(ks[4], (DEPTH, DEC_BATCH, swa_len, SWA_KV_HEADS, HEAD_DIM), 1.0),
        'cache_swa_v': nrm(ks[5], (DEPTH, DEC_BATCH, swa_len, SWA_KV_HEADS, HEAD_DIM), 1.0),
        'w_in': nrm(ks[6], (DEPTH, D_MODEL, IN_W), D_MODEL ** -0.5),
        'b_gate': nrm(ks[7], (DEPTH, GATE_W), 0.1),
        'swa_sink': nrm(ks[8], (DEPTH, SWA_Q_HEADS), 0.5),
        'w_sb_o': nrm(ks[9], (DEPTH, SB_W, D_MODEL), SB_W ** -0.5),
        'w_swa_o': nrm(ks[10], (DEPTH, SWA_QW, D_MODEL), SWA_QW ** -0.5),
        'w_out': nrm(ks[11], (DEPTH, D_MODEL, D_MODEL), D_MODEL ** -0.5),
        'g_mix': 1.0 + nrm(ks[12], (DEPTH, D_MODEL), 0.01),
        'g_ffn': 1.0 + nrm(ks[13], (DEPTH, D_MODEL), 0.01),
        'w_rg': nrm(ks[14], (DEPTH, D_MODEL, N_GROUPS), D_MODEL ** -0.5),
        'b_rg': nrm(ks[15], (DEPTH, N_GROUPS), 0.01),
        'w_re': nrm(ks[16], (DEPTH, D_MODEL, N_EXPERTS), D_MODEL ** -0.5),
        'b_re': nrm(ks[17], (DEPTH, N_EXPERTS), 0.01),
        'w_e_gate': nrm(ks[18], (DEPTH, N_EXPERTS, D_MODEL, D_EXPERT), D_MODEL ** -0.5),
        'w_e_up': nrm(ks[19], (DEPTH, N_EXPERTS, D_MODEL, D_EXPERT), D_MODEL ** -0.5),
        'w_e_down': nrm(ks[20], (DEPTH, N_EXPERTS, D_EXPERT, D_MODEL), D_EXPERT ** -0.5),
        'g_final': 1.0 + nrm(ks[21], (D_MODEL,), 0.01),
    }

def reference(x_prompt, x_sample, cache_sb_k, cache_sb_v, cache_swa_k, cache_swa_v,
              w_in, b_gate, swa_sink, w_sb_o, w_swa_o, w_out, g_mix, g_ffn,
              w_rg, b_rg, w_re, b_re, w_e_gate, w_e_up, w_e_down, g_final):
    s = x_prompt.shape[1]
    t = x_sample.shape[1]
    past = cache_sb_k.shape[2]
    swa_past = cache_swa_k.shape[2]
    keep_p = min(WINDOW, s)
    pos_p = jnp.arange(s, dtype=jnp.int32)
    pos_s = past + jnp.arange(t, dtype=jnp.int32)
    pos_sb_keys = jnp.arange(past + t, dtype=jnp.int32)
    pos_swa_keys = jnp.concatenate(
        [past - swa_past + jnp.arange(swa_past, dtype=jnp.int32), pos_s])

    hp, hs = x_prompt, x_sample
    sbk_p, sbv_p, swk_p, swv_p = [], [], [], []
    sbk_s, sbv_s, swk_s, swv_s = [], [], [], []
    for l in range(DEPTH):
        lp = {'b_gate': b_gate[l], 'w_sb_o': w_sb_o[l], 'w_swa_o': w_swa_o[l], 'w_out': w_out[l],
              'g_ffn': g_ffn[l], 'w_rg': w_rg[l], 'b_rg': b_rg[l], 'w_re': w_re[l], 'b_re': b_re[l],
              'w_e_gate': w_e_gate[l], 'w_e_up': w_e_up[l], 'w_e_down': w_e_down[l]}

        q_sb, k_sb, v_sb, q_sw, k_sw, v_sw, gate_pre = mixer_inputs(hp, g_mix[l], w_in[l])
        q_sw = rope(q_sw, pos_p)
        k_sw = rope(k_sw, pos_p)
        o_sb = sb_prompt(q_sb, k_sb, v_sb)
        o_sw = swa_prompt(q_sw, k_sw, v_sw, swa_sink[l])
        hp = merge_and_ffn(hp, o_sb, o_sw, gate_pre, lp)
        sbk_p.append(k_sb)
        sbv_p.append(v_sb)
        swk_p.append(k_sw[:, s - keep_p:])
        swv_p.append(v_sw[:, s - keep_p:])

        q_sb, k_sb, v_sb, q_sw, k_sw, v_sw, gate_pre = mixer_inputs(hs, g_mix[l], w_in[l])
        q_sw = rope(q_sw, pos_s)
        k_sw = rope(k_sw, pos_s)
        k_sb_all = jnp.concatenate([cache_sb_k[l], k_sb], axis=1)
        v_sb_all = jnp.concatenate([cache_sb_v[l], v_sb], axis=1)
        o_sb = stick_breaking(q_sb, k_sb_all, v_sb_all, pos_s, pos_sb_keys).reshape(hs.shape[0], t, SB_W)
        k_sw_all = jnp.concatenate([cache_swa_k[l], k_sw], axis=1)
        v_sw_all = jnp.concatenate([cache_swa_v[l], v_sw], axis=1)
        o_sw = swa_attend(q_sw, k_sw_all, v_sw_all, swa_sink[l], pos_s, pos_swa_keys)
        hs = merge_and_ffn(hs, o_sb, o_sw, gate_pre, lp)
        sbk_s.append(k_sb)
        sbv_s.append(v_sb)
        swk_s.append(k_sw_all[:, t:])
        swv_s.append(v_sw_all[:, t:])

    y_prompt = rms_norm(hp, g_final)
    y_sample = rms_norm(hs, g_final)
    return (y_prompt, y_sample,
            jnp.stack(sbk_p), jnp.stack(sbv_p), jnp.stack(swk_p), jnp.stack(swv_p),
            jnp.stack(sbk_s), jnp.stack(sbv_s), jnp.stack(swk_s), jnp.stack(swv_s))


_drawn_inputs = setup_inputs


def setup_inputs(seed=0):
    import zlib

    import numpy as np

    out = dict(_drawn_inputs(seed))
    spreads = {}
    factors = {'swa_sink': 8.0,
     'g_mix': 5.806,
     'g_ffn': 3.711,
     'b_rg': 64.0,
     'b_re': 4.174,
     'g_final': 30.557}
    for name, (base, spread) in spreads.items():
        noise = np.random.default_rng([zlib.crc32(name.encode()), seed]).standard_normal(out[name].shape)
        drawn = base * np.exp(spread * noise) if base else spread * noise
        out[name] = __import__('jax').numpy.asarray(drawn.astype(out[name].dtype))
    for name, factor in factors.items():
        out[name] = (out[name] * factor).astype(out[name].dtype)
    return out
```

```python
from contextlib import ExitStack

import concourse.bass as bass
import numpy as np
from concourse import mybir

F32 = mybir.dt.float32
F32R = mybir.dt.float32r
I32 = mybir.dt.int32
U32 = mybir.dt.uint32
ACT = mybir.ActivationFunctionType
ALU = mybir.AluOpType
AX = mybir.AxisListType.X

P = 128
D = 2048
KT = D // P
SEQ, DEC, PAST = 256, 32, 128
NT = SEQ + DEC
NTP = 3 * P
TILES = (P, P, DEC)
HD = 128
H = 8
KV = 2
GRP = H // KV
CHUNK = 64
SBW = H * HD
GATE0 = 3 * SBW + H * HD + 2 * KV * HD
INW = GATE0 + 2 * D
NG, EPG = 4, 4
NE = NG * EPG
DE = 512
FT = DE // P
EPS = 1e-6
SCALE = HD ** -0.5
NEG = -1e30
SLOTS = 64
MAXOV = 2 * NT // SLOTS
NL = NG + NE
SBUF0 = 16640
PAIR = 2 * P
FAR = 1000.0

IT_QSB, IT_KSB, IT_VSB, IT_QSW, IT_KVSW, IT_ATT, IT_PROJ, IT_OUT, IT_END = 0, 2, 4, 6, 8, 9, 13, 21, 25

C_ID, C_TRI, C_SU, C_ONE = 0, 128, 256, 384
C_MSB = 512
SBC = 448
C_MSW = C_MSB + SBC
SWC = 384
C_MSS = C_MSW + SWC
SSC = 160
C_COS = C_MSS + SSC
C_SIN = C_COS + NT
C_I64 = C_SIN + NT
C_I16 = C_I64 + SLOTS
C_GRP = C_I16 + NE
C_VAL = C_GRP + NE
NC_ = C_VAL + 4


def constants():
    c = np.zeros((P, NC_), np.float32)
    r = np.arange(P)
    c[:, C_ID:C_ID + P] = np.eye(P)
    c[:, C_TRI:C_TRI + P] = r[:, None] >= r[None]
    c[:, C_SU:C_SU + P] = r[:, None] < r[None]
    c[:, C_ONE:C_ONE + P] = 1
    tri = np.where(r[:, None] < r[None], 0, NEG)
    c[:, C_MSB:C_MSB + P] = tri
    c[:, C_MSB + SEQ:C_MSB + SEQ + P] = tri
    c[:, C_MSB + SEQ + P + DEC:C_MSB + SBC] = tri[:, :DEC]
    for j, (q0, n) in enumerate(((0, P), (P, SEQ))):
        d = (q0 + r)[:, None] // CHUNK - np.arange(n)[None] // CHUNK
        at = C_MSW + j * P
        c[:, at:at + n] = np.where((d >= 0) & (d < 2), 0, NEG)
    d = (PAST + r % DEC)[:, None] // CHUNK - np.arange(SSC)[None] // CHUNK
    c[:, C_MSS:C_MSS + SSC] = np.where((d >= 0) & (d < 2), 0, NEG)
    half = HD // 2
    inv = np.power(np.float32(10000.0), -np.arange(half, dtype=np.float32) * np.float32(2.0 / HD))
    pos = np.concatenate([np.arange(SEQ), PAST + np.arange(DEC)]).astype(np.float32)
    ang = (pos[None] * inv[:, None].astype(np.float32)).astype(np.float32)
    c[:, C_COS:C_COS + NT] = np.tile(np.cos(ang), (2, 1))
    c[:half, C_SIN:C_SIN + NT] = np.sin(ang)
    c[half:, C_SIN:C_SIN + NT] = -np.sin(ang)
    c[:, C_I64:C_I64 + SLOTS] = np.arange(SLOTS)
    c[:, C_I16:C_I16 + NE] = np.arange(NE)
    c[:, C_GRP:C_GRP + NE] = np.arange(NE) // EPG
    for t, n in enumerate(TILES):
        c[:n, C_VAL + t] = 1
    return c


class Steps:

    def __init__(self, eng, sem):
        self.eng, self.sem, self.n, self.i, self.per, self.base = eng, sem, 0, None, 0, 0

    def at(self):
        return self.n if self.i is None else self.i * self.per + (self.base + self.n)

    def __call__(self, ins):
        ins.then_inc(self.sem, 1)
        self.n += 1

    def wait(self):
        if self.i is None and self.n == 0:
            return
        self.eng.wait_ge(self.sem, self.at())

    def enter(self, i, per):
        self.base, self.i, self.per, self.n = self.n, i, per, 0

    def leave(self, trips):
        assert self.n == self.per, (self.n, self.per)
        self.n, self.i = self.base + self.per * trips, None



def build(nc, x_prompt, x_sample, cache_sb_k, cache_sb_v, cache_swa_k, cache_swa_v, w_in, b_gate, swa_sink,
          w_sb_o, w_swa_o, w_out, g_mix, g_ffn, w_rg, b_rg, w_re, b_re, w_e_gate, w_e_up, w_e_down, g_final,
          const, y_prompt, y_sample, sb_kv_prompt, sb_kv_sample, swa_kv_prompt, swa_kv_new, swa_kv_kept):
    xT_spill = nc.dram_tensor("xT_spill", (P, KT * NT), F32, kind="Internal").ap()
    y_rows = nc.dram_tensor("y_rows", ((NE + MAXOV) * SLOTS, D), F32, kind="Internal").ap()

    def at(name, kb, shape, dt=F32):
        return nc.alloc_sbuf_tensor_at(name, shape, dt, offset=SBUF0 + int(kb * 1024))

    ring = at("ring", 0, [P, 2, KT, PAIR])
    wh = at("wh", 32, [P, 2, KT, P], F32R)
    wl = at("wl", 48, [P, 2, KT, P], F32R)
    xh = at("xh", 64, [P, KT, NT], F32R)
    xl = at("xl", 82, [P, KT, NT], F32R)
    kT_sb = at("kT_sb", 100, [P, H, NTP])
    v_sb = at("v_sb", 112, [P, 3, SBW])
    vc_sb = at("vc_sb", 124, [P, SBW])
    kcT_sb = at("kcT_sb", 128, [P, H, P])
    kT_sw = at("kT_sw", 132, [P, KV, NTP])
    v_sw = at("v_sw", 135, [P, 3, KV * HD])
    oh = at("oh", 100, [P, 2 * H, NT], F32R)
    ol = at("ol", 118, [P, 2 * H, NT], F32R)
    x_nat = at("x_nat", 138, [P, 3, D])
    squares = at("squares", 162, [P, D])
    kc_nat = at("kc_nat", 170, [P, SBW])
    headT = at("headT", 138, [P, 4, NTP])
    nat = at("nat", 144, [P, 3, 4 * P])
    gates = at("gates", 138, [P, KT, NT])
    qT = at("qT", 156, [P, 2 * H, NT])
    mh = at("mh", 138, [P, KT, NT], F32R)
    ml = at("ml", 156, [P, KT, NT], F32R)
    xT = at("xT", 174, [P, KT, NT])
    kcT_sw = at("kcT_sw", 174, [P, KV, P])
    vc_sw = at("vc_sw", 175, [P, KV * HD])
    kst = at("kst", 176, [P, 4, P])
    vst = at("vst", 178, [P, 4, P])
    qst = at("qst", 180, [P, SEQ])
    zm = at("zm", 181, [P, SBC])
    lg = at("lg", 182.75, [P, SBC])
    spb = at("spb", 184.5, [P, SBC])
    zw = at("zw", 186.25, [P, SWC])
    pT = at("pT", 187.75, [P, SWC])
    st = at("st", 189.25, [P, 16])
    kcw_nat = at("kcw_nat", 189.5, [P, KV * HD])
    rope_a = at("rope_a", 181, [P, NT])
    rope_b = at("rope_b", 182.25, [P, NT])
    zero = at("zero", 184, [P, 512])
    sg1 = at("sg1", 174, [P, NT])
    sg2 = at("sg2", 175.25, [P, NT])
    m1 = at("m1", 176.5, [P, NT])
    m2 = at("m2", 177.75, [P, NT])
    diag = at("diag", 32, [P, 3, P])
    rstd_b = at("rstd_b", 34, [P, NT])
    con = at("con", 192, [P, NC_])
    hbuf = at("hbuf", 201, [P, 2, NT])
    par = at("par", 203.5, [P, 64])
    par_nat = at("par_nat", 203.75, [64, P])
    wr = at("wr", 204.25, [P, KT, NL])
    sinks = at("sinks", 205.5, [P, H])
    sinks_s = at("sinks_s", 205.53125, [P, KV])
    br = at("br", 205.5625, [P, NL])
    stat = at("stat", 205.6875, [P, 16])
    slot_g = at("slot_g", 100, [P, KT, DE])
    slot_u = at("slot_u", 64, [P, KT, DE])
    slot_d = at("slot_d", 0, [P, FT, D])
    hg = at("hg", 32, [P, KT, SLOTS])
    y_sb = at("y_sb", 36, [SLOTS, D])
    sgl = at("sgl", 44, [P, FT, SLOTS])
    aT = at("aT", 45, [P, FT, SLOTS])
    pick = at("pick", 46, [P, 3, SLOTS])
    rt = at("rt", 47, [P, 768])
    ri = at("ri", 50, [P, 64], U32)
    rows = at("rows", 50.25, [P, 8], U32)
    ints = at("ints", 50.3125, [1, 16], I32)
    rk = at("rk", 50.5, [P, 3, NE + 1])
    rko = at("rko", 50.75, [P, 4])
    squares2 = at("squares2", 52, [P, D])
    x2 = at("x2", 138, [P, 3, D])
    gfin = at("gfin", 162, [P, D])
    ya = [at(f"ya{t}", 100 + 8 * t, [P, D]) for t in range(3)]
    yb = [at(f"yb{t}", 64 + 8 * t, [P, D]) for t in range(3)]

    c0 = [0]

    def cols(n, shape=None):
        a = c0[0]
        c0[0] += n
        v = rt[:, a:a + n]
        return v if shape is None else v.rearrange("p (a b) -> p a b", b=shape)
    lgt = cols(3 * NL, NL)
    gl8 = cols(24, 8)
    gm8 = cols(24, 8)
    em = cols(3 * NE, NE)
    em8 = cols(24, 8)
    gex = cols(3 * NG, NG)
    d21 = cols(3)
    gi = cols(3)
    gsum = cols(3)
    gp = cols(3)
    dn = cols(3)
    wt = cols(6, 3)
    ei = cols(6, 3)
    gmask = cols(3 * NE, NE)
    tmp = cols(3 * NE, NE)
    M1 = cols(3 * NE, NE)
    M2 = cols(3 * NE, NE)
    MM = cols(3 * NE, NE)
    rank = cols(3 * NE, NE)
    cnt = cols(NE)
    ov = cols(NE)
    ovc = cols(NE)
    ovx = cols(NE)
    sel = cols(MAXOV * NE, NE)
    se = cols(MAXOV)
    so = cols(MAXOV)
    rr = cols(6, 3)
    ro = cols(6, 3)
    assert c0[0] <= 768, c0[0]

    with ExitStack() as ctx:
        ps = [ctx.enter_context(nc.psum_tensor(f"bank{i}", [P, 512], F32)) for i in range(8)]
        names = """const_in x_in w_load0 w_load1 kc_in vc_in swc_in small_in xT_out act_own dve_own
                   rms diag_done rb_ps x_turned h_done xh_done xl_done xT_done par_ps par_sb kc_ps kc_sb pads
                   wh_ready wl_ready blk ev_a ev_d rope_done h_turned nat_done nat_out kept_out pool_head
                   kst_st vst_st qst_st z_sb z_sw zm_done zw_done l_done sp_done c_done e_done a_done
                   p_ready pT_ps pT_sb o_sb o_sw o_sb_ev o_sw_ev sums_done oh_done ol_done sig_done m_done mh_done
                   ml_done xT_in wr_scaled x2_ps x2_a x2_d ssq2 lg_ps masks rk_ps rk_done
                   g_in u_in d_in picked hg_ps hg_sb gate_ps up_ps silu_done a_ready dn_ps y_act y_dve y_out ov_out
                   zero_set zero_out rows_ready ints_ready gf_in y_in0 y_in1 y_in2 sum_done fin out_done
                   ex_in ex_out half_done ssq3 inv_done""".split()
        S = {n: ctx.enter_context(nc.semaphore(n)) for n in names}
        block = ctx.enter_context(nc.Block())
        ds = bass.ds
        v, a_ = nc.vector, nc.scalar

        def upto(it, j):
            return it * 4 + (j + 1)

        def tok(t):
            return slice(t * P, t * P + TILES[t])

        def flat(ap):
            return ap.rearrange("p a n -> p (a n)")

        def main(j):
            return ps[j % 2][:, 0:NT]

        def raw(j):
            return ring[:, j // 2, :, (j % 2) * P:(j % 2 + 1) * P]

        EV_KVSW_A, EV_KVSW_D = 1 + 24, 1 + 8
        EV_ATT = EV_KVSW_A + 2
        EV_PROJ = EV_ATT + 16
        EV_OUT_D = EV_KVSW_D + 2

        @block.sync
        def _(sp):
            sp.dma_start(x_nat[:, 0:2, :], x_prompt[0].rearrange("(t p) d -> p t d", p=P)).then_inc(S["x_in"], 16)
            sp.dma_start(x_nat[0:DEC, 2, :], x_sample[0]).then_inc(S["x_in"], 16)

            def load_pair(j, src):
                sp.dma_start(ring[:, j], src.rearrange("(k p) n -> p k n", p=P)).then_inc(S[f"w_load{j}"], 16)

            def slot_free(j, it):
                sp.wait_ge(S["wl_ready"], (it - 1) * 4 + (2 * j + 2))

            load_pair(0, w_in[0, :, 0:PAIR])
            load_pair(1, w_in[0, :, PAIR:2 * PAIR])
            with sp.Fori(1, IT_PROJ) as it:
                for j in range(2):
                    slot_free(j, it)
                    load_pair(j, w_in[0, :, ds(it * (2 * PAIR) + j * PAIR, PAIR)])
            with sp.Fori(IT_PROJ, IT_OUT) as it:
                slot_free(0, it)
                load_pair(0, w_in[0, :, ds(it * PAIR + (GATE0 + D - IT_PROJ * PAIR), PAIR)])
                slot_free(1, it)
                for k, w in enumerate((w_sb_o, w_swa_o)):
                    sp.dma_start(ring[:, 1, k * H:(k + 1) * H],
                                 w[0, :, ds((it - IT_PROJ) * PAIR, PAIR)].rearrange("(k p) n -> p k n", p=P))\
                        .then_inc(S["w_load1"], 16)
            with sp.Fori(IT_OUT, IT_END) as it:
                for j in range(2):
                    slot_free(j, it)
                    load_pair(j, w_out[0, :, ds((it - IT_OUT) * (2 * PAIR) + j * PAIR, PAIR)])

            def load(dst, w, e, sem):
                sp.dma_start(dst[:], w[0, ds(e, 1)].rearrange("a (k p) n -> p (a k) n", p=P)).then_inc(S[sem], 16)

            sp.wait_ge(S["blk"], upto(IT_OUT - 1, 3))
            load(slot_g, w_e_gate, 0, "g_in")
            load(slot_u, w_e_up, 0, "u_in")
            sp.wait_ge(S["wl_ready"], upto(IT_END - 1, 3))
            load(slot_d, w_e_down, 0, "d_in")

            def next_matrices(e, s):
                sp.wait_ge(S["gate_ps"], s)
                load(slot_g, w_e_gate, e, "g_in")
                sp.wait_ge(S["up_ps"], s)
                load(slot_u, w_e_up, e, "u_in")
                sp.wait_ge(S["dn_ps"], s)
                load(slot_d, w_e_down, e, "d_in")

            with sp.Fori(1, NE) as e:
                next_matrices(e, e)
            sp.wait_ge(S["ints_ready"], 1)
            more = sp.value_load(ints[0:1, MAXOV:MAXOV + 1], min_val=0, max_val=MAXOV)
            with sp.If(more > 0):
                with sp.Fori(0, more) as i:
                    e = sp.value_load(ints[0:1, ds(i, 1)], min_val=0, max_val=NE - 1)
                    next_matrices(e, i + NE)
            for t, n in enumerate(TILES):
                sp.wait_ge(S["fin"], t + 1)
                sp.dma_start(y_prompt[0, tok(t)] if t < 2 else y_sample[0], ya[t][0:n]).then_inc(S["out_done"], 16)
            sp.wait_ge(S["out_done"], 16 * 3)
            sp.wait_ge(S["nat_out"], 32 * 5)
            sp.wait_ge(S["kept_out"], 16 * 2)

        @block.gpsimd
        def _(pool):
            pool.dma_start(con[:], const).then_inc(S["const_in"], 16)
            for src, r0, r1 in ((b_gate, 0, 32), (g_mix, 32, 48), (g_ffn, 48, 64)):
                pool.dma_start(par_nat[r0:r1, :], src[0].rearrange("(r p) -> r p", p=P)).then_inc(S["const_in"], 16)
            pool.dma_start(kc_nat[:], cache_sb_k[0, 0].rearrange("s h d -> s (h d)")).then_inc(S["kc_in"], 16)
            pool.dma_start(vc_sb[:], cache_sb_v[0, 0].rearrange("s h d -> s (h d)")).then_inc(S["vc_in"], 16)
            pool.dma_start(sinks[:], swa_sink[0:1, :].to_broadcast([P, H])).then_inc(S["small_in"], 16)
            with nc.allow_non_contiguous_dma(reason="8 sinks"):
                for g in range(GRP):
                    for kv in range(KV):
                        pool.dma_start(sinks_s[DEC * g:DEC * g + DEC, kv:kv + 1],
                                       swa_sink[0:1, GRP * kv + g:GRP * kv + g + 1].to_broadcast([DEC, 1]))\
                            .then_inc(S["small_in"], 16)
            pool.dma_start(wr[:, :, 0:NG], w_rg[0].rearrange("(k p) n -> p k n", p=P)).then_inc(S["small_in"], 16)
            pool.dma_start(wr[:, :, NG:], w_re[0].rearrange("(k p) n -> p k n", p=P)).then_inc(S["small_in"], 16)
            pool.dma_start(br[:, 0:NG], b_rg[0:1, :].to_broadcast([P, NG])).then_inc(S["small_in"], 16)
            pool.dma_start(br[:, NG:], b_re[0:1, :].to_broadcast([P, NE])).then_inc(S["small_in"], 16)
            for n, c in enumerate((cache_swa_k, cache_swa_v)):
                pool.dma_start(swa_kv_kept[n], c[0, 0, DEC:PAST].rearrange("s h d -> s (h d)"))\
                    .then_inc(S["kept_out"], 16)
            pool.wait_ge(S["xT_out"], 16)
            pool.dma_start(kcw_nat[:], cache_swa_k[0, 0].rearrange("s h d -> s (h d)")).then_inc(S["swc_in"], 16)
            pool.dma_start(vc_sw[:], cache_swa_v[0, 0].rearrange("s h d -> s (h d)")).then_inc(S["swc_in"], 16)
            pool.memset(zero[:], 0.0).then_inc(S["zero_set"], 1)
            pool.wait_ge(S["zero_set"], 1)
            for r0, k in ((NE * SLOTS, 4), (NE * SLOTS + 4 * P, 0)):
                n, m = (P, k) if k else (MAXOV * SLOTS - 4 * P, 1)
                for q in range(m):
                    pool.dma_start(y_rows[r0 + q * P:r0 + q * P + n, :].rearrange("p (b n) -> p b n", n=512),
                                   zero[0:n, :].rearrange("p (a n) -> p a n", a=1).to_broadcast([n, 4, 512]))\
                        .then_inc(S["zero_out"], 16)

            def nat_store(i, src, dst_prompt, dst_sample):
                pool.wait_ge(S["nat_done"], i * 4 + 4)
                pool.dma_start(dst_prompt, src).then_inc(S["nat_out"], 16)
                pool.dma_start(dst_sample, nat[0:DEC, 2, :]).then_inc(S["nat_out"], 16)

            for n in range(2):
                with pool.Fori(0, 2) as ii:
                    i = ii + 2 * n
                    for j in range(4):
                        if n == 0:
                            pool.wait_ge(S["ev_a"], i * 4 + (1 + 8 + j + 1))
                            pool.tensor_copy(kT_sb[:, ds(ii * 4 + j, 1), 0:NT], headT[:, j:j + 1, 0:NT])\
                                .then_inc(S["pool_head"], 1)
                        else:
                            pool.wait_ge(S["nat_done"], i * 4 + (j + 1))
                            pool.tensor_copy(v_sb[:, :, ds(ii * (4 * P) + j * P, P)], nat[:, :, j * P:(j + 1) * P])\
                                .then_inc(S["pool_head"], 1)
                    nat_store(i, nat[:, 0:2, :],
                              sb_kv_prompt[ds(i, 1)].rearrange("a (t p) n -> p (a t) n", p=P),
                              sb_kv_sample[ds(i, 1)].rearrange("a p n -> p (a n)"))
            pool.wait_ge(S["nat_done"], 20)
            pool.tensor_copy(v_sw[:], nat[:, :, KV * HD:]).then_inc(S["pool_head"], 1)
            nat_store(4, nat[:, 1, :], swa_kv_prompt, swa_kv_new)

            pool.wait_ge(S["pool_head"], 17)
            pool.wait_ge(S["vc_in"], 16)
            pool.wait_ge(S["kc_sb"], 2)
            pool.wait_ge(S["rope_done"], 10)
            for g in range(KV):
                pool.tensor_copy(qst[:, g * P:(g + 1) * P].rearrange("p (h n) -> p h n", h=GRP),
                                 qT[:, H + GRP * g:H + GRP * g + GRP, SEQ:NT]).then_inc(S["qst_st"], 1)
            with pool.Fori(0, IT_PROJ - IT_ATT) as i:
                for u in range(2):
                    hd = i * 2 + u
                    pool.wait_ge(S["z_sb"], hd)
                    pool.tensor_copy(kst[:, 0:3, :], kT_sb[:, ds(hd, 1), :].rearrange("p a (t n) -> p (a t) n", n=P))\
                        .then_inc(S["kst_st"], 1)
                    pool.tensor_copy(kst[:, 3:4, :], kcT_sb[:, ds(hd, 1), :]).then_inc(S["kst_st"], 1)
                    pool.wait_ge(S["z_sw"], hd + KV)
                    pool.tensor_copy(qst[:].rearrange("p (a n) -> p a n", a=1),
                                     qT[:, ds(i + (H + GRP * u), 1), 0:SEQ]).then_inc(S["qst_st"], 1)
                    pool.wait_ge(S["o_sb"], hd)
                    pool.tensor_copy(vst[:, 0:3, :], v_sb[:, :, ds(hd * P, P)]).then_inc(S["vst_st"], 1)
                    pool.tensor_copy(vst[:, 3:4, :], vc_sb[:, ds(hd * P, P)].rearrange("p (a n) -> p a n", a=1))\
                        .then_inc(S["vst_st"], 1)
            pool.wait_ge(S["ml_done"], KT)
            pool.dma_start(xT[:], xT_spill.rearrange("p (k n) -> p k n", k=KT)).then_inc(S["xT_in"], 16)
            pool.wait_ge(S["blk"], upto(IT_END - 1, 3))
            pool.dma_start(gfin[:], g_final.rearrange("(a n) -> a n", a=1).to_broadcast([P, D]))\
                .then_inc(S["gf_in"], 16)
            with pool.Fori(0, NE) as e:
                pool.wait_ge(S["y_act"], e * 2 + 2)
                pool.wait_ge(S["y_dve"], e * 2 + 2)
                pool.dma_start(y_rows[ds(e * SLOTS, SLOTS), :], y_sb[:]).then_inc(S["y_out"], 16)
            pool.wait_ge(S["ints_ready"], 1)
            more = pool.value_load(ints[0:1, MAXOV:MAXOV + 1], min_val=0, max_val=MAXOV)
            pool.wait_ge(S["y_out"], 16 * NE)
            pool.wait_ge(S["zero_out"], 16 * 5)
            with pool.If(more > 0):
                with pool.Fori(0, more) as i:
                    pool.wait_ge(S["y_act"], i * 2 + (2 * NE + 2))
                    pool.wait_ge(S["y_dve"], i * 2 + (2 * NE + 2))
                    pool.dma_start(y_rows[ds(i * SLOTS + NE * SLOTS, SLOTS), :], y_sb[:]).then_inc(S["ov_out"], 16)
                    pool.wait_ge(S["ov_out"], i * 16 + 16)
            pool.wait_ge(S["rows_ready"], 1)
            for t, n in enumerate(TILES):
                for c, dst in enumerate((ya, yb)):
                    pool.indirect_dma_start(
                        dst[t][0:n, :], None, y_rows,
                        bass.IndirectOffsetOnAxis(ap=rows[0:n, 2 * t + c:2 * t + c + 1], axis=0))\
                        .then_inc(S[f"y_in{t}"], 16)

        @block.scalar
        def _(act):
            own = Steps(act, S["act_own"])
            act.wait_ge(S["dve_own"], 1)
            act.wait_ge(S["x_in"], 32)
            for t, n in enumerate(TILES):
                own.wait()
                own(a_.activation(squares[0:n], x_nat[0:n, t, :], ACT.Square, accum_out=stat[0:n, t:t + 1]))
            act.wait_ge(S["rms"], 1)
            a_.activation(stat[:, 4:7], stat[:, 4:7], ACT.Sqrt).then_inc(S["rms"], 1)
            act.wait_ge(S["par_ps"], 1)
            a_.activation(par[:], ps[1][:, 0:64], ACT.Copy).then_inc(S["par_sb"], 1)
            for n in range(2):
                act.wait_ge(S["kc_ps"], n + 1)
                a_.activation(kcT_sb[:, 4 * n:4 * n + 4, :], ps[5 + n][:].rearrange("p (h n) -> p h n", h=4), ACT.Copy)\
                    .then_inc(S["kc_sb"], 1)
            for k in range(KT):
                act.wait_ge(S["x_turned"], k + 1)
                a_.activation(xT[:, k, :], ps[2 + k % 3][:, 0:NT], ACT.Copy).then_inc(S["xT_done"], 1)
                act.wait_ge(S["h_done"], k + 1)
                a_.activation(xh[:, k, :], hbuf[:, k % 2, :], ACT.Copy).then_inc(S["xh_done"], 1)

            def split(j, loads):
                act.wait_ge(S[f"w_load{j // 2}"], loads)
                a_.activation(wh[:, j % 2], raw(j), ACT.Copy).then_inc(S["wh_ready"], 1)

            act.wait_ge(S["rb_ps"], 1)
            act.wait_ge(S["h_done"], KT)
            split(0, 16)
            split(1, 16)
            act.wait_ge(S["xT_done"], KT)
            act.dma_start(xT_spill.rearrange("p (k n) -> p k n", k=KT), xT[:]).then_inc(S["xT_out"], 16)
            own(a_.activation(stat[:, 12:13], stat[:, 8:9], ACT.Copy))
            a_.activation(stat[:, 13:14], stat[:, 8:9], ACT.Copy).then_inc(S["ev_a"], 1)

            def step(it, j, evac, loads1=None):
                act.wait_ge(S["blk"], upto(it, j))
                if evac:
                    evac()
                if j < 2:
                    split(j + 2, it * 16 + 16 if loads1 is None else loads1)
                else:
                    split(j - 2, it * 16 + 32)

            with act.Fori(IT_QSB, IT_KSB) as it:
                for j in range(4):
                    step(it, j, lambda: a_.activation(flat(qT[:, ds(it * 4 + j, 1), :]), main(j), ACT.Copy)
                         .then_inc(S["ev_a"], 1))
            act.wait_ge(S["pads"], 1)
            with act.Fori(0, 4) as i:
                for j in range(4):
                    if j == 0:
                        act.wait_ge(S["h_turned"], i * 4)
                        act.wait_ge(S["pool_head"], i * 4)
                    step(i + IT_KSB, j, lambda: a_.activation(headT[:, j, 0:NT], main(j), ACT.Copy)
                         .then_inc(S["ev_a"], 1))
            with act.Fori(IT_QSW, IT_KVSW) as it:
                for j in range(4):
                    step(it, j, None)
            act.wait_ge(S["h_turned"], 16)
            act.wait_ge(S["pool_head"], 16)
            for j in range(4):
                step(IT_KVSW, j, None if j < 2 else lambda: a_.activation(
                    headT[:, j, 0:NT], main(j), ACT.Copy).then_inc(S["ev_a"], 1))
            act.wait_ge(S["kc_ps"], 3)
            a_.activation(kcT_sw[:], ps[6][:, 0:KV * P].rearrange("p (h n) -> p h n", h=KV), ACT.Copy)\
                .then_inc(S["kc_sb"], 1)

            def softmax(segments, sink, n):
                act.wait_ge(S["zw_done"], n)
                for c, (a, b) in enumerate(segments):
                    a_.activation(zw[:, a:b], zw[:, a:b], ACT.Exp, bias=st[:, 2 + c:3 + c],
                                  accum_out=st[:, 4 + c:5 + c]).then_inc(S["sums_done"], 1)
                c = len(segments)
                a_.activation(st[:, 6:6 + c], st[:, 2:2 + c], ACT.Exp, bias=sink).then_inc(S["sums_done"], 1)

            act.wait_ge(S["small_in"], 16 * 13)
            for g in range(KV):
                softmax([(0, SSC)], sinks_s[:, g:g + 1], g + 1)
                act.wait_ge(S["pT_ps"], g + 1)
                if g:
                    act.wait_ge(S["o_sw"], g)
                a_.activation(pT[:, 0:P], ps[5][:, 0:P], ACT.Copy).then_inc(S["pT_sb"], 1)
                a_.activation(pT[0:DEC, P:2 * P], ps[5][0:DEC, P:2 * P], ACT.Copy).then_inc(S["pT_sb"], 1)
                act.wait_ge(S["o_sw"], g + 1)
                a_.activation(qT[:, H + GRP * g:H + GRP * g + GRP, SEQ:NT],
                              ps[7][:, 0:P].rearrange("p (h n) -> p h n", h=GRP), ACT.Copy)\
                    .then_inc(S["o_sw_ev"], 1)
            act.wait_ge(S["nat_out"], 32 * 5)
            act.wait_ge(S["pool_head"], 17)
            with act.Fori(0, IT_PROJ - IT_ATT) as i:
                own.enter(i, 4)
                for u in range(2):
                    hd = i * 2 + u
                    act.wait_ge(S["zm_done"], hd + 1)
                    own(a_.activation(lg[:], zm[:], ACT.Abs))
                    own.wait()
                    own(a_.activation(lg[:], lg[:], ACT.Exp, scale=-1.0))
                    own.wait()
                    a_.activation(lg[:], lg[:], ACT.Ln, bias=1.0).then_inc(S["l_done"], 1)
                    softmax([(0, P), (P, SWC)], sinks[:, ds(i + GRP * u, 1)], hd + (KV + 1))

                    def gate(j):
                        return lambda: a_.activation(flat(gates[:, ds(i * 4 + j, 1), :]), main(j), ACT.Identity,
                                                     bias=par[:, ds(i * 4 + j, 1)]).then_inc(S["ev_a"], 1)
                    step(i + IT_ATT, 2 * u, gate(2 * u))
                    act.wait_ge(S["e_done"], hd + 1)
                    a_.activation(spb[:], lg[:], ACT.Exp).then_inc(S["a_done"], 1)
                    act.wait_ge(S["pT_ps"], hd + (KV + 1))
                    act.wait_ge(S["o_sw"], hd + KV)
                    a_.activation(pT[:], ps[5][:, 0:SWC], ACT.Copy).then_inc(S["pT_sb"], 1)
                    step(i + IT_ATT, 2 * u + 1, gate(2 * u + 1))
                    act.wait_ge(S["o_sb"], hd + 1)
                    a_.activation(flat(qT[:, ds(hd, 1), :]), ps[6][:, 0:NT], ACT.Copy).then_inc(S["o_sb_ev"], 1)
                own.leave(IT_PROJ - IT_ATT)
            act.wait_ge(S["o_sw"], KV + H)
            act.wait_ge(S["vst_st"], 2 * H)
            act.wait_ge(S["o_sb_ev"], H)
            act.wait_ge(S["o_sw_ev"], KV + H)
            for h in range(2 * H):
                a_.activation(oh[:, h, :], qT[:, h, :], ACT.Copy).then_inc(S["oh_done"], 1)
            with act.Fori(0, IT_OUT - IT_PROJ) as i:
                it = i + IT_PROJ
                for j in range(2):
                    step(it, j, None, i * 32 + (16 * IT_PROJ + 32))
                for j in range(2):
                    m = i * 2 + j
                    act.wait_ge(S["m_done"], m)
                    a_.activation(sg1[:], flat(gates[:, ds(m, 1), :]), ACT.Sigmoid).then_inc(S["sig_done"], 1)
                    a_.activation(sg2[:], main(j), ACT.Sigmoid, bias=par[:, ds(m + KT, 1)]).then_inc(S["ev_a"], 1)

                    def high():
                        act.wait_ge(S["m_done"], m + 1)
                        a_.activation(flat(mh[:, ds((i + 1) * 2 + (j - 2), 1), :]), m1[:], ACT.Copy).then_inc(S["mh_done"], 1)
                    step(it, 2 + j, high)
            slot1 = 16 * IT_PROJ + 32 * (IT_OUT - IT_PROJ)
            with act.Fori(0, IT_END - IT_OUT - 1) as i:
                for j in range(4):
                    step(i + IT_OUT, j, None, i * 16 + (slot1 + 16))
            for j in range(2):
                step(IT_END - 1, j, None, slot1 + 16 * (IT_END - IT_OUT))
            for n in range(0, 12, 2):
                t, q = n // 4, n % 4
                act.wait_ge(S["x2_ps"], n + 1)
                a_.activation(x2[0:TILES[t], t, q * 512:(q + 1) * 512], ps[n % 4][0:TILES[t], :], ACT.Copy)\
                    .then_inc(S["x2_a"], 1)
                if q == 2:
                    act.wait_ge(S["x2_a"], 2 * t + 2)
                    act.wait_ge(S["x2_d"], 2 * t + 2)
                    if t:
                        act.wait_ge(S["ssq2"], t)
                    m = TILES[t]
                    a_.activation(squares2[0:m], x2[0:m, t, :], ACT.Square, accum_out=stat[0:m, t:t + 1])\
                        .then_inc(S["ssq2"], 1)
            act.wait_ge(S["rms"], 3)
            a_.activation(stat[:, 4:7], stat[:, 4:7], ACT.Sqrt).then_inc(S["rms"], 1)
            act.wait_ge(S["ex_in"], 1)
            a_.activation(gex, gex, ACT.Exp).then_inc(S["ex_out"], 1)
            act.wait_ge(S["ex_in"], 2)
            a_.activation(d21, d21, ACT.Exp).then_inc(S["ex_out"], 1)

            def expert(s):
                act.wait_ge(S["gate_ps"], s + 1)
                a_.activation(flat(sgl[:]), ps[2][:, 0:FT * SLOTS], ACT.Silu).then_inc(S["silu_done"], 1)
                act.wait_ge(S["dn_ps"], s + 1)
                for q in (0, 2):
                    a_.activation(y_sb[:, q * 512:(q + 1) * 512], ps[4 + q][0:SLOTS, :], ACT.Copy)\
                        .then_inc(S["y_act"], 1)

            with act.Fori(0, NE) as e:
                act.wait_ge(S["a_ready"], e)
                act.wait_ge(S["y_out"], e * 16)
                expert(e)
            act.wait_ge(S["y_out"], 16 * NE)
            act.wait_ge(S["ints_ready"], 1)
            more = act.value_load(ints[0:1, MAXOV:MAXOV + 1], min_val=0, max_val=MAXOV)
            with act.If(more > 0):
                with act.Fori(0, more) as i:
                    act.wait_ge(S["a_ready"], i + NE)
                    act.wait_ge(S["ov_out"], i * 16)
                    expert(i + NE)
            for t, n in enumerate(TILES):
                act.wait_ge(S["sum_done"], t + 1)
                a_.activation(yb[t][0:n], ya[t][0:n], ACT.Square, accum_out=stat[0:n, t:t + 1])\
                    .then_inc(S["ssq3"], 1)
                act.wait_ge(S["rms"], 5 + 2 * t)
                a_.activation(stat[0:n, 4 + t:5 + t], stat[0:n, 4 + t:5 + t], ACT.Sqrt).then_inc(S["rms"], 1)

        @block.tensor
        def _(pe):
            mm_, tr = nc.tensor.matmul, nc.tensor.transpose
            ident = con[:, C_ID:C_ID + P]
            ones = con[:, C_ONE:C_ONE + P]
            pe.wait_ge(S["const_in"], 16 * 4)
            tr(ps[1][:, 0:64], par_nat[:], ident[0:64, 0:64]).then_inc(S["par_ps"], 1)
            pe.wait_ge(S["kc_in"], 16)
            for n in range(2):
                for h in range(4):
                    k0 = (4 * n + h) * P
                    mm = tr(ps[5 + n][:, h * P:(h + 1) * P], kc_nat[:, k0:k0 + P], ident)
                mm.then_inc(S["kc_ps"], 1)
            pe.wait_ge(S["diag_done"], 3)
            for t, n in enumerate(TILES):
                mm = mm_(ps[7][:, 64 + t * P:64 + t * P + n], ones[0:n, :], diag[0:n, t, 0:n], start=True, stop=True)
            mm.then_inc(S["rb_ps"], 1)
            pe.wait_ge(S["x_in"], 32)
            for k in range(KT):
                if k >= 3:
                    pe.wait_ge(S["xT_done"], k - 2)
                for t, n in enumerate(TILES):
                    mm = tr(ps[2 + k % 3][:, t * P:t * P + n], x_nat[0:n, t, k * P:(k + 1) * P], ident[0:n, 0:n])
                mm.then_inc(S["x_turned"], 1)

            def products(it, j, hi, lo, sums=None):
                pe.wait_ge(S["wl_ready"], upto(it, j))
                for dst, k0, k1 in sums or ((main(j), 0, KT),):
                    for k in range(k0, k1):
                        mm_(dst, wh[:, j % 2, k, :], hi[:, k, :], start=(k == k0), stop=False)
                        mm_(dst, wh[:, j % 2, k, :], lo[:, k, :], start=False, stop=False)
                        mm = mm_(dst, wl[:, j % 2, k, :], hi[:, k, :], start=False, stop=(k == k1 - 1))
                mm.then_inc(S["blk"], 1)

            def turn(src, j):
                for t in range(3):
                    mm = tr(ps[5 + j % 2][:, t * P:(t + 1) * P], src[:, t * P:(t + 1) * P], ident)
                mm.then_inc(S["h_turned"], 1)

            pe.wait_ge(S["xl_done"], KT)
            with pe.Fori(IT_QSB, IT_KSB) as it:
                for j in range(4):
                    pe.wait_ge(S["ev_a"], it * 4 + j)
                    products(it, j, xh, xl)
            with pe.Fori(0, 4) as i:
                for j in range(4):
                    pe.wait_ge(S["ev_a"], i * 4 + (4 * IT_KSB + j))
                    products(i + IT_KSB, j, xh, xl)
                    if j:
                        pe.wait_ge(S["ev_a"], i * 4 + (4 * IT_KSB + 1 + j))
                        pe.wait_ge(S["nat_done"], i * 4 + max(j - 2, 0))
                        turn(headT[:, j - 1], j - 1)
                pe.wait_ge(S["ev_a"], i * 4 + (4 * IT_KSB + 5))
                pe.wait_ge(S["nat_done"], i * 4 + 2)
                turn(headT[:, 3], 3)
            with pe.Fori(0, 2) as i:
                for j in range(4):
                    if j < 2:
                        pe.wait_ge(S["ev_a"], 24 + j)
                    pe.wait_ge(S["ev_d"], i * 4 + j)
                    products(i + IT_QSW, j, xh, xl)
            for j in range(4):
                pe.wait_ge(S["ev_d"], EV_KVSW_D - 1 + j)
                products(IT_KVSW, j, xh, xl)
                if j:
                    if j < 3:
                        pe.wait_ge(S["rope_done"], 8 + j)
                    else:
                        pe.wait_ge(S["ev_a"], EV_KVSW_A + 1)
                    pe.wait_ge(S["nat_done"], 16 + max(j - 2, 0))
                    turn(kT_sw[:, j - 1] if j < 3 else headT[:, 2], j - 1)
            pe.wait_ge(S["ev_a"], EV_ATT)
            pe.wait_ge(S["nat_done"], 18)
            turn(headT[:, 3], 3)
            pe.wait_ge(S["swc_in"], 32)
            pe.wait_ge(S["nat_done"], 20)
            for g in range(KV):
                mm = tr(ps[6][:, g * P:(g + 1) * P], kcw_nat[:, g * P:(g + 1) * P], ident)
            mm.then_inc(S["kc_ps"], 1)
            pe.wait_ge(S["kc_sb"], 3)
            pe.wait_ge(S["pool_head"], 17)
            for g in range(KV):
                pe.wait_ge(S["zw_done"], g)
                pe.wait_ge(S["qst_st"], g + 1)
                lhs = qst[:, g * P:(g + 1) * P]
                mm_(ps[4][:, 0:P], lhs, kcT_sw[:, g, :], start=True, stop=True)
                mm_(ps[4][:, P:SSC], lhs, kT_sw[:, g, SEQ:NT], start=True, stop=True).then_inc(S["z_sw"], 1)
                pe.wait_ge(S["p_ready"], g + 1)
                pe.wait_ge(S["pT_sb"], 2 * g)
                tr(ps[5][:, 0:P], zw[:, 0:P], ident)
                tr(ps[5][0:DEC, P:2 * P], zw[:, P:SSC], ident).then_inc(S["pT_ps"], 1)
                pe.wait_ge(S["pT_sb"], 2 * g + 2)
                pe.wait_ge(S["o_sw_ev"], g)
                mm_(ps[7][:, 0:P], vc_sw[:, g * P:(g + 1) * P], pT[:, 0:P], start=True, stop=False)
                mm_(ps[7][:, 0:P], v_sw[0:DEC, 2, g * P:(g + 1) * P], pT[0:DEC, P:2 * P], start=False, stop=True)\
                    .then_inc(S["o_sw"], 1)

            with pe.Fori(0, IT_PROJ - IT_ATT) as i:
                for u in range(2):
                    hd = i * 2 + u

                    def q(a, b):
                        return flat(qT[:, ds(hd, 1), a:b])

                    def gate_block(j):
                        pe.wait_ge(S["ev_a"], i * 4 + (EV_ATT - 1 + j))
                        products(i + IT_ATT, j, xh, xl)

                    pe.wait_ge(S["kst_st"], hd * 2 + 2)
                    pe.wait_ge(S["zm_done"], hd)
                    mm_(ps[2][:, 0:SEQ], kst[:, 0, :], q(0, SEQ), start=True, stop=True)
                    mm_(ps[2][:, SEQ:SEQ + P], kst[:, 1, :], q(P, SEQ), start=True, stop=True)
                    mm_(ps[2][:, SEQ + P:SEQ + P + DEC], kst[:, 3, :], q(SEQ, NT), start=True, stop=True)
                    mm_(ps[2][:, SEQ + P + DEC:SBC], kst[:, 2, :], q(SEQ, NT), start=True, stop=True)\
                        .then_inc(S["z_sb"], 1)
                    pe.wait_ge(S["qst_st"], hd + (KV + 1))
                    pe.wait_ge(S["zw_done"], hd + KV)
                    mm_(ps[4][:, 0:P], qst[:, 0:P], kT_sw[:, u, 0:P], start=True, stop=True)
                    mm_(ps[4][:, P:SWC], qst[:, P:SEQ], kT_sw[:, u, 0:SEQ], start=True, stop=True)\
                        .then_inc(S["z_sw"], 1)
                    gate_block(2 * u)
                    pe.wait_ge(S["sp_done"], hd + 1)
                    pe.wait_ge(S["e_done"], hd)
                    mm_(ps[3][:, 0:SBC], con[:, C_TRI:C_TRI + P], spb[:], start=True, stop=False)
                    mm_(ps[3][:, P:SEQ], ones, spb[:, SEQ:SEQ + P], start=False, stop=False)
                    mm_(ps[3][:, SEQ + P:SEQ + P + DEC], ones, spb[:, SEQ + P + DEC:SBC], start=False, stop=True)\
                        .then_inc(S["c_done"], 1)
                    pe.wait_ge(S["p_ready"], hd + (KV + 1))
                    pe.wait_ge(S["pT_sb"], hd + 2 * KV)
                    for c in range(3):
                        mm = tr(ps[5][:, c * P:(c + 1) * P], zw[:, c * P:(c + 1) * P], ident)
                    mm.then_inc(S["pT_ps"], 1)
                    gate_block(2 * u + 1)
                    pe.wait_ge(S["a_done"], hd + 1)
                    pe.wait_ge(S["vst_st"], hd * 2 + 2)
                    pe.wait_ge(S["o_sb_ev"], hd)
                    mm_(ps[6][:, 0:SEQ], vst[:, 0, :], spb[:, 0:SEQ], start=True, stop=False, skip_group_check=True)
                    mm_(ps[6][:, P:SEQ], vst[:, 1, :], spb[:, SEQ:SEQ + P], start=False, stop=False,
                        skip_group_check=True)
                    mm_(ps[6][:, SEQ:NT], vst[:, 3, :], spb[:, SEQ + P:SEQ + P + DEC], start=False, stop=False,
                        skip_group_check=True)
                    mm_(ps[6][:, SEQ:NT], vst[:, 2, :], spb[:, SEQ + P + DEC:SBC], start=False, stop=True,
                        skip_group_check=True).then_inc(S["o_sb"], 1)
                    pe.wait_ge(S["pT_sb"], hd + (2 * KV + 1))
                    pe.wait_ge(S["o_sw_ev"], hd + KV)
                    mm_(ps[7][:, 0:SEQ], v_sw[:, 0, u * P:(u + 1) * P], pT[:, 0:SEQ], start=True, stop=False)
                    mm_(ps[7][:, P:SEQ], v_sw[:, 1, u * P:(u + 1) * P], pT[:, SEQ:SWC], start=False, stop=True)\
                        .then_inc(S["o_sw"], 1)

            with pe.Fori(0, IT_OUT - IT_PROJ) as i:
                it = i + IT_PROJ
                for j in range(2):
                    pe.wait_ge(S["ev_a"], i * 2 + (EV_PROJ - 1 + j))
                    products(it, j, xh, xl)
                pe.wait_ge(S["ol_done"], 2 * H)
                pe.wait_ge(S["m_done"], i * 2)
                for j in range(2):
                    products(it, 2 + j, oh, ol, ((ps[2 + j][:, 0:NT], 0, H), (ps[4 + j][:, 0:NT], H, 2 * H)))
            pe.wait_ge(S["ev_a"], EV_PROJ + 16)
            pe.wait_ge(S["ml_done"], KT)
            with pe.Fori(0, IT_END - IT_OUT) as i:
                for j in range(4):
                    pe.wait_ge(S["ev_d"], i * 4 + (EV_OUT_D - 1 + j))
                    products(i + IT_OUT, j, mh, ml)
            pe.wait_ge(S["ev_d"], EV_OUT_D + KT)
            for n in range(12):
                t, q = n // 4, n % 4
                if n >= 4:
                    pe.wait_ge(S["x2_d" if n % 2 else "x2_a"], n // 2 - 1)
                for k in range(4):
                    mm = tr(ps[n % 4][0:TILES[t], k * P:(k + 1) * P], xT[:, 4 * q + k, tok(t)], ident)
                mm.then_inc(S["x2_ps"], 1)
            pe.wait_ge(S["wr_scaled"], 1)
            for t, n in enumerate(TILES):
                for k in range(KT):
                    mm = mm_(ps[7][0:n, t * 32:t * 32 + NL], xT[:, k, tok(t)], wr[:, k, :],
                             start=(k == 0), stop=(k == KT - 1))
            mm.then_inc(S["lg_ps"], 1)
            pe.wait_ge(S["masks"], 1)
            su = con[:, C_SU:C_SU + P]
            for t in range(3):
                for s in range(t + 1):
                    mm_(ps[6][:, t * NE:(t + 1) * NE], su if s == t else ones, MM[:, s, :],
                        start=(s == 0), stop=(s == t))
            for s in range(3):
                mm = mm_(ps[6][:, 3 * NE:4 * NE], ones, MM[:, s, :], start=(s == 0), stop=(s == 2))
            mm.then_inc(S["rk_ps"], 1)

            def gather(picks, free):
                pe.wait_ge(S["picked"], picks)
                pe.wait_ge(S["hg_sb"], free)
                for k in range(KT):
                    for t, n in enumerate(TILES):
                        mm = mm_(ps[k // 8][:, (k % 8) * SLOTS:(k % 8 + 1) * SLOTS], x2[0:n, t, k * P:(k + 1) * P],
                                 pick[0:n, t, :], start=(t == 0), stop=(t == 2))
                mm.then_inc(S["hg_ps"], 1)

            def up_gate(s, gathered):
                pe.wait_ge(S["hg_sb"], gathered)
                pe.wait_ge(S["a_ready"], s)
                for sem, w, bank, done in (("g_in", slot_g, 2, "gate_ps"), ("u_in", slot_u, 3, "up_ps")):
                    pe.wait_ge(S[sem], s * 16 + 16)
                    for f in range(FT):
                        for k in range(KT):
                            mm = mm_(ps[bank][:, f * SLOTS:(f + 1) * SLOTS], w[:, k, f * P:(f + 1) * P], hg[:, k, :],
                                     start=(k == 0), stop=(k == KT - 1))
                    mm.then_inc(S[done], 1)

            def down(s):
                pe.wait_ge(S["d_in"], s * 16 + 16)
                pe.wait_ge(S["a_ready"], s + 1)
                pe.wait_ge(S["y_act"], s * 2)
                pe.wait_ge(S["y_dve"], s * 2)
                for f in range(FT):
                    for q in range(4):
                        mm = mm_(ps[4 + q][0:SLOTS, :], aT[:, f, :], slot_d[:, f, q * 512:(q + 1) * 512],
                                 start=(f == 0), stop=(f == FT - 1))
                mm.then_inc(S["dn_ps"], 1)

            pe.wait_ge(S["rk_done"], 1)
            gather(3, 0)
            with pe.Fori(0, NE) as e:
                up_gate(e, e * 2 + 2)
                gather(e * 3 + 6, e * 2 + 2)
                down(e)
            pe.wait_ge(S["ints_ready"], 1)
            more = pe.value_load(ints[0:1, MAXOV:MAXOV + 1], min_val=0, max_val=MAXOV)
            with pe.If(more > 0):
                with pe.Fori(0, more) as i:
                    gather(i * 3 + (3 * NE + 6), i * 2 + (2 * NE + 2))
                    up_gate(i + NE, i * 2 + (2 * NE + 4))
                    down(i + NE)

        @block.vector
        def _(dve):
            own = Steps(dve, S["dve_own"])

            def then(ins):
                own(ins)
                own.wait()

            then(v.memset(stat[:], 1.0))

            def rms():
                v.tensor_scalar(stat[:, 4:7], stat[:, 0:3], 1.0 / D, EPS, ALU.mult, ALU.add).then_inc(S["rms"], 1)

            dve.wait_ge(S["act_own"], 3)
            rms()
            dve.wait_ge(S["rms"], 2)
            then(v.reciprocal(stat[:, 8:11], stat[:, 4:7]))
            dve.wait_ge(S["const_in"], 16 * 4)
            for t in range(3):
                v.tensor_scalar(diag[:, t, :], con[:, C_ID:C_ID + P], stat[:, 8 + t:9 + t], None, ALU.mult)\
                    .then_inc(S["diag_done"], 1)
            dve.wait_ge(S["rb_ps"], 1)
            then(v.tensor_copy(rstd_b[:], ps[7][:, 64:64 + NT]))
            dve.wait_ge(S["par_sb"], 1)

            def low(k):
                dve.wait_ge(S["xh_done"], k + 1)
                v.tensor_tensor(xl[:, k, :], hbuf[:, k % 2, :], xh[:, k, :].bitcast(F32), ALU.subtract)\
                    .then_inc(S["xl_done"], 1)

            for k in range(KT):
                dve.wait_ge(S["xT_done"], k + 1)
                if k > 1:
                    dve.wait_ge(S["xl_done"], k - 1)
                v.scalar_tensor_tensor(out=hbuf[:, k % 2, :], in0=xT[:, k, :], scalar=par[:, 32 + k:33 + k],
                                       in1=rstd_b[:], op0=ALU.mult, op1=ALU.mult).then_inc(S["h_done"], 1)
                if k:
                    low(k - 1)
            low(KT - 1)

            def split(j, b):
                dve.wait_ge(S["wh_ready"], b)
                v.tensor_tensor(wl[:, j % 2], raw(j), wh[:, j % 2].bitcast(F32), ALU.subtract)\
                    .then_inc(S["wl_ready"], 1)

            split(0, 1)
            split(1, 2)
            own(v.memset(headT[:, :, NT:], 0.0))
            v.memset(kT_sb[:, :, NT:], 0.0).then_inc(S["ev_d"], 1)
            v.memset(kT_sw[:, :, NT:], 0.0).then_inc(S["pads"], 1)
            with dve.Fori(IT_QSB, IT_KSB) as it:
                for j in range(4):
                    split((j + 2) % 4, it * 4 + (j + 3))

            def token_major(n, j):
                dve.wait_ge(S["h_turned"], n)
                v.tensor_copy(nat[:, :, j * P:(j + 1) * P], ps[5 + j % 2][:, 0:3 * P].rearrange("p (t n) -> p t n", t=3))\
                    .then_inc(S["nat_done"], 1)

            with dve.Fori(0, 4) as i:
                for j in range(4):
                    if j == 1:
                        dve.wait_ge(S["nat_out"], i * 32)
                        dve.wait_ge(S["pool_head"], i * 4)
                    if j:
                        token_major(i * 4 + j, j - 1)
                    if j == 3:
                        token_major(i * 4 + 4, 3)
                    split((j + 2) % 4, i * 4 + (4 * IT_KSB + j + 3))

            def rotary(j):
                h = HD // 2
                src = main(j)
                own(v.tensor_tensor(rope_a[:], src, con[:, C_COS:C_COS + NT], ALU.mult))
                own(v.tensor_tensor(rope_b[0:h], src[h:P], con[h:P, C_SIN:C_SIN + NT], ALU.mult))
                v.tensor_tensor(rope_b[h:P], src[0:h], con[0:h, C_SIN:C_SIN + NT], ALU.mult).then_inc(S["ev_d"], 1)
                own.wait()

            dve.wait_ge(S["xT_out"], 16)
            with dve.Fori(0, 2) as i:
                own.enter(i, 8)
                for j in range(4):
                    dve.wait_ge(S["blk"], i * 4 + (4 * IT_QSW + j + 1))
                    dve.wait_ge(S["rope_done"], i * 4 + j)
                    rotary(j)
                    dve.wait_ge(S["ev_d"], i * 4 + (j + 2))
                    v.tensor_tensor(flat(qT[:, ds(i * 4 + (H + j), 1), :]), rope_a[:], rope_b[:], ALU.add)\
                        .then_inc(S["rope_done"], 1)
                    split((j + 2) % 4, i * 4 + (4 * IT_QSW + j + 3))
                own.leave(2)
            for j in range(4):
                if j < 2:
                    dve.wait_ge(S["blk"], upto(IT_KVSW, j))
                    dve.wait_ge(S["rope_done"], 8 + j)
                    rotary(j)
                    dve.wait_ge(S["ev_d"], EV_KVSW_D + 1 + j)
                    v.tensor_tensor(kT_sw[:, j, 0:NT], rope_a[:], rope_b[:], ALU.add).then_inc(S["rope_done"], 1)
                if j == 1:
                    dve.wait_ge(S["nat_out"], 32 * 4)
                    dve.wait_ge(S["pool_head"], 16)
                if j:
                    token_major(16 + j, j - 1)
                if j == 3:
                    token_major(20, 3)
                split((j + 2) % 4, upto(IT_KVSW, j + 2))

            def scores(n, width, mask, segments, sinks_of):
                dve.wait_ge(S["z_sw"], n)
                if not isinstance(n, int) or n > 1:
                    dve.wait_ge(S["pT_ps"], n - 1)
                then(v.scalar_tensor_tensor(out=zw[:, 0:width], in0=ps[4][:, 0:width], scalar=SCALE,
                                            in1=con[:, mask:mask + width], op0=ALU.mult, op1=ALU.add))
                for c, (a, b) in enumerate(segments):
                    own(v.tensor_reduce(st[:, c:c + 1], zw[:, a:b], AX, ALU.max))
                own.wait()
                c = len(segments)
                v.tensor_scalar(st[:, 2:2 + c], st[:, 0:c], sinks_of, -1.0, ALU.max, ALU.mult).then_inc(S["zw_done"], 1)

            def divide(sums, segments):
                dve.wait_ge(S["sums_done"], sums)
                c = len(segments)
                then(v.tensor_tensor(st[:, 8:8 + c], st[:, 4:4 + c], st[:, 6:6 + c], ALU.add))
                then(v.reciprocal(st[:, 10:10 + c], st[:, 8:8 + c]))
                for n, (a, b) in enumerate(segments):
                    ins = v.tensor_scalar(zw[:, a:b], zw[:, a:b], st[:, 10 + n:11 + n], None, ALU.mult)
                    if n == c - 1:
                        ins.then_inc(S["p_ready"], 1)

            dve.wait_ge(S["small_in"], 16 * 13)
            for g in range(KV):
                scores(g + 1, SSC, C_MSS, [(0, SSC)], sinks_s[:, g:g + 1])
                divide(2 * g + 2, [(0, SSC)])
            heads = [(0, P), (P, SWC)]
            dve.wait_ge(S["zero_out"], 16 * 5)
            with dve.Fori(0, IT_PROJ - IT_ATT) as i:
                own.enter(i, 10)
                for u in range(2):
                    hd = i * 2 + u
                    dve.wait_ge(S["z_sb"], hd + 1)
                    v.scalar_tensor_tensor(out=zm[:], in0=ps[2][:, 0:SBC], scalar=SCALE, in1=con[:, C_MSB:C_MSB + SBC],
                                           op0=ALU.mult, op1=ALU.add).then_inc(S["zm_done"], 1)
                    scores(hd + (KV + 1), SWC, C_MSW, heads, sinks[:, ds(i + GRP * u, 1)])
                    dve.wait_ge(S["l_done"], hd + 1)
                    dve.wait_ge(S["o_sb"], hd)
                    v.scalar_tensor_tensor(out=spb[:], in0=zm[:], scalar=0.0, in1=lg[:], op0=ALU.max, op1=ALU.add)\
                        .then_inc(S["sp_done"], 1)
                    divide(hd * 3 + (2 * KV + 3), heads)
                    split((2 * u + 2) % 4, i * 4 + (4 * IT_ATT + 2 * u + 3))
                    dve.wait_ge(S["c_done"], hd + 1)
                    v.tensor_tensor(lg[:], zm[:], ps[3][:, 0:SBC], ALU.subtract).then_inc(S["e_done"], 1)
                    split((2 * u + 3) % 4, i * 4 + (4 * IT_ATT + 2 * u + 4))
                    dve.wait_ge(S["o_sw"], hd + (KV + 1))
                    v.tensor_copy(flat(qT[:, ds(i + (H + GRP * u), 1), 0:SEQ]), ps[7][:, 0:SEQ])\
                        .then_inc(S["o_sw_ev"], 1)
                own.leave(IT_PROJ - IT_ATT)
            for h in range(2 * H):
                dve.wait_ge(S["oh_done"], h + 1)
                v.tensor_tensor(ol[:, h, :], qT[:, h, :], oh[:, h, :].bitcast(F32), ALU.subtract)\
                    .then_inc(S["ol_done"], 1)
            with dve.Fori(0, IT_OUT - IT_PROJ) as i:
                own.enter(i, 4)
                for j in range(2):
                    split(j + 2, i * 4 + (4 * IT_PROJ + j + 3))
                for j in range(2):
                    m = i * 2 + j
                    dve.wait_ge(S["sig_done"], m + 1)
                    dve.wait_ge(S["blk"], i * 4 + (4 * IT_PROJ + 3 + j))
                    dve.wait_ge(S["ml_done"], m)
                    own(v.tensor_tensor(m1[:], sg1[:], ps[2 + j][:, 0:NT], ALU.mult))
                    dve.wait_ge(S["ev_a"], m + (EV_PROJ + 1))
                    own(v.tensor_tensor(m2[:], sg2[:], ps[4 + j][:, 0:NT], ALU.mult))
                    own.wait()
                    v.tensor_tensor(m1[:], m1[:], m2[:], ALU.add).then_inc(S["m_done"], 1)
                    dve.wait_ge(S["mh_done"], m + 1)
                    v.tensor_tensor(flat(ml[:, ds(m, 1), :]), m1[:], flat(mh[:, ds(m, 1), :]).bitcast(F32),
                                    ALU.subtract).then_inc(S["ml_done"], 1)
                    split(j, i * 4 + (4 * IT_PROJ + j + 5))
                own.leave(IT_OUT - IT_PROJ)
            dve.wait_ge(S["xT_in"], 16)

            def residual(it, j, m):
                dve.wait_ge(S["blk"], upto(it, j))
                v.tensor_tensor(m, m, main(j), ALU.add).then_inc(S["ev_d"], 1)

            with dve.Fori(0, IT_END - IT_OUT - 1) as i:
                for j in range(4):
                    residual(i + IT_OUT, j, flat(xT[:, ds(i * 4 + j, 1), :]))
                    split((j + 2) % 4, i * 4 + (4 * IT_OUT + j + 3))
            for j in range(4):
                residual(IT_END - 1, j, xT[:, KT - 4 + j, :])
                if j < 2:
                    split(j + 2, upto(IT_END - 1, j + 2))
                if j == 2:
                    v.tensor_tensor(wr[:], wr[:], par[:, 48:64].rearrange("p (k a) -> p k a", a=1)
                                    .to_broadcast([P, KT, NL]), ALU.mult).then_inc(S["wr_scaled"], 1)
            for n in range(1, 12, 2):
                t, q = n // 4, n % 4
                dve.wait_ge(S["x2_ps"], n + 1)
                v.tensor_copy(x2[0:TILES[t], t, q * 512:(q + 1) * 512], ps[n % 4][0:TILES[t], :])\
                    .then_inc(S["x2_d"], 1)
            own(v.memset(lgt, 0.0))
            own(v.memset(rk[:], -FAR))
            own(v.memset(gl8, NEG))
            dve.wait_ge(S["ssq2"], 3)
            rms()
            dve.wait_ge(S["rms"], 4)
            then(v.reciprocal(stat[:, 8:11], stat[:, 4:7]))
            dve.wait_ge(S["lg_ps"], 1)
            for t, n in enumerate(TILES):
                own(v.scalar_tensor_tensor(out=lgt[0:n, t, :], in0=ps[7][0:n, t * 32:t * 32 + NL],
                                           scalar=stat[0:n, 8 + t:9 + t], in1=br[0:n], op0=ALU.mult, op1=ALU.add))
            own.wait()
            then(v.tensor_copy(gl8[:, :, 0:NG], lgt[:, :, 0:NG]))

            def wide(ap, n):
                return ap.rearrange("p (k a) -> p k a", a=1).to_broadcast([P, ap.shape[1], n])

            def each(ap, k):
                return ap.rearrange("p (a n) -> p a n", a=1).to_broadcast([P, k, ap.shape[1]])

            for t in range(3):
                own(v.max(gm8[:, t, :], gl8[:, t, :]))
            own.wait()
            for t in range(3):
                own(v.max_index(ri[:, 8 * t:8 * t + 8], gm8[:, t, :], gl8[:, t, :]))
            v.tensor_tensor(gex, gl8[:, :, 0:NG], gm8[:, :, 0:1].to_broadcast([P, 3, NG]),
                            ALU.subtract).then_inc(S["ex_in"], 1)
            own.wait()
            then(v.tensor_copy(gi, ri[:, 0:24:8]))
            then(v.tensor_tensor(gmask, wide(gi, NE), each(con[:, C_GRP:C_GRP + NE], 3), ALU.is_equal))
            own(v.tensor_tensor(em, gmask, lgt[:, :, NG:], ALU.mult))
            own(v.tensor_scalar(tmp, gmask, -NEG, NEG, ALU.mult, ALU.add))
            own.wait()
            then(v.tensor_tensor(em, em, tmp, ALU.add))
            for t in range(3):
                own(v.max(em8[:, t, :], em[:, t, :]))
            own.wait()
            for t in range(3):
                own(v.max_index(ri[:, 24 + 8 * t:32 + 8 * t], em8[:, t, :], em[:, t, :]))
            v.tensor_tensor(d21.rearrange("p (k a) -> p k a", a=1), em8[:, :, 1:2], em8[:, :, 0:1], ALU.subtract)\
                .then_inc(S["ex_in"], 1)
            own.wait()
            for c in range(2):
                own(v.tensor_copy(ei[:, c, :], ri[:, 24 + c:48:8]))
            own.wait()
            for c, M in enumerate((M1, M2)):
                own(v.tensor_tensor(M, wide(ei[:, c, :], NE), each(con[:, C_I16:C_I16 + NE], 3), ALU.is_equal))
            own.wait()
            then(v.tensor_tensor(MM, M1, M2, ALU.add))
            v.tensor_tensor(MM, MM, wide(con[:, C_VAL:C_VAL + 3], NE), ALU.mult).then_inc(S["masks"], 1)
            dve.wait_ge(S["masks"], 1)
            dve.wait_ge(S["rk_ps"], 1)
            own(v.tensor_copy(rank, ps[6][:, 0:3 * NE].rearrange("p (t n) -> p t n", t=3)))
            own(v.tensor_copy(cnt, ps[6][:, 3 * NE:4 * NE]))
            own.wait()
            then(v.scalar_tensor_tensor(out=tmp, in0=rank, scalar=FAR, in1=MM, op0=ALU.add, op1=ALU.mult))
            v.tensor_scalar(rk[:, :, 0:NE], tmp, -FAR, None, ALU.add).then_inc(S["rk_done"], 1)
            dve.wait_ge(S["rk_done"], 1)

            def choose(column, t, n):
                v.tensor_scalar(pick[0:n, t, :], con[0:n, C_I64:C_I64 + SLOTS], column, stat[0:n, 8 + t:9 + t],
                                ALU.is_equal, ALU.mult).then_inc(S["picked"], 1)

            for t, n in enumerate(TILES):
                choose(rk[0:n, t, 0:1], t, n)

            def gathered(s):
                dve.wait_ge(S["hg_ps"], s + 1)
                for n in range(2):
                    v.tensor_tensor(hg[:, 8 * n:8 * n + 8, :], ps[n][:].rearrange("p (k n) -> p k n", k=8),
                                    wide(par[:, 48 + 8 * n:56 + 8 * n], SLOTS), ALU.mult).then_inc(S["hg_sb"], 1)

            gathered(0)
            dve.wait_ge(S["ex_out"], 2)
            own(v.tensor_reduce(gsum, gex, AX, ALU.add))
            own(v.tensor_scalar(dn, d21, 1.0, None, ALU.add))
            own.wait()
            own(v.reciprocal(gp, gsum))
            own(v.reciprocal(gi, dn))
            own.wait()
            then(v.tensor_tensor(wt[:, 0, :], gp, gi, ALU.mult))
            own(v.tensor_tensor(wt[:, 1, :], wt[:, 0, :], d21, ALU.mult))
            then(v.tensor_scalar(ov, cnt, float(SLOTS), None, ALU.is_gt))
            for c in range(2, -(-NT // SLOTS)):
                then(v.scalar_tensor_tensor(out=ov, in0=cnt, scalar=float(c * SLOTS), in1=ov, op0=ALU.is_gt,
                                            op1=ALU.add))
            then(v.tensor_tensor_scan(ovc, con[:, C_ONE:C_ONE + NE], ov, 0.0, ALU.mult, ALU.add))
            own(v.tensor_tensor(ovx, ovc, ov, ALU.subtract))
            own(v.tensor_tensor(sel, each(ovc, MAXOV), wide(con[:, C_I64:C_I64 + MAXOV], NE), ALU.is_le))
            own.wait()
            then(v.tensor_reduce(se, sel, AX, ALU.add))
            then(v.tensor_tensor(sel, sel, each(ov, MAXOV), ALU.mult))
            then(v.tensor_reduce(so, sel, AX, ALU.add))
            then(v.tensor_tensor(so, con[:, C_I64:C_I64 + MAXOV], so, ALU.subtract))
            own(v.tensor_scalar(so, so, 1.0, float(SLOTS), ALU.add, ALU.mult))
            own(v.tensor_scalar(se, se, float(NE - 1), None, ALU.min))
            own.wait()
            own(v.tensor_copy(ints[:, 0:MAXOV], se[0:1, :]))
            own.wait()
            v.tensor_copy(ints[:, MAXOV:MAXOV + 1], ovc[0:1, NE - 1:NE]).then_inc(S["ints_ready"], 1)
            for c, M in enumerate((M1, M2)):
                then(v.tensor_tensor(tmp, rank, M, ALU.mult))
                own(v.tensor_reduce(rr[:, c, :], tmp, AX, ALU.add))
                then(v.tensor_tensor(gmask, M, each(ovx, 3), ALU.mult))
                then(v.tensor_reduce(ro[:, c, :], gmask, AX, ALU.add))
            then(v.tensor_tensor(ro, ro, ei, ALU.subtract))
            own(v.tensor_scalar(ro, ro, float(NE - 1), float(SLOTS), ALU.add, ALU.mult))
            own(v.tensor_scalar(tmp[:, 0:2, 0:3], rr, float(SLOTS), None, ALU.is_ge))
            own.wait()
            own(v.tensor_tensor(ro, ro, tmp[:, 0:2, 0:3], ALU.mult))
            then(v.scalar_tensor_tensor(out=rr, in0=ei, scalar=float(SLOTS), in1=rr, op0=ALU.mult, op1=ALU.add))
            then(v.tensor_tensor(rr, rr, ro, ALU.add))
            v.tensor_copy(rows[:, 0:6].rearrange("p (t c) -> p c t", c=2), rr).then_inc(S["rows_ready"], 1)

            def expert(s):
                dve.wait_ge(S["silu_done"], s + 1)
                dve.wait_ge(S["up_ps"], s + 1)
                v.tensor_tensor(flat(aT[:]), flat(sgl[:]), ps[3][:, 0:FT * SLOTS], ALU.mult).then_inc(S["a_ready"], 1)

            def half_rows(s):
                dve.wait_ge(S["dn_ps"], s + 1)
                for q in (1, 3):
                    v.tensor_copy(y_sb[:, q * 512:(q + 1) * 512], ps[4 + q][0:SLOTS, :]).then_inc(S["y_dve"], 1)

            with dve.Fori(0, NE) as e:
                dve.wait_ge(S["hg_ps"], e + 1)
                for t, n in enumerate(TILES):
                    choose(rk[0:n, t, ds(e + 1, 1)], t, n)
                expert(e)
                gathered(e + 1)
                dve.wait_ge(S["y_out"], e * 16)
                half_rows(e)
            dve.wait_ge(S["y_out"], 16 * NE)
            dve.wait_ge(S["ints_ready"], 1)
            more = dve.value_load(ints[0:1, MAXOV:MAXOV + 1], min_val=0, max_val=MAXOV)
            with dve.If(more > 0):
                with dve.Fori(0, more) as i:
                    own.enter(i, 1)
                    e = dve.value_load(ints[0:1, ds(i, 1)], min_val=0, max_val=NE - 1)
                    dve.wait_ge(S["hg_ps"], i + (NE + 1))
                    then(v.tensor_scalar(rko[:, 0:3].rearrange("p (k a) -> p k a", a=1), rk[:, :, ds(e, 1)],
                                         so[:, ds(i, 1)], None, ALU.subtract))
                    for t, n in enumerate(TILES):
                        choose(rko[0:n, t:t + 1], t, n)
                    gathered(i + (NE + 1))
                    expert(i + NE)
                    dve.wait_ge(S["ov_out"], i * 16)
                    half_rows(i + NE)
            dve.wait_ge(S["gf_in"], 16)
            for t, n in enumerate(TILES):
                dve.wait_ge(S[f"y_in{t}"], 32)
                v.scalar_tensor_tensor(out=ya[t][0:n], in0=ya[t][0:n], scalar=wt[0:n, 0, t:t + 1], in1=x2[0:n, t, :],
                                       op0=ALU.mult, op1=ALU.add).then_inc(S["half_done"], 1)
                dve.wait_ge(S["half_done"], t + 1)
                v.scalar_tensor_tensor(out=ya[t][0:n], in0=yb[t][0:n], scalar=wt[0:n, 1, t:t + 1], in1=ya[t][0:n],
                                       op0=ALU.mult, op1=ALU.add).then_inc(S["sum_done"], 1)
            for t, n in enumerate(TILES):
                dve.wait_ge(S["ssq3"], t + 1)
                v.tensor_scalar(stat[0:n, 4 + t:5 + t], stat[0:n, t:t + 1], 1.0 / D, EPS, ALU.mult, ALU.add)\
                    .then_inc(S["rms"], 1)
                dve.wait_ge(S["rms"], 6 + 2 * t)
                v.reciprocal(stat[0:n, 8 + t:9 + t], stat[0:n, 4 + t:5 + t]).then_inc(S["inv_done"], 1)
                dve.wait_ge(S["inv_done"], t + 1)
                v.scalar_tensor_tensor(out=ya[t][0:n], in0=ya[t][0:n], scalar=stat[0:n, 8 + t:9 + t], in1=gfin[0:n],
                                       op0=ALU.mult, op1=ALU.mult).then_inc(S["fin"], 1)


_INS = """x_prompt x_sample cache_sb_k cache_sb_v cache_swa_k cache_swa_v w_in b_gate swa_sink w_sb_o w_swa_o w_out
g_mix g_ffn w_rg b_rg w_re b_re w_e_gate w_e_up w_e_down g_final""".split()
_OUTS = [(1, SEQ, D), (1, DEC, D), (4, SEQ, 512), (4, DEC, 512), (P, 512), (DEC, 512), (2, PAST - DEC, KV * HD)]


def kernel(**inputs):
    import concourse.bacc as bacc
    from concourse.bass_utils import run_bass_kernel_spmd

    nc = bacc.Bacc("TRN2", target_bir_lowering=False, num_devices=1)
    arrays, args = {}, []
    for name, a in [(n, inputs[n]) for n in _INS] + [("const", constants())]:
        a = np.ascontiguousarray(a)
        arrays[f"in_{name}"] = a
        args.append(nc.dram_tensor(f"in_{name}", a.shape, F32, kind="ExternalInput").ap())
    for i, shape in enumerate(_OUTS):
        args.append(nc.dram_tensor(f"out_{i}", shape, F32, kind="ExternalOutput").ap())
    build(nc, *args)
    r = run_bass_kernel_spmd(nc, [arrays], core_ids=[0])
    yp, ys, kvp, kvs, wp, wn, wk = (r.results[0][f"out_{i}"] for i in range(len(_OUTS)))

    def heads(a, n):
        return a.reshape(1, 1, a.shape[0], n, HD)

    halves = [np.concatenate([x[2 * n], x[2 * n + 1]], axis=1) for x in (kvp, kvs) for n in range(2)]
    w = KV * HD
    return (yp, ys, heads(halves[0], H), heads(halves[1], H), heads(wp[:, :w], KV), heads(wp[:, w:], KV),
            heads(halves[2], H), heads(halves[3], H),
            heads(np.concatenate([wk[0], wn[:, :w]]), KV), heads(np.concatenate([wk[1], wn[:, w:]]), KV))
```

```python
from contextlib import ExitStack

import concourse.bass as bass
import numpy as np
from concourse import mybir

F32 = mybir.dt.float32
F32R = mybir.dt.float32r
I32 = mybir.dt.int32
U32 = mybir.dt.uint32
ACT = mybir.ActivationFunctionType
ALU = mybir.AluOpType
AX = mybir.AxisListType.X

P = 128
D = 2048
KT = D // P
SEQ, DEC, PAST = 256, 32, 128
NT = SEQ + DEC
NTP = 3 * P
TILES = (P, P, DEC)
HD = 128
H = 8
KV = 2
GRP = H // KV
CHUNK = 64
SBW = H * HD
GATE0 = 3 * SBW + H * HD + 2 * KV * HD
INW = GATE0 + 2 * D
NG, EPG = 4, 4
NE = NG * EPG
DE = 512
FT = DE // P
EPS = 1e-6
SCALE = HD ** -0.5
NEG = -1e30
SLOTS = 64
MAXOV = 2 * NT // SLOTS
NL = NG + NE
SBUF0 = 16640
PAIR = 2 * P
PIECE = D // 2
CH = 24
AHEAD = 3
FAR = 1000.0

IT_QSB, IT_KSB, IT_VSB, IT_QSW, IT_KVSW, IT_ATT, IT_PROJ, IT_OUT, IT_END = 0, 2, 4, 6, 8, 9, 13, 21, 25

C_ID, C_TRI, C_SU, C_ONE = 0, 128, 256, 384
C_MSB = 512
SBC = 448
C_MSW = C_MSB + SBC
SWC = 384
C_MSS = C_MSW + SWC
SSC = 160
C_COS = C_MSS + SSC
C_SIN = C_COS + NT
C_I64 = C_SIN + NT
C_I16 = C_I64 + SLOTS
C_GRP = C_I16 + NE
C_VAL = C_GRP + NE
NC_ = C_VAL + 4


def constants():
    c = np.zeros((P, NC_), np.float32)
    r = np.arange(P)
    c[:, C_ID:C_ID + P] = np.eye(P)
    c[:, C_TRI:C_TRI + P] = r[:, None] >= r[None]
    c[:, C_SU:C_SU + P] = r[:, None] < r[None]
    c[:, C_ONE:C_ONE + P] = 1
    tri = np.where(r[:, None] < r[None], 0, NEG)
    c[:, C_MSB:C_MSB + P] = tri
    c[:, C_MSB + SEQ:C_MSB + SEQ + P] = tri
    c[:, C_MSB + SEQ + P + DEC:C_MSB + SBC] = tri[:, :DEC]
    for j, (q0, n) in enumerate(((0, P), (P, SEQ))):
        d = (q0 + r)[:, None] // CHUNK - np.arange(n)[None] // CHUNK
        at = C_MSW + j * P
        c[:, at:at + n] = np.where((d >= 0) & (d < 2), 0, NEG)
    d = (PAST + r % DEC)[:, None] // CHUNK - np.arange(SSC)[None] // CHUNK
    c[:, C_MSS:C_MSS + SSC] = np.where((d >= 0) & (d < 2), 0, NEG)
    half = HD // 2
    inv = np.power(np.float32(10000.0), -np.arange(half, dtype=np.float32) * np.float32(2.0 / HD))
    pos = np.concatenate([np.arange(SEQ), PAST + np.arange(DEC)]).astype(np.float32)
    ang = (pos[None] * inv[:, None].astype(np.float32)).astype(np.float32)
    c[:, C_COS:C_COS + NT] = np.tile(np.cos(ang), (2, 1))
    c[:half, C_SIN:C_SIN + NT] = np.sin(ang)
    c[half:, C_SIN:C_SIN + NT] = -np.sin(ang)
    c[:, C_I64:C_I64 + SLOTS] = np.arange(SLOTS)
    c[:, C_I16:C_I16 + NE] = np.arange(NE)
    c[:, C_GRP:C_GRP + NE] = np.arange(NE) // EPG
    for t, n in enumerate(TILES):
        c[:n, C_VAL + t] = 1
    return c


RAISED = """z_sb o_sb h_turned pool_head m_done a_ready y_free nat_done zm_done e_done o_sb_ev nat_free
            rope_done ml_done y_act y_dve aT_ps aTl_done ev_a ev_d""".split()


class Steps:

    def __init__(self, eng, sem):
        self.eng, self.sem, self.n, self.i, self.per, self.base = eng, sem, 0, None, 0, 0

    def at(self):
        return self.n if self.i is None else self.i * self.per + (self.base + self.n)

    def __call__(self, ins):
        ins.then_inc(self.sem, 1)
        self.n += 1

    def wait(self):
        if self.i is None and self.n == 0:
            return
        self.eng.wait_ge(self.sem, self.at())

    def enter(self, i, per):
        self.base, self.i, self.per, self.n = self.n, i, per, 0

    def leave(self, trips):
        assert self.n == self.per, (self.n, self.per)
        self.n, self.i = self.base + self.per * trips, None



def build(nc, x_prompt, x_sample, cache_sb_k, cache_sb_v, cache_swa_k, cache_swa_v, w_in, b_gate, swa_sink,
          w_sb_o, w_swa_o, w_out, g_mix, g_ffn, w_rg, b_rg, w_re, b_re, w_e_gate, w_e_up, w_e_down, g_final,
          const, y_prompt, y_sample, sb_kv_prompt, sb_kv_sample, swa_kv_prompt, swa_kv_new, swa_kv_kept):
    xT_spill = nc.dram_tensor("xT_spill", (P, KT * NT), F32, kind="Internal").ap()
    y_rows = nc.dram_tensor("y_rows", ((NE + MAXOV) * SLOTS, D), F32, kind="Internal").ap()

    def at(name, kb, shape, dt=F32):
        return nc.alloc_sbuf_tensor_at(name, shape, dt, offset=SBUF0 + int(kb * 1024))

    ring = at("ring", 0, [P, 2, KT, PAIR])
    wh = at("wh", 32, [P, 2, KT, P], F32R)
    wl = at("wl", 48, [P, 2, KT, P], F32R)
    xh = at("xh", 64, [P, KT, NT], F32R)
    xl = at("xl", 82, [P, KT, NT], F32R)
    kT_sb = at("kT_sb", 100, [P, H, NTP])
    v_sb = at("v_sb", 112, [P, 3, SBW])
    vc_sb = at("vc_sb", 124, [P, SBW])
    kcT_sb = at("kcT_sb", 128, [P, H, P])
    kT_sw = at("kT_sw", 132, [P, KV, NTP])
    v_sw = at("v_sw", 135, [P, 3, KV * HD])
    oh = at("oh", 100, [P, 2 * H, NT], F32R)
    ol = at("ol", 118, [P, 2 * H, NT], F32R)
    x_nat = at("x_nat", 138, [P, 3, D])
    squares = at("squares", 162, [P, D])
    kc_nat = at("kc_nat", 170, [P, SBW])
    headT = at("headT", 138, [P, 4, NTP])
    nat = at("nat", 144, [P, 3, 4 * P])
    gates = at("gates", 138, [P, KT, NT])
    qT = at("qT", 156, [P, 2 * H, NT])
    mh = at("mh", 138, [P, KT, NT], F32R)
    ml = at("ml", 156, [P, KT, NT], F32R)
    xT = at("xT", 174, [P, KT, NT])
    kcT_sw = at("kcT_sw", 174, [P, KV, P])
    vc_sw = at("vc_sw", 175, [P, KV * HD])
    kst = at("kst", 176, [P, 4, P])
    vst = at("vst", 178, [P, 4, P])
    qst = at("qst", 180, [P, SEQ])
    zm = at("zm", 181, [P, SBC])
    lg = at("lg", 182.75, [P, SBC])
    spb = at("spb", 184.5, [P, SBC])
    zw = at("zw", 186.25, [P, SWC])
    pT = at("pT", 187.75, [P, SWC])
    st = at("st", 189.25, [P, 16])
    kcw_nat = at("kcw_nat", 189.5, [P, KV * HD])
    rope_a = at("rope_a", 181, [P, NT])
    rope_b = at("rope_b", 182.25, [P, NT])
    zero = at("zero", 184, [P, 512])
    sg1 = at("sg1", 174, [P, NT])
    sg2 = at("sg2", 175.25, [P, NT])
    m1 = at("m1", 176.5, [P, NT])
    m2 = at("m2", 177.75, [P, NT])
    diag = at("diag", 32, [P, 3, P])
    rstd_b = at("rstd_b", 34, [P, NT])
    con = at("con", 192, [P, NC_])
    hbuf = at("hbuf", 201, [P, 2, NT])
    par = at("par", 203.5, [P, 64])
    par_nat = at("par_nat", 203.75, [64, P])
    wr = at("wr", 204.25, [P, KT, NL])
    sinks = at("sinks", 205.5, [P, H])
    sinks_s = at("sinks_s", 205.53125, [P, KV])
    br = at("br", 205.5625, [P, NL])
    stat = at("stat", 205.6875, [P, 32])
    slot_g = at("slot_g", 100, [P, KT, DE])
    slot_u = at("slot_u", 64, [P, KT, DE])
    slot_d = at("slot_d", 0, [P, FT, D])
    eh = [at(f"eh{j}", 156 + 8 * j, [P, PIECE], F32R) for j in range(AHEAD + 1)]
    el = [at(f"el{j}", 160 + 8 * j, [P, PIECE], F32R) for j in range(AHEAD + 1)]
    hgx = at("hgx", 32, [P, KT, 2 * SLOTS], F32R)
    hg = at("hg", 40, [P, KT, SLOTS])
    aTx = at("aTx", 44, [P, FT, 2 * SLOTS], F32R)
    pick = at("pick", 46, [P, 3, SLOTS])
    y_sb = at("y_sb", 52, [SLOTS, D])
    g_sb = at("g_sb", 60, [SLOTS, DE])
    u_sb = at("u_sb", 62, [SLOTS, DE])
    rt = at("rt", 47, [P, 768])
    ri = at("ri", 50, [P, 64], U32)
    rows = at("rows", 50.25, [P, 8], U32)
    ints = at("ints", 50.3125, [1, 16], I32)
    rk = at("rk", 50.5, [P, 3, NE + 1])
    rko = at("rko", 50.75, [P, 4])
    squares2 = at("squares2", 52, [P, D])
    x2 = at("x2", 132, [P, 3, D])
    gfin = at("gfin", 88, [P, D])
    ya = [at(f"ya{t}", 100 + 8 * t, [P, D]) for t in range(3)]
    yb = [at(f"yb{t}", 64 + 8 * t, [P, D]) for t in range(3)]

    c0 = [0]

    def cols(n, shape=None):
        a = c0[0]
        c0[0] += n
        v = rt[:, a:a + n]
        return v if shape is None else v.rearrange("p (a b) -> p a b", b=shape)
    lgt = cols(3 * NL, NL)
    gl8 = cols(24, 8)
    gm8 = cols(24, 8)
    em = cols(3 * NE, NE)
    em8 = cols(24, 8)
    gex = cols(3 * NG, NG)
    d21 = cols(3)
    gi = cols(3)
    gsum = cols(3)
    gp = cols(3)
    dn = cols(3)
    wt = cols(6, 3)
    ei = cols(6, 3)
    gmask = cols(3 * NE, NE)
    tmp = cols(3 * NE, NE)
    M1 = cols(3 * NE, NE)
    M2 = cols(3 * NE, NE)
    MM = cols(3 * NE, NE)
    rank = cols(3 * NE, NE)
    cnt = cols(NE)
    ov = cols(NE)
    ovc = cols(NE)
    ovx = cols(NE)
    sel = cols(MAXOV * NE, NE)
    se = cols(MAXOV)
    so = cols(MAXOV)
    rr = cols(6, 3)
    ro = cols(6, 3)
    assert c0[0] <= 768, c0[0]

    with ExitStack() as ctx:
        ps = [ctx.enter_context(nc.psum_tensor(f"bank{i}", [P, 512], F32)) for i in range(8)]
        names = """const_in x_in w_load0 w_load1 kc_in vc_in swc_in small_in xT_out act_own dve_own
                   rms diag_done rb_ps x_turned h_done xh_done xl_done xT_done par_ps par_sb kc_ps kc_sb pads
                   wh_ready wl_ready blk ev_a ev_d rope_done h_turned nat_done nat_out nat_free kept_out pool_head
                   kst_st vst_st qst_st z_sb z_sw zm_done zw_done l_done sp_done c_done e_done a_done
                   p_ready pT_ps pT_sb o_sb o_sw o_sb_ev o_sw_ev sums_done oh_done ol_done sig_done m_done mh_done
                   ml_done xT_in wr_scaled x2_ps x2_a x2_d ssq2 lg_ps masks rk_ps rk_done
                   g_in u_in d_in picked hg_ps hg_sb hgh_done hgl_done eh_ready el_ready ch_used g_low g_sum
                   silu_done u_low u_sum a_ready aT_ps aTh_done aTl_done y_act y_dve y_out y_free
                   zero_set zero_out rows_ready ints_ready gf_in y_in0 y_in1 y_in2 sum_done fin out_done
                   ex_in ex_out half_done ssq3 rko_done""".split()
        S = {n: ctx.enter_context(nc.semaphore(n)) for n in names}
        block = ctx.enter_context(nc.Block())
        ds = bass.ds
        v, a_ = nc.vector, nc.scalar

        def upto(it, j):
            return it * 4 + (j + 1)

        def tok(t):
            return slice(t * P, t * P + TILES[t])

        def piece(c):
            m, q = c % CH // 8, c % 8
            if m == 2:
                return "d_in", slot_d[:, q // 2, q % 2 * PIECE:(q % 2 + 1) * PIECE]
            w = (slot_g, slot_u)[m]
            return ("g_in", "u_in")[m], w[:, 2 * q:2 * q + 2, :].rearrange("p k n -> p (k n)")

        def used(s, c):
            return s * CH + (c + 2 + AHEAD)

        def flat(ap):
            return ap.rearrange("p a n -> p (a n)")

        def main(j):
            return ps[j % 2][:, 0:NT]

        def raw(j):
            return ring[:, j // 2, :, (j % 2) * P:(j % 2 + 1) * P]

        EV_KVSW_A, EV_KVSW_D = 1 + 24, 1 + 8
        EV_ATT = EV_KVSW_A + 2
        EV_PROJ = EV_ATT + 16
        EV_OUT_D = EV_KVSW_D + 2

        @block.sync
        def _(sp):
            sp.dma_start(x_nat[:, 0:2, :], x_prompt[0].rearrange("(t p) d -> p t d", p=P)).then_inc(S["x_in"], 16)
            sp.dma_start(x_nat[0:DEC, 2, :], x_sample[0]).then_inc(S["x_in"], 16)

            def load_pair(j, src):
                sp.dma_start(ring[:, j], src.rearrange("(k p) n -> p k n", p=P)).then_inc(S[f"w_load{j}"], 16)

            def slot_free(j, it):
                sp.wait_ge(S["wl_ready"], (it - 1) * 4 + (2 * j + 2))

            load_pair(0, w_in[0, :, 0:PAIR])
            load_pair(1, w_in[0, :, PAIR:2 * PAIR])
            with sp.Fori(1, IT_PROJ) as it:
                for j in range(2):
                    slot_free(j, it)
                    load_pair(j, w_in[0, :, ds(it * (2 * PAIR) + j * PAIR, PAIR)])
            with sp.Fori(IT_PROJ, IT_OUT) as it:
                slot_free(0, it)
                load_pair(0, w_in[0, :, ds(it * PAIR + (GATE0 + D - IT_PROJ * PAIR), PAIR)])
                slot_free(1, it)
                for k, w in enumerate((w_sb_o, w_swa_o)):
                    sp.dma_start(ring[:, 1, k * H:(k + 1) * H],
                                 w[0, :, ds((it - IT_PROJ) * PAIR, PAIR)].rearrange("(k p) n -> p k n", p=P))\
                        .then_inc(S["w_load1"], 16)
            with sp.Fori(IT_OUT, IT_END) as it:
                for j in range(2):
                    slot_free(j, it)
                    load_pair(j, w_out[0, :, ds((it - IT_OUT) * (2 * PAIR) + j * PAIR, PAIR)])

            def load(dst, w, e, sem):
                sp.dma_start(dst[:], w[0, ds(e, 1)].rearrange("a (k p) n -> p (a k) n", p=P)).then_inc(S[sem], 16)

            sp.wait_ge(S["blk"], upto(IT_OUT - 1, 3))
            load(slot_g, w_e_gate, 0, "g_in")
            load(slot_u, w_e_up, 0, "u_in")
            sp.wait_ge(S["wl_ready"], upto(IT_END - 1, 3))
            load(slot_d, w_e_down, 0, "d_in")

            def next_matrices(e, s):
                sp.wait_ge(S["el_ready"], s * CH + (8 - CH))
                load(slot_g, w_e_gate, e, "g_in")
                sp.wait_ge(S["el_ready"], s * CH + (16 - CH))
                load(slot_u, w_e_up, e, "u_in")
                sp.wait_ge(S["el_ready"], s * CH)
                load(slot_d, w_e_down, e, "d_in")

            with sp.Fori(1, NE) as e:
                next_matrices(e, e)
            sp.wait_ge(S["ints_ready"], 1)
            more = sp.value_load(ints[0:1, MAXOV:MAXOV + 1], min_val=0, max_val=MAXOV)
            with sp.If(more > 0):
                with sp.Fori(0, more) as i:
                    e = sp.value_load(ints[0:1, ds(i, 1)], min_val=0, max_val=NE - 1)
                    next_matrices(e, i + NE)
            for t, n in enumerate(TILES):
                sp.wait_ge(S["fin"], t + 1)
                sp.dma_start(y_prompt[0, tok(t)] if t < 2 else y_sample[0], ya[t][0:n]).then_inc(S["out_done"], 16)
            sp.wait_ge(S["out_done"], 16 * 3)
            sp.wait_ge(S["nat_out"], 32 * 5)
            sp.wait_ge(S["kept_out"], 16 * 2)

        @block.gpsimd
        def _(pool):
            pool.dma_start(con[:], const).then_inc(S["const_in"], 16)
            for name in RAISED:
                pool.sem_inc(S[name], 1)
            for src, r0, r1 in ((b_gate, 0, 32), (g_mix, 32, 48), (g_ffn, 48, 64)):
                pool.dma_start(par_nat[r0:r1, :], src[0].rearrange("(r p) -> r p", p=P)).then_inc(S["const_in"], 16)
            pool.dma_start(kc_nat[:], cache_sb_k[0, 0].rearrange("s h d -> s (h d)")).then_inc(S["kc_in"], 16)
            pool.dma_start(vc_sb[:], cache_sb_v[0, 0].rearrange("s h d -> s (h d)")).then_inc(S["vc_in"], 16)
            pool.dma_start(sinks[:], swa_sink[0:1, :].to_broadcast([P, H])).then_inc(S["small_in"], 16)
            with nc.allow_non_contiguous_dma(reason="8 sinks"):
                for g in range(GRP):
                    for kv in range(KV):
                        pool.dma_start(sinks_s[DEC * g:DEC * g + DEC, kv:kv + 1],
                                       swa_sink[0:1, GRP * kv + g:GRP * kv + g + 1].to_broadcast([DEC, 1]))\
                            .then_inc(S["small_in"], 16)
            pool.dma_start(wr[:, :, 0:NG], w_rg[0].rearrange("(k p) n -> p k n", p=P)).then_inc(S["small_in"], 16)
            pool.dma_start(wr[:, :, NG:], w_re[0].rearrange("(k p) n -> p k n", p=P)).then_inc(S["small_in"], 16)
            pool.dma_start(br[:, 0:NG], b_rg[0:1, :].to_broadcast([P, NG])).then_inc(S["small_in"], 16)
            pool.dma_start(br[:, NG:], b_re[0:1, :].to_broadcast([P, NE])).then_inc(S["small_in"], 16)
            for n, c in enumerate((cache_swa_k, cache_swa_v)):
                pool.dma_start(swa_kv_kept[n], c[0, 0, DEC:PAST].rearrange("s h d -> s (h d)"))\
                    .then_inc(S["kept_out"], 16)
            pool.wait_ge(S["xT_out"], 16)
            pool.dma_start(kcw_nat[:], cache_swa_k[0, 0].rearrange("s h d -> s (h d)")).then_inc(S["swc_in"], 16)
            pool.dma_start(vc_sw[:], cache_swa_v[0, 0].rearrange("s h d -> s (h d)")).then_inc(S["swc_in"], 16)
            pool.memset(zero[:], 0.0).then_inc(S["zero_set"], 1)
            pool.wait_ge(S["zero_set"], 1)
            for r0, k in ((NE * SLOTS, 4), (NE * SLOTS + 4 * P, 0)):
                n, m = (P, k) if k else (MAXOV * SLOTS - 4 * P, 1)
                for q in range(m):
                    pool.dma_start(y_rows[r0 + q * P:r0 + q * P + n, :].rearrange("p (b n) -> p b n", n=512),
                                   zero[0:n, :].rearrange("p (a n) -> p a n", a=1).to_broadcast([n, 4, 512]))\
                        .then_inc(S["zero_out"], 16)

            def nat_store(i, src, dst_prompt, dst_sample):
                pool.wait_ge(S["nat_done"], i * 4 + 5)
                pool.dma_start(dst_prompt, src).then_inc(S["nat_out"], 16)
                pool.dma_start(dst_sample, nat[0:DEC, 2, :]).then_inc(S["nat_out"], 16)
                pool.wait_ge(S["nat_out"], i * 32 + 32)
                pool.sem_inc(S["nat_free"], 1)

            for n in range(2):
                with pool.Fori(0, 2) as ii:
                    i = ii + 2 * n
                    for j in range(4):
                        if n == 0:
                            pool.wait_ge(S["ev_a"], i * 4 + (1 + 8 + j + 1 + 1))
                            pool.tensor_copy(kT_sb[:, ds(ii * 4 + j, 1), 0:NT], headT[:, j:j + 1, 0:NT])\
                                .then_inc(S["pool_head"], 1)
                        else:
                            pool.wait_ge(S["nat_done"], i * 4 + (j + 1 + 1))
                            pool.tensor_copy(v_sb[:, :, ds(ii * (4 * P) + j * P, P)], nat[:, :, j * P:(j + 1) * P])\
                                .then_inc(S["pool_head"], 1)
                    nat_store(i, nat[:, 0:2, :],
                              sb_kv_prompt[ds(i, 1)].rearrange("a (t p) n -> p (a t) n", p=P),
                              sb_kv_sample[ds(i, 1)].rearrange("a p n -> p (a n)"))
            pool.wait_ge(S["nat_done"], 21)
            pool.tensor_copy(v_sw[:], nat[:, :, KV * HD:]).then_inc(S["pool_head"], 1)
            nat_store(4, nat[:, 1, :], swa_kv_prompt, swa_kv_new)

            pool.wait_ge(S["pool_head"], 18)
            pool.wait_ge(S["vc_in"], 16)
            pool.wait_ge(S["kc_sb"], 2)
            pool.wait_ge(S["rope_done"], 11)
            for g in range(KV):
                pool.tensor_copy(qst[:, g * P:(g + 1) * P].rearrange("p (h n) -> p h n", h=GRP),
                                 qT[:, H + GRP * g:H + GRP * g + GRP, SEQ:NT]).then_inc(S["qst_st"], 1)
            with pool.Fori(0, IT_PROJ - IT_ATT) as i:
                for u in range(2):
                    hd = i * 2 + u
                    pool.wait_ge(S["z_sb"], hd + 1)
                    pool.tensor_copy(kst[:, 0:3, :], kT_sb[:, ds(hd, 1), :].rearrange("p a (t n) -> p (a t) n", n=P))\
                        .then_inc(S["kst_st"], 1)
                    pool.tensor_copy(kst[:, 3:4, :], kcT_sb[:, ds(hd, 1), :]).then_inc(S["kst_st"], 1)
                    pool.wait_ge(S["z_sw"], hd + KV)
                    pool.tensor_copy(qst[:].rearrange("p (a n) -> p a n", a=1),
                                     qT[:, ds(i + (H + GRP * u), 1), 0:SEQ]).then_inc(S["qst_st"], 1)
                    pool.wait_ge(S["o_sb"], hd + 1)
                    pool.tensor_copy(vst[:, 0:3, :], v_sb[:, :, ds(hd * P, P)]).then_inc(S["vst_st"], 1)
                    pool.tensor_copy(vst[:, 3:4, :], vc_sb[:, ds(hd * P, P)].rearrange("p (a n) -> p a n", a=1))\
                        .then_inc(S["vst_st"], 1)
            pool.wait_ge(S["ml_done"], KT + 1)
            pool.dma_start(xT[:], xT_spill.rearrange("p (k n) -> p k n", k=KT)).then_inc(S["xT_in"], 16)
            with pool.Fori(0, NE) as e:
                pool.wait_ge(S["y_dve"], e * 4 + 5)
                pool.dma_start(y_rows[ds(e * SLOTS, SLOTS), :], y_sb[:]).then_inc(S["y_out"], 16)
                pool.wait_ge(S["y_out"], e * 16 + 16)
                pool.sem_inc(S["y_free"], 1)
            pool.wait_ge(S["ints_ready"], 1)
            more = pool.value_load(ints[0:1, MAXOV:MAXOV + 1], min_val=0, max_val=MAXOV)
            pool.wait_ge(S["zero_out"], 16 * 5)
            with pool.If(more > 0):
                with pool.Fori(0, more) as i:
                    pool.wait_ge(S["y_dve"], i * 4 + (4 * NE + 5))
                    pool.dma_start(y_rows[ds(i * SLOTS + NE * SLOTS, SLOTS), :], y_sb[:]).then_inc(S["y_out"], 16)
                    pool.wait_ge(S["y_out"], i * 16 + (16 * NE + 16))
                    pool.sem_inc(S["y_free"], 1)
            pool.wait_ge(S["rows_ready"], 1)
            pool.dma_start(gfin[:], g_final.rearrange("(a n) -> a n", a=1).to_broadcast([P, D]))\
                .then_inc(S["gf_in"], 16)
            for t, n in enumerate(TILES):
                for c, dst in enumerate((ya, yb)):
                    pool.indirect_dma_start(
                        dst[t][0:n, :], None, y_rows,
                        bass.IndirectOffsetOnAxis(ap=rows[0:n, 2 * t + c:2 * t + c + 1], axis=0))\
                        .then_inc(S[f"y_in{t}"], 16)

        @block.scalar
        def _(act):
            own = Steps(act, S["act_own"])
            act.wait_ge(S["dve_own"], 1)
            act.wait_ge(S["x_in"], 32)
            for t, n in enumerate(TILES):
                own.wait()
                own(a_.activation(squares[0:n], x_nat[0:n, t, :], ACT.Square, accum_out=stat[0:n, t:t + 1]))
            act.wait_ge(S["rms"], 1)
            a_.activation(stat[:, 16:19], stat[:, 4:7], ACT.Sqrt).then_inc(S["rms"], 1)
            act.wait_ge(S["par_ps"], 1)
            a_.activation(par[:], ps[1][:, 0:64], ACT.Copy).then_inc(S["par_sb"], 1)
            for n in range(2):
                act.wait_ge(S["kc_ps"], n + 1)
                a_.activation(kcT_sb[:, 4 * n:4 * n + 4, :], ps[5 + n][:].rearrange("p (h n) -> p h n", h=4), ACT.Copy)\
                    .then_inc(S["kc_sb"], 1)
            for k in range(KT):
                act.wait_ge(S["x_turned"], k + 1)
                a_.activation(xT[:, k, :], ps[2 + k % 3][:, 0:NT], ACT.Copy).then_inc(S["xT_done"], 1)
                act.wait_ge(S["h_done"], k + 1)
                a_.activation(xh[:, k, :], hbuf[:, k % 2, :], ACT.Copy).then_inc(S["xh_done"], 1)

            def split(j, loads):
                act.wait_ge(S[f"w_load{j // 2}"], loads)
                a_.activation(wh[:, j % 2], raw(j), ACT.Copy).then_inc(S["wh_ready"], 1)

            act.wait_ge(S["rb_ps"], 1)
            act.wait_ge(S["h_done"], KT)
            split(0, 16)
            split(1, 16)
            act.wait_ge(S["xT_done"], KT)
            act.dma_start(xT_spill.rearrange("p (k n) -> p k n", k=KT), xT[:]).then_inc(S["xT_out"], 16)
            own(a_.activation(stat[:, 12:13], stat[:, 8:9], ACT.Copy))
            a_.activation(stat[:, 13:14], stat[:, 8:9], ACT.Copy).then_inc(S["ev_a"], 1)

            def step(it, j, evac, loads1=None):
                act.wait_ge(S["blk"], upto(it, j))
                if evac:
                    evac()
                if j < 2:
                    split(j + 2, it * 16 + 16 if loads1 is None else loads1)
                else:
                    split(j - 2, it * 16 + 32)

            with act.Fori(IT_QSB, IT_KSB) as it:
                for j in range(4):
                    step(it, j, lambda: a_.activation(flat(qT[:, ds(it * 4 + j, 1), :]), main(j), ACT.Copy)
                         .then_inc(S["ev_a"], 1))
            act.wait_ge(S["pads"], 1)
            with act.Fori(0, 4) as i:
                for j in range(4):
                    if j == 0:
                        act.wait_ge(S["h_turned"], i * 4 + 1)
                        act.wait_ge(S["pool_head"], i * 4 + 1)
                    step(i + IT_KSB, j, lambda: a_.activation(headT[:, j, 0:NT], main(j), ACT.Copy)
                         .then_inc(S["ev_a"], 1))
            with act.Fori(IT_QSW, IT_KVSW) as it:
                for j in range(4):
                    step(it, j, None)
            act.wait_ge(S["h_turned"], 17)
            act.wait_ge(S["pool_head"], 17)
            for j in range(4):
                step(IT_KVSW, j, None if j < 2 else lambda: a_.activation(
                    headT[:, j, 0:NT], main(j), ACT.Copy).then_inc(S["ev_a"], 1))
            act.wait_ge(S["kc_ps"], 3)
            a_.activation(kcT_sw[:], ps[6][:, 0:KV * P].rearrange("p (h n) -> p h n", h=KV), ACT.Copy)\
                .then_inc(S["kc_sb"], 1)

            def softmax(segments, sink, n):
                act.wait_ge(S["zw_done"], n)
                for c, (a, b) in enumerate(segments):
                    a_.activation(zw[:, a:b], zw[:, a:b], ACT.Exp, bias=st[:, 2 + c:3 + c],
                                  accum_out=st[:, 4 + c:5 + c]).then_inc(S["sums_done"], 1)
                c = len(segments)
                a_.activation(st[:, 6:6 + c], st[:, 2:2 + c], ACT.Exp, bias=sink).then_inc(S["sums_done"], 1)

            act.wait_ge(S["small_in"], 16 * 13)
            for g in range(KV):
                softmax([(0, SSC)], sinks_s[:, g:g + 1], g + 1)
                act.wait_ge(S["pT_ps"], g + 1)
                if g:
                    act.wait_ge(S["o_sw"], g)
                a_.activation(pT[:, 0:P], ps[5][:, 0:P], ACT.Copy).then_inc(S["pT_sb"], 1)
                a_.activation(pT[0:DEC, P:2 * P], ps[5][0:DEC, P:2 * P], ACT.Copy).then_inc(S["pT_sb"], 1)
                act.wait_ge(S["o_sw"], g + 1)
                a_.activation(qT[:, H + GRP * g:H + GRP * g + GRP, SEQ:NT],
                              ps[7][:, 0:P].rearrange("p (h n) -> p h n", h=GRP), ACT.Copy)\
                    .then_inc(S["o_sw_ev"], 1)
            act.wait_ge(S["nat_free"], 6)
            act.wait_ge(S["pool_head"], 18)
            with act.Fori(0, IT_PROJ - IT_ATT) as i:
                own.enter(i, 4)
                for u in range(2):
                    hd = i * 2 + u
                    act.wait_ge(S["zm_done"], hd + 2)
                    own(a_.activation(lg[:], zm[:], ACT.Abs))
                    own.wait()
                    own(a_.activation(lg[:], lg[:], ACT.Exp, scale=-1.0))
                    own.wait()
                    a_.activation(lg[:], lg[:], ACT.Ln, bias=1.0).then_inc(S["l_done"], 1)
                    softmax([(0, P), (P, SWC)], sinks[:, ds(i + GRP * u, 1)], hd + (KV + 1))

                    def gate(j):
                        return lambda: a_.activation(flat(gates[:, ds(i * 4 + j, 1), :]), main(j), ACT.Identity,
                                                     bias=par[:, ds(i * 4 + j, 1)]).then_inc(S["ev_a"], 1)
                    step(i + IT_ATT, 2 * u, gate(2 * u))
                    act.wait_ge(S["e_done"], hd + 2)
                    a_.activation(spb[:], lg[:], ACT.Exp).then_inc(S["a_done"], 1)
                    act.wait_ge(S["pT_ps"], hd + (KV + 1))
                    act.wait_ge(S["o_sw"], hd + KV)
                    a_.activation(pT[:], ps[5][:, 0:SWC], ACT.Copy).then_inc(S["pT_sb"], 1)
                    step(i + IT_ATT, 2 * u + 1, gate(2 * u + 1))
                    act.wait_ge(S["o_sb"], hd + 2)
                    a_.activation(flat(qT[:, ds(hd, 1), :]), ps[6][:, 0:NT], ACT.Copy).then_inc(S["o_sb_ev"], 1)
                own.leave(IT_PROJ - IT_ATT)
            act.wait_ge(S["o_sw"], KV + H)
            act.wait_ge(S["vst_st"], 2 * H)
            act.wait_ge(S["o_sb_ev"], H + 1)
            act.wait_ge(S["o_sw_ev"], KV + H)
            for h in range(2 * H):
                a_.activation(oh[:, h, :], qT[:, h, :], ACT.Copy).then_inc(S["oh_done"], 1)
            with act.Fori(0, IT_OUT - IT_PROJ) as i:
                it = i + IT_PROJ
                for j in range(2):
                    step(it, j, None, i * 32 + (16 * IT_PROJ + 32))
                for j in range(2):
                    m = i * 2 + j
                    act.wait_ge(S["m_done"], m + 1)
                    a_.activation(sg1[:], flat(gates[:, ds(m, 1), :]), ACT.Sigmoid).then_inc(S["sig_done"], 1)
                    a_.activation(sg2[:], main(j), ACT.Sigmoid, bias=par[:, ds(m + KT, 1)]).then_inc(S["ev_a"], 1)

                    def high():
                        act.wait_ge(S["m_done"], m + 2)
                        a_.activation(flat(mh[:, ds((i + 1) * 2 + (j - 2), 1), :]), m1[:], ACT.Copy).then_inc(S["mh_done"], 1)
                    step(it, 2 + j, high)
            slot1 = 16 * IT_PROJ + 32 * (IT_OUT - IT_PROJ)
            with act.Fori(0, IT_END - IT_OUT - 1) as i:
                for j in range(4):
                    step(i + IT_OUT, j, None, i * 16 + (slot1 + 16))
            for j in range(2):
                step(IT_END - 1, j, None, slot1 + 16 * (IT_END - IT_OUT))
            for n in range(0, 12, 2):
                t, q = n // 4, n % 4
                act.wait_ge(S["x2_ps"], n + 1)
                a_.activation(x2[0:TILES[t], t, q * 512:(q + 1) * 512], ps[n % 4][0:TILES[t], :], ACT.Copy)\
                    .then_inc(S["x2_a"], 1)
                if q == 2:
                    act.wait_ge(S["x2_a"], 2 * t + 2)
                    act.wait_ge(S["x2_d"], 2 * t + 2)
                    if t:
                        act.wait_ge(S["ssq2"], t)
                    m = TILES[t]
                    a_.activation(squares2[0:m], x2[0:m, t, :], ACT.Square, accum_out=stat[0:m, t:t + 1])\
                        .then_inc(S["ssq2"], 1)
            act.wait_ge(S["rms"], 3)
            a_.activation(stat[:, 16:19], stat[:, 4:7], ACT.Sqrt).then_inc(S["rms"], 1)
            act.wait_ge(S["ex_in"], 1)
            a_.activation(gex, gex, ACT.Exp).then_inc(S["ex_out"], 1)
            act.wait_ge(S["ex_in"], 2)
            a_.activation(d21, d21, ACT.Exp).then_inc(S["ex_out"], 1)

            def high(s, c):
                sem, w = piece(c)
                act.wait_ge(S[sem], s * 16 + 16 * (1 + c // CH))
                act.wait_ge(S["ch_used"], used(s, c - AHEAD - 1))
                a_.activation(eh[c % 4][:], w, ACT.Copy).then_inc(S["eh_ready"], 1)

            def tokens_high(s):
                act.wait_ge(S["hg_sb"], s * 2 + 2)
                if not isinstance(s, int) or s:
                    act.wait_ge(S["ch_used"], used(s, 15 - CH))
                a_.activation(hgx[:, :, 0:SLOTS], hg[:], ACT.Copy).then_inc(S["hgh_done"], 1)

            def expert(s, nxt):
                for c in range(AHEAD, 11):
                    high(s, c)
                act.wait_ge(S["ch_used"], used(s, 7))
                act.wait_ge(S["a_ready"], s + 1)
                act.wait_ge(S["aT_ps"], s + 1)
                a_.activation(g_sb[:], ps[2][SLOTS:P, :], ACT.Copy).then_inc(S["g_low"], 1)
                high(s, 11)
                high(s, 12)
                act.wait_ge(S["g_sum"], s + 1)
                a_.activation(g_sb[:], g_sb[:], ACT.Silu).then_inc(S["silu_done"], 1)
                for c in range(13, 19):
                    high(s, c)
                act.wait_ge(S["ch_used"], used(s, 15))
                a_.activation(u_sb[:], ps[3][SLOTS:P, :], ACT.Copy).then_inc(S["u_low"], 1)
                high(s, 19)
                act.wait_ge(S["aT_ps"], s + 2)
                a_.activation(aTx[:, :, 0:SLOTS], ps[2][:, 0:FT * SLOTS].rearrange("p (f n) -> p f n", f=FT), ACT.Copy)\
                    .then_inc(S["aTh_done"], 1)
                high(s, 20)
                high(s, 21)
                if nxt:
                    tokens_high(s + 1)
                high(s, 22)
                high(s, 23)
                if nxt:
                    for c in range(AHEAD):
                        high(s, CH + c)
                act.wait_ge(S["ch_used"], used(s, CH - 1))
                act.wait_ge(S["y_free"], s + 1)
                for q in range(4):
                    a_.activation(y_sb[:, q * 512:(q + 1) * 512], ps[4 + q][SLOTS:P, :], ACT.Copy)\
                        .then_inc(S["y_act"], 1)

            for c in range(AHEAD):
                high(0, c)
            tokens_high(0)
            with act.Fori(0, NE - 1) as e:
                expert(e, True)
            expert(NE - 1, False)
            act.wait_ge(S["ints_ready"], 1)
            more = act.value_load(ints[0:1, MAXOV:MAXOV + 1], min_val=0, max_val=MAXOV)
            with act.If(more > 0):
                with act.Fori(0, more) as i:
                    tokens_high(i + NE)
                    for c in range(AHEAD):
                        high(i + NE, c)
                    expert(i + NE, False)
            for t, n in enumerate(TILES):
                act.wait_ge(S["sum_done"], t + 1)
                a_.activation(yb[t][0:n], ya[t][0:n], ACT.Square, accum_out=stat[0:n, t:t + 1])\
                    .then_inc(S["ssq3"], 1)
                act.wait_ge(S["rms"], 5 + 2 * t)
                a_.activation(stat[0:n, 16 + t:17 + t], stat[0:n, 4 + t:5 + t], ACT.Sqrt).then_inc(S["rms"], 1)

        @block.tensor
        def _(pe):
            mm_, tr = nc.tensor.matmul, nc.tensor.transpose
            ident = con[:, C_ID:C_ID + P]
            ones = con[:, C_ONE:C_ONE + P]
            pe.wait_ge(S["const_in"], 16 * 4)
            tr(ps[1][:, 0:64], par_nat[:], ident[0:64, 0:64]).then_inc(S["par_ps"], 1)
            pe.wait_ge(S["kc_in"], 16)
            for n in range(2):
                for h in range(4):
                    k0 = (4 * n + h) * P
                    mm = tr(ps[5 + n][:, h * P:(h + 1) * P], kc_nat[:, k0:k0 + P], ident)
                mm.then_inc(S["kc_ps"], 1)
            pe.wait_ge(S["diag_done"], 3)
            for t, n in enumerate(TILES):
                mm = mm_(ps[7][:, 64 + t * P:64 + t * P + n], ones[0:n, :], diag[0:n, t, 0:n], start=True, stop=True)
            mm.then_inc(S["rb_ps"], 1)
            pe.wait_ge(S["x_in"], 32)
            for k in range(KT):
                if k >= 3:
                    pe.wait_ge(S["xT_done"], k - 2)
                for t, n in enumerate(TILES):
                    mm = tr(ps[2 + k % 3][:, t * P:t * P + n], x_nat[0:n, t, k * P:(k + 1) * P], ident[0:n, 0:n])
                mm.then_inc(S["x_turned"], 1)

            def products(it, j, hi, lo, sums=None):
                pe.wait_ge(S["wl_ready"], upto(it, j))
                for dst, k0, k1 in sums or ((main(j), 0, KT),):
                    for k in range(k0, k1):
                        mm_(dst, wh[:, j % 2, k, :], hi[:, k, :], start=(k == k0), stop=False)
                        mm_(dst, wh[:, j % 2, k, :], lo[:, k, :], start=False, stop=False)
                        mm = mm_(dst, wl[:, j % 2, k, :], hi[:, k, :], start=False, stop=(k == k1 - 1))
                mm.then_inc(S["blk"], 1)

            def turn(src, j):
                for t in range(3):
                    mm = tr(ps[5 + j % 2][:, t * P:(t + 1) * P], src[:, t * P:(t + 1) * P], ident)
                mm.then_inc(S["h_turned"], 1)

            pe.wait_ge(S["xl_done"], KT)
            with pe.Fori(IT_QSB, IT_KSB) as it:
                for j in range(4):
                    pe.wait_ge(S["ev_a"], it * 4 + j + 1)
                    products(it, j, xh, xl)
            with pe.Fori(0, 4) as i:
                for j in range(4):
                    pe.wait_ge(S["ev_a"], i * 4 + (4 * IT_KSB + j + 1))
                    products(i + IT_KSB, j, xh, xl)
                    if j:
                        pe.wait_ge(S["ev_a"], i * 4 + (4 * IT_KSB + 1 + j + 1))
                        pe.wait_ge(S["nat_done"], i * 4 + max(j - 2, 0) + 1)
                        turn(headT[:, j - 1], j - 1)
                pe.wait_ge(S["ev_a"], i * 4 + (4 * IT_KSB + 5 + 1))
                pe.wait_ge(S["nat_done"], i * 4 + 3)
                turn(headT[:, 3], 3)
            with pe.Fori(0, 2) as i:
                for j in range(4):
                    if j < 2:
                        pe.wait_ge(S["ev_a"], 24 + j + 1)
                    pe.wait_ge(S["ev_d"], i * 4 + j + 1)
                    products(i + IT_QSW, j, xh, xl)
            for j in range(4):
                pe.wait_ge(S["ev_d"], EV_KVSW_D - 1 + j + 1)
                products(IT_KVSW, j, xh, xl)
                if j:
                    if j < 3:
                        pe.wait_ge(S["rope_done"], 8 + j + 1)
                    else:
                        pe.wait_ge(S["ev_a"], EV_KVSW_A + 1 + 1)
                    pe.wait_ge(S["nat_done"], 16 + max(j - 2, 0) + 1)
                    turn(kT_sw[:, j - 1] if j < 3 else headT[:, 2], j - 1)
            pe.wait_ge(S["ev_a"], EV_ATT + 1)
            pe.wait_ge(S["nat_done"], 19)
            turn(headT[:, 3], 3)
            pe.wait_ge(S["swc_in"], 32)
            pe.wait_ge(S["nat_done"], 21)
            for g in range(KV):
                mm = tr(ps[6][:, g * P:(g + 1) * P], kcw_nat[:, g * P:(g + 1) * P], ident)
            mm.then_inc(S["kc_ps"], 1)
            pe.wait_ge(S["kc_sb"], 3)
            pe.wait_ge(S["pool_head"], 18)
            for g in range(KV):
                pe.wait_ge(S["zw_done"], g)
                pe.wait_ge(S["qst_st"], g + 1)
                lhs = qst[:, g * P:(g + 1) * P]
                mm_(ps[4][:, 0:P], lhs, kcT_sw[:, g, :], start=True, stop=True)
                mm_(ps[4][:, P:SSC], lhs, kT_sw[:, g, SEQ:NT], start=True, stop=True).then_inc(S["z_sw"], 1)
                pe.wait_ge(S["p_ready"], g + 1)
                pe.wait_ge(S["pT_sb"], 2 * g)
                tr(ps[5][:, 0:P], zw[:, 0:P], ident)
                tr(ps[5][0:DEC, P:2 * P], zw[:, P:SSC], ident).then_inc(S["pT_ps"], 1)
                pe.wait_ge(S["pT_sb"], 2 * g + 2)
                pe.wait_ge(S["o_sw_ev"], g)
                mm_(ps[7][:, 0:P], vc_sw[:, g * P:(g + 1) * P], pT[:, 0:P], start=True, stop=False)
                mm_(ps[7][:, 0:P], v_sw[0:DEC, 2, g * P:(g + 1) * P], pT[0:DEC, P:2 * P], start=False, stop=True)\
                    .then_inc(S["o_sw"], 1)

            with pe.Fori(0, IT_PROJ - IT_ATT) as i:
                for u in range(2):
                    hd = i * 2 + u

                    def q(a, b):
                        return flat(qT[:, ds(hd, 1), a:b])

                    def gate_block(j):
                        pe.wait_ge(S["ev_a"], i * 4 + (EV_ATT - 1 + j + 1))
                        products(i + IT_ATT, j, xh, xl)

                    pe.wait_ge(S["kst_st"], hd * 2 + 2)
                    pe.wait_ge(S["zm_done"], hd + 1)
                    mm_(ps[2][:, 0:SEQ], kst[:, 0, :], q(0, SEQ), start=True, stop=True)
                    mm_(ps[2][:, SEQ:SEQ + P], kst[:, 1, :], q(P, SEQ), start=True, stop=True)
                    mm_(ps[2][:, SEQ + P:SEQ + P + DEC], kst[:, 3, :], q(SEQ, NT), start=True, stop=True)
                    mm_(ps[2][:, SEQ + P + DEC:SBC], kst[:, 2, :], q(SEQ, NT), start=True, stop=True)\
                        .then_inc(S["z_sb"], 1)
                    pe.wait_ge(S["qst_st"], hd + (KV + 1))
                    pe.wait_ge(S["zw_done"], hd + KV)
                    mm_(ps[4][:, 0:P], qst[:, 0:P], kT_sw[:, u, 0:P], start=True, stop=True)
                    mm_(ps[4][:, P:SWC], qst[:, P:SEQ], kT_sw[:, u, 0:SEQ], start=True, stop=True)\
                        .then_inc(S["z_sw"], 1)
                    gate_block(2 * u)
                    pe.wait_ge(S["sp_done"], hd + 1)
                    pe.wait_ge(S["e_done"], hd + 1)
                    mm_(ps[3][:, 0:SBC], con[:, C_TRI:C_TRI + P], spb[:], start=True, stop=False)
                    mm_(ps[3][:, P:SEQ], ones, spb[:, SEQ:SEQ + P], start=False, stop=False)
                    mm_(ps[3][:, SEQ + P:SEQ + P + DEC], ones, spb[:, SEQ + P + DEC:SBC], start=False, stop=True)\
                        .then_inc(S["c_done"], 1)
                    pe.wait_ge(S["p_ready"], hd + (KV + 1))
                    pe.wait_ge(S["pT_sb"], hd + 2 * KV)
                    for c in range(3):
                        mm = tr(ps[5][:, c * P:(c + 1) * P], zw[:, c * P:(c + 1) * P], ident)
                    mm.then_inc(S["pT_ps"], 1)
                    gate_block(2 * u + 1)
                    pe.wait_ge(S["a_done"], hd + 1)
                    pe.wait_ge(S["vst_st"], hd * 2 + 2)
                    pe.wait_ge(S["o_sb_ev"], hd + 1)
                    mm_(ps[6][:, 0:SEQ], vst[:, 0, :], spb[:, 0:SEQ], start=True, stop=False, skip_group_check=True)
                    mm_(ps[6][:, P:SEQ], vst[:, 1, :], spb[:, SEQ:SEQ + P], start=False, stop=False,
                        skip_group_check=True)
                    mm_(ps[6][:, SEQ:NT], vst[:, 3, :], spb[:, SEQ + P:SEQ + P + DEC], start=False, stop=False,
                        skip_group_check=True)
                    mm_(ps[6][:, SEQ:NT], vst[:, 2, :], spb[:, SEQ + P + DEC:SBC], start=False, stop=True,
                        skip_group_check=True).then_inc(S["o_sb"], 1)
                    pe.wait_ge(S["pT_sb"], hd + (2 * KV + 1))
                    pe.wait_ge(S["o_sw_ev"], hd + KV)
                    mm_(ps[7][:, 0:SEQ], v_sw[:, 0, u * P:(u + 1) * P], pT[:, 0:SEQ], start=True, stop=False)
                    mm_(ps[7][:, P:SEQ], v_sw[:, 1, u * P:(u + 1) * P], pT[:, SEQ:SWC], start=False, stop=True)\
                        .then_inc(S["o_sw"], 1)

            with pe.Fori(0, IT_OUT - IT_PROJ) as i:
                it = i + IT_PROJ
                for j in range(2):
                    pe.wait_ge(S["ev_a"], i * 2 + (EV_PROJ - 1 + j + 1))
                    products(it, j, xh, xl)
                pe.wait_ge(S["ol_done"], 2 * H)
                pe.wait_ge(S["m_done"], i * 2 + 1)
                for j in range(2):
                    products(it, 2 + j, oh, ol, ((ps[2 + j][:, 0:NT], 0, H), (ps[4 + j][:, 0:NT], H, 2 * H)))
            pe.wait_ge(S["ev_a"], EV_PROJ + 16 + 1)
            pe.wait_ge(S["ml_done"], KT + 1)
            with pe.Fori(0, IT_END - IT_OUT) as i:
                for j in range(4):
                    pe.wait_ge(S["ev_d"], i * 4 + (EV_OUT_D - 1 + j + 1))
                    products(i + IT_OUT, j, mh, ml)
            pe.wait_ge(S["ev_d"], EV_OUT_D + KT + 1)
            for n in range(12):
                t, q = n // 4, n % 4
                if n >= 4:
                    pe.wait_ge(S["x2_d" if n % 2 else "x2_a"], n // 2 - 1)
                for k in range(4):
                    mm = tr(ps[n % 4][0:TILES[t], k * P:(k + 1) * P], xT[:, 4 * q + k, tok(t)], ident)
                mm.then_inc(S["x2_ps"], 1)
            pe.wait_ge(S["wr_scaled"], 1)
            for t, n in enumerate(TILES):
                for k in range(KT):
                    mm = mm_(ps[7][0:n, t * 32:t * 32 + NL], xT[:, k, tok(t)], wr[:, k, :],
                             start=(k == 0), stop=(k == KT - 1))
            mm.then_inc(S["lg_ps"], 1)
            pe.wait_ge(S["lg_ps"], 1)
            pe.sem_inc(S["ch_used"], AHEAD + 1)
            pe.wait_ge(S["masks"], 1)
            su = con[:, C_SU:C_SU + P]
            for t in range(3):
                for s in range(t + 1):
                    mm_(ps[6][:, t * NE:(t + 1) * NE], su if s == t else ones, MM[:, s, :],
                        start=(s == 0), stop=(s == t))
            for s in range(3):
                mm = mm_(ps[6][:, 3 * NE:4 * NE], ones, MM[:, s, :], start=(s == 0), stop=(s == 2))
            mm.then_inc(S["rk_ps"], 1)

            def gather(s, ks):
                if ks[0] == 0:
                    pe.wait_ge(S["picked"], s * 3 + 3)
                    if not isinstance(s, int) or s:
                        pe.wait_ge(S["hg_sb"], s * 2)
                for k in ks:
                    for t, n in enumerate(TILES):
                        mm = mm_(ps[k // 8][:, (k % 8) * SLOTS:(k % 8 + 1) * SLOTS], x2[0:n, t, k * P:(k + 1) * P],
                                 pick[0:n, t, :], start=(t == 0), stop=(t == 2))
                if ks[-1] == KT - 1:
                    mm.then_inc(S["hg_ps"], 1)

            def up_gate_piece(s, c):
                pe.wait_ge(S["el_ready"], s * CH + (c + 1))
                for low, part in enumerate((eh[c % 4], el[c % 4])):
                    for k in range(2):
                        kt = c % 8 * 2 + k
                        mm = mm_(ps[2 + c // 8][:], hgx[:, kt, :], part[:, k * DE:(k + 1) * DE],
                                 start=(low == 0 and kt == 0), stop=(low == 1 and kt == KT - 1))
                mm.then_inc(S["ch_used"], 1)

            def expert(s, nxt):
                pe.wait_ge(S["hgl_done"], s + 1)
                pe.wait_ge(S["aTl_done"], s + 1)
                for c in range(16):
                    up_gate_piece(s, c)
                    if nxt and c >= 4:
                        gather(s + 1, range(c - 4, c - 3))
                if nxt:
                    gather(s + 1, range(12, 14))
                pe.wait_ge(S["a_ready"], s + 2)
                for f in range(FT):
                    mm = mm_(ps[2][:, f * SLOTS:(f + 1) * SLOTS], g_sb[:, f * P:(f + 1) * P],
                             ident[0:SLOTS, 0:SLOTS], start=True, stop=True)
                mm.then_inc(S["aT_ps"], 1)
                if nxt:
                    gather(s + 1, range(14, 16))
                pe.wait_ge(S["aTl_done"], s + 2)
                pe.wait_ge(S["y_dve"], s * 4 + 1)
                for c in range(16, CH):
                    f, q0 = (c - 16) // 2, c % 2 * 2
                    pe.wait_ge(S["el_ready"], s * CH + (c + 1))
                    for low, part in enumerate((eh[c % 4], el[c % 4])):
                        for q in range(2):
                            mm = mm_(ps[4 + q0 + q][:], aTx[:, f, :], part[:, q * 512:(q + 1) * 512],
                                     start=(low == 0 and f == 0), stop=(low == 1 and f == FT - 1))
                    mm.then_inc(S["ch_used"], 1)

            pe.wait_ge(S["rk_done"], 1)
            gather(0, range(KT))
            with pe.Fori(0, NE - 1) as e:
                expert(e, True)
            expert(NE - 1, False)
            pe.wait_ge(S["ints_ready"], 1)
            more = pe.value_load(ints[0:1, MAXOV:MAXOV + 1], min_val=0, max_val=MAXOV)
            with pe.If(more > 0):
                with pe.Fori(0, more) as i:
                    gather(i + NE, range(KT))
                    expert(i + NE, False)

        @block.vector
        def _(dve):
            own = Steps(dve, S["dve_own"])

            def then(ins):
                own(ins)
                own.wait()

            then(v.memset(stat[:], 1.0))

            def rms():
                v.tensor_scalar(stat[:, 4:7], stat[:, 0:3], 1.0 / D, EPS, ALU.mult, ALU.add).then_inc(S["rms"], 1)

            def inverse(n, a, b):
                m, inv, root, t = (stat[0:n, c + a:c + b] for c in (4, 8, 16, 20))
                then(v.reciprocal(inv, root))
                then(v.tensor_tensor(t, inv, inv, ALU.mult))
                then(v.tensor_tensor(t, t, m, ALU.mult))
                then(v.tensor_scalar(t, t, -0.5, 1.5, ALU.mult, ALU.add))
                then(v.tensor_tensor(inv, inv, t, ALU.mult))

            dve.wait_ge(S["act_own"], 3)
            rms()
            dve.wait_ge(S["rms"], 2)
            inverse(P, 0, 3)
            dve.wait_ge(S["const_in"], 16 * 4)
            for t in range(3):
                v.tensor_scalar(diag[:, t, :], con[:, C_ID:C_ID + P], stat[:, 8 + t:9 + t], None, ALU.mult)\
                    .then_inc(S["diag_done"], 1)
            dve.wait_ge(S["rb_ps"], 1)
            then(v.tensor_copy(rstd_b[:], ps[7][:, 64:64 + NT]))
            dve.wait_ge(S["par_sb"], 1)

            def low(k):
                dve.wait_ge(S["xh_done"], k + 1)
                v.tensor_tensor(xl[:, k, :], hbuf[:, k % 2, :], xh[:, k, :].bitcast(F32), ALU.subtract)\
                    .then_inc(S["xl_done"], 1)

            for k in range(KT):
                dve.wait_ge(S["xT_done"], k + 1)
                if k > 1:
                    dve.wait_ge(S["xl_done"], k - 1)
                v.scalar_tensor_tensor(out=hbuf[:, k % 2, :], in0=xT[:, k, :], scalar=par[:, 32 + k:33 + k],
                                       in1=rstd_b[:], op0=ALU.mult, op1=ALU.mult).then_inc(S["h_done"], 1)
                if k:
                    low(k - 1)
            low(KT - 1)

            def split(j, b):
                dve.wait_ge(S["wh_ready"], b)
                v.tensor_tensor(wl[:, j % 2], raw(j), wh[:, j % 2].bitcast(F32), ALU.subtract)\
                    .then_inc(S["wl_ready"], 1)

            split(0, 1)
            split(1, 2)
            own(v.memset(headT[:, :, NT:], 0.0))
            v.memset(kT_sb[:, :, NT:], 0.0).then_inc(S["ev_d"], 1)
            v.memset(kT_sw[:, :, NT:], 0.0).then_inc(S["pads"], 1)
            with dve.Fori(IT_QSB, IT_KSB) as it:
                for j in range(4):
                    split((j + 2) % 4, it * 4 + (j + 3))

            def token_major(n, j):
                dve.wait_ge(S["h_turned"], n + 1)
                v.tensor_copy(nat[:, :, j * P:(j + 1) * P], ps[5 + j % 2][:, 0:3 * P].rearrange("p (t n) -> p t n", t=3))\
                    .then_inc(S["nat_done"], 1)

            with dve.Fori(0, 4) as i:
                for j in range(4):
                    if j == 1:
                        dve.wait_ge(S["nat_free"], i + 1)
                        dve.wait_ge(S["pool_head"], i * 4 + 1)
                    if j:
                        token_major(i * 4 + j, j - 1)
                    if j == 3:
                        token_major(i * 4 + 4, 3)
                    split((j + 2) % 4, i * 4 + (4 * IT_KSB + j + 3))

            def rotary(j):
                h = HD // 2
                src = main(j)
                own(v.tensor_tensor(rope_a[:], src, con[:, C_COS:C_COS + NT], ALU.mult))
                own(v.tensor_tensor(rope_b[0:h], src[h:P], con[h:P, C_SIN:C_SIN + NT], ALU.mult))
                v.tensor_tensor(rope_b[h:P], src[0:h], con[0:h, C_SIN:C_SIN + NT], ALU.mult).then_inc(S["ev_d"], 1)
                own.wait()

            dve.wait_ge(S["xT_out"], 16)
            with dve.Fori(0, 2) as i:
                own.enter(i, 8)
                for j in range(4):
                    dve.wait_ge(S["blk"], i * 4 + (4 * IT_QSW + j + 1))
                    dve.wait_ge(S["rope_done"], i * 4 + j + 1)
                    rotary(j)
                    dve.wait_ge(S["ev_d"], i * 4 + (j + 2 + 1))
                    v.tensor_tensor(flat(qT[:, ds(i * 4 + (H + j), 1), :]), rope_a[:], rope_b[:], ALU.add)\
                        .then_inc(S["rope_done"], 1)
                    split((j + 2) % 4, i * 4 + (4 * IT_QSW + j + 3))
                own.leave(2)
            for j in range(4):
                if j < 2:
                    dve.wait_ge(S["blk"], upto(IT_KVSW, j))
                    dve.wait_ge(S["rope_done"], 8 + j + 1)
                    rotary(j)
                    dve.wait_ge(S["ev_d"], EV_KVSW_D + 1 + j + 1)
                    v.tensor_tensor(kT_sw[:, j, 0:NT], rope_a[:], rope_b[:], ALU.add).then_inc(S["rope_done"], 1)
                if j == 1:
                    dve.wait_ge(S["nat_free"], 5)
                    dve.wait_ge(S["pool_head"], 17)
                if j:
                    token_major(16 + j, j - 1)
                if j == 3:
                    token_major(20, 3)
                split((j + 2) % 4, upto(IT_KVSW, j + 2))

            def scores(n, width, mask, segments, sinks_of):
                dve.wait_ge(S["z_sw"], n)
                if not isinstance(n, int) or n > 1:
                    dve.wait_ge(S["pT_ps"], n - 1)
                then(v.scalar_tensor_tensor(out=zw[:, 0:width], in0=ps[4][:, 0:width], scalar=SCALE,
                                            in1=con[:, mask:mask + width], op0=ALU.mult, op1=ALU.add))
                for c, (a, b) in enumerate(segments):
                    own(v.tensor_reduce(st[:, c:c + 1], zw[:, a:b], AX, ALU.max))
                own.wait()
                c = len(segments)
                v.tensor_scalar(st[:, 2:2 + c], st[:, 0:c], sinks_of, -1.0, ALU.max, ALU.mult).then_inc(S["zw_done"], 1)

            def divide(sums, segments):
                dve.wait_ge(S["sums_done"], sums)
                c = len(segments)
                then(v.tensor_tensor(st[:, 8:8 + c], st[:, 4:4 + c], st[:, 6:6 + c], ALU.add))
                then(v.reciprocal(st[:, 10:10 + c], st[:, 8:8 + c]))
                for n, (a, b) in enumerate(segments):
                    ins = v.tensor_scalar(zw[:, a:b], zw[:, a:b], st[:, 10 + n:11 + n], None, ALU.mult)
                    if n == c - 1:
                        ins.then_inc(S["p_ready"], 1)

            dve.wait_ge(S["small_in"], 16 * 13)
            for g in range(KV):
                scores(g + 1, SSC, C_MSS, [(0, SSC)], sinks_s[:, g:g + 1])
                divide(2 * g + 2, [(0, SSC)])
            heads = [(0, P), (P, SWC)]
            dve.wait_ge(S["zero_out"], 16 * 5)
            with dve.Fori(0, IT_PROJ - IT_ATT) as i:
                own.enter(i, 10)
                for u in range(2):
                    hd = i * 2 + u
                    dve.wait_ge(S["z_sb"], hd + 2)
                    v.scalar_tensor_tensor(out=zm[:], in0=ps[2][:, 0:SBC], scalar=SCALE, in1=con[:, C_MSB:C_MSB + SBC],
                                           op0=ALU.mult, op1=ALU.add).then_inc(S["zm_done"], 1)
                    scores(hd + (KV + 1), SWC, C_MSW, heads, sinks[:, ds(i + GRP * u, 1)])
                    dve.wait_ge(S["l_done"], hd + 1)
                    dve.wait_ge(S["o_sb"], hd + 1)
                    v.scalar_tensor_tensor(out=spb[:], in0=zm[:], scalar=0.0, in1=lg[:], op0=ALU.max, op1=ALU.add)\
                        .then_inc(S["sp_done"], 1)
                    divide(hd * 3 + (2 * KV + 3), heads)
                    split((2 * u + 2) % 4, i * 4 + (4 * IT_ATT + 2 * u + 3))
                    dve.wait_ge(S["c_done"], hd + 1)
                    v.tensor_tensor(lg[:], zm[:], ps[3][:, 0:SBC], ALU.subtract).then_inc(S["e_done"], 1)
                    split((2 * u + 3) % 4, i * 4 + (4 * IT_ATT + 2 * u + 4))
                    dve.wait_ge(S["o_sw"], hd + (KV + 1))
                    v.tensor_copy(flat(qT[:, ds(i + (H + GRP * u), 1), 0:SEQ]), ps[7][:, 0:SEQ])\
                        .then_inc(S["o_sw_ev"], 1)
                own.leave(IT_PROJ - IT_ATT)
            for h in range(2 * H):
                dve.wait_ge(S["oh_done"], h + 1)
                v.tensor_tensor(ol[:, h, :], qT[:, h, :], oh[:, h, :].bitcast(F32), ALU.subtract)\
                    .then_inc(S["ol_done"], 1)
            with dve.Fori(0, IT_OUT - IT_PROJ) as i:
                own.enter(i, 4)
                for j in range(2):
                    split(j + 2, i * 4 + (4 * IT_PROJ + j + 3))
                for j in range(2):
                    m = i * 2 + j
                    dve.wait_ge(S["sig_done"], m + 1)
                    dve.wait_ge(S["blk"], i * 4 + (4 * IT_PROJ + 3 + j))
                    dve.wait_ge(S["ml_done"], m + 1)
                    own(v.tensor_tensor(m1[:], sg1[:], ps[2 + j][:, 0:NT], ALU.mult))
                    dve.wait_ge(S["ev_a"], m + (EV_PROJ + 1 + 1))
                    own(v.tensor_tensor(m2[:], sg2[:], ps[4 + j][:, 0:NT], ALU.mult))
                    own.wait()
                    v.tensor_tensor(m1[:], m1[:], m2[:], ALU.add).then_inc(S["m_done"], 1)
                    dve.wait_ge(S["mh_done"], m + 1)
                    v.tensor_tensor(flat(ml[:, ds(m, 1), :]), m1[:], flat(mh[:, ds(m, 1), :]).bitcast(F32),
                                    ALU.subtract).then_inc(S["ml_done"], 1)
                    split(j, i * 4 + (4 * IT_PROJ + j + 5))
                own.leave(IT_OUT - IT_PROJ)
            dve.wait_ge(S["xT_in"], 16)

            def residual(it, j, m):
                dve.wait_ge(S["blk"], upto(it, j))
                v.tensor_tensor(m, m, main(j), ALU.add).then_inc(S["ev_d"], 1)

            with dve.Fori(0, IT_END - IT_OUT - 1) as i:
                for j in range(4):
                    residual(i + IT_OUT, j, flat(xT[:, ds(i * 4 + j, 1), :]))
                    split((j + 2) % 4, i * 4 + (4 * IT_OUT + j + 3))
            for j in range(4):
                residual(IT_END - 1, j, xT[:, KT - 4 + j, :])
                if j < 2:
                    split(j + 2, upto(IT_END - 1, j + 2))
                if j == 2:
                    v.tensor_tensor(wr[:], wr[:], par[:, 48:64].rearrange("p (k a) -> p k a", a=1)
                                    .to_broadcast([P, KT, NL]), ALU.mult).then_inc(S["wr_scaled"], 1)
            for n in range(1, 12, 2):
                t, q = n // 4, n % 4
                dve.wait_ge(S["x2_ps"], n + 1)
                v.tensor_copy(x2[0:TILES[t], t, q * 512:(q + 1) * 512], ps[n % 4][0:TILES[t], :])\
                    .then_inc(S["x2_d"], 1)
            own(v.memset(lgt, 0.0))
            own(v.memset(rk[:], -FAR))
            own(v.memset(gl8, NEG))
            dve.wait_ge(S["ssq2"], 3)
            rms()
            dve.wait_ge(S["rms"], 4)
            inverse(P, 0, 3)
            dve.wait_ge(S["lg_ps"], 1)
            for t, n in enumerate(TILES):
                own(v.scalar_tensor_tensor(out=lgt[0:n, t, :], in0=ps[7][0:n, t * 32:t * 32 + NL],
                                           scalar=stat[0:n, 8 + t:9 + t], in1=br[0:n], op0=ALU.mult, op1=ALU.add))
            own.wait()
            then(v.tensor_copy(gl8[:, :, 0:NG], lgt[:, :, 0:NG]))

            def wide(ap, n):
                return ap.rearrange("p (k a) -> p k a", a=1).to_broadcast([P, ap.shape[1], n])

            def each(ap, k):
                return ap.rearrange("p (a n) -> p a n", a=1).to_broadcast([P, k, ap.shape[1]])

            for t in range(3):
                own(v.max(gm8[:, t, :], gl8[:, t, :]))
            own.wait()
            for t in range(3):
                own(v.max_index(ri[:, 8 * t:8 * t + 8], gm8[:, t, :], gl8[:, t, :]))
            v.tensor_tensor(gex, gl8[:, :, 0:NG], gm8[:, :, 0:1].to_broadcast([P, 3, NG]),
                            ALU.subtract).then_inc(S["ex_in"], 1)
            own.wait()
            then(v.tensor_copy(gi, ri[:, 0:24:8]))
            then(v.tensor_tensor(gmask, wide(gi, NE), each(con[:, C_GRP:C_GRP + NE], 3), ALU.is_equal))
            own(v.tensor_tensor(em, gmask, lgt[:, :, NG:], ALU.mult))
            own(v.tensor_scalar(tmp, gmask, -NEG, NEG, ALU.mult, ALU.add))
            own.wait()
            then(v.tensor_tensor(em, em, tmp, ALU.add))
            for t in range(3):
                own(v.max(em8[:, t, :], em[:, t, :]))
            own.wait()
            for t in range(3):
                own(v.max_index(ri[:, 24 + 8 * t:32 + 8 * t], em8[:, t, :], em[:, t, :]))
            v.tensor_tensor(d21.rearrange("p (k a) -> p k a", a=1), em8[:, :, 1:2], em8[:, :, 0:1], ALU.subtract)\
                .then_inc(S["ex_in"], 1)
            own.wait()
            for c in range(2):
                own(v.tensor_copy(ei[:, c, :], ri[:, 24 + c:48:8]))
            own.wait()
            for c, M in enumerate((M1, M2)):
                own(v.tensor_tensor(M, wide(ei[:, c, :], NE), each(con[:, C_I16:C_I16 + NE], 3), ALU.is_equal))
            own.wait()
            then(v.tensor_tensor(MM, M1, M2, ALU.add))
            v.tensor_tensor(MM, MM, wide(con[:, C_VAL:C_VAL + 3], NE), ALU.mult).then_inc(S["masks"], 1)

            def low_part(s, c):
                dve.wait_ge(S["eh_ready"], s * CH + (c + 1))
                v.tensor_tensor(el[c % 4][:], piece(c)[1], eh[c % 4][:].bitcast(F32), ALU.subtract)\
                    .then_inc(S["el_ready"], 1)

            low_part(0, 0)
            dve.wait_ge(S["masks"], 1)
            dve.wait_ge(S["rk_ps"], 1)
            own(v.tensor_copy(rank, ps[6][:, 0:3 * NE].rearrange("p (t n) -> p t n", t=3)))
            own(v.tensor_copy(cnt, ps[6][:, 3 * NE:4 * NE]))
            own.wait()
            then(v.scalar_tensor_tensor(out=tmp, in0=rank, scalar=FAR, in1=MM, op0=ALU.add, op1=ALU.mult))
            v.tensor_scalar(rk[:, :, 0:NE], tmp, -FAR, None, ALU.add).then_inc(S["rk_done"], 1)
            dve.wait_ge(S["rk_done"], 1)

            def choose(column, t, n):
                v.tensor_scalar(pick[0:n, t, :], con[0:n, C_I64:C_I64 + SLOTS], column, stat[0:n, 8 + t:9 + t],
                                ALU.is_equal, ALU.mult).then_inc(S["picked"], 1)

            def gathered(s):
                dve.wait_ge(S["hg_ps"], s + 1)
                for n in range(2):
                    v.tensor_tensor(hg[:, 8 * n:8 * n + 8, :], ps[n][:].rearrange("p (k n) -> p k n", k=8),
                                    wide(par[:, 48 + 8 * n:56 + 8 * n], SLOTS), ALU.mult).then_inc(S["hg_sb"], 1)

            def tokens_low(s):
                dve.wait_ge(S["hgh_done"], s + 1)
                v.tensor_tensor(hgx[:, :, SLOTS:], hg[:], hgx[:, :, 0:SLOTS].bitcast(F32), ALU.subtract)\
                    .then_inc(S["hgl_done"], 1)

            for t, n in enumerate(TILES):
                choose(rk[0:n, t, 0:1], t, n)
            gathered(0)
            tokens_low(0)
            for c in range(1, AHEAD):
                low_part(0, c)
            dve.wait_ge(S["ex_out"], 2)
            own(v.tensor_reduce(gsum, gex, AX, ALU.add))
            own(v.tensor_scalar(dn, d21, 1.0, None, ALU.add))
            own.wait()
            own(v.reciprocal(gp, gsum))
            own(v.reciprocal(gi, dn))
            own.wait()
            then(v.tensor_tensor(wt[:, 0, :], gp, gi, ALU.mult))
            own(v.tensor_tensor(wt[:, 1, :], wt[:, 0, :], d21, ALU.mult))
            then(v.tensor_scalar(ov, cnt, float(SLOTS), None, ALU.is_gt))
            for c in range(2, -(-NT // SLOTS)):
                then(v.scalar_tensor_tensor(out=ov, in0=cnt, scalar=float(c * SLOTS), in1=ov, op0=ALU.is_gt,
                                            op1=ALU.add))
            then(v.tensor_tensor_scan(ovc, con[:, C_ONE:C_ONE + NE], ov, 0.0, ALU.mult, ALU.add))
            own(v.tensor_tensor(ovx, ovc, ov, ALU.subtract))
            own(v.tensor_tensor(sel, each(ovc, MAXOV), wide(con[:, C_I64:C_I64 + MAXOV], NE), ALU.is_le))
            own.wait()
            then(v.tensor_reduce(se, sel, AX, ALU.add))
            then(v.tensor_tensor(sel, sel, each(ov, MAXOV), ALU.mult))
            then(v.tensor_reduce(so, sel, AX, ALU.add))
            then(v.tensor_tensor(so, con[:, C_I64:C_I64 + MAXOV], so, ALU.subtract))
            own(v.tensor_scalar(so, so, 1.0, float(SLOTS), ALU.add, ALU.mult))
            own(v.tensor_scalar(se, se, float(NE - 1), None, ALU.min))
            own.wait()
            own(v.tensor_copy(ints[:, 0:MAXOV], se[0:1, :]))
            own.wait()
            v.tensor_copy(ints[:, MAXOV:MAXOV + 1], ovc[0:1, NE - 1:NE]).then_inc(S["ints_ready"], 1)
            for c, M in enumerate((M1, M2)):
                then(v.tensor_tensor(tmp, rank, M, ALU.mult))
                own(v.tensor_reduce(rr[:, c, :], tmp, AX, ALU.add))
                then(v.tensor_tensor(gmask, M, each(ovx, 3), ALU.mult))
                then(v.tensor_reduce(ro[:, c, :], gmask, AX, ALU.add))
            then(v.tensor_tensor(ro, ro, ei, ALU.subtract))
            own(v.tensor_scalar(ro, ro, float(NE - 1), float(SLOTS), ALU.add, ALU.mult))
            own(v.tensor_scalar(tmp[:, 0:2, 0:3], rr, float(SLOTS), None, ALU.is_ge))
            own.wait()
            own(v.tensor_tensor(ro, ro, tmp[:, 0:2, 0:3], ALU.mult))
            then(v.scalar_tensor_tensor(out=rr, in0=ei, scalar=float(SLOTS), in1=rr, op0=ALU.mult, op1=ALU.add))
            then(v.tensor_tensor(rr, rr, ro, ALU.add))
            v.tensor_copy(rows[:, 0:6].rearrange("p (t c) -> p c t", c=2), rr).then_inc(S["rows_ready"], 1)

            def expert(s, nxt):
                if nxt:
                    dve.wait_ge(S["hg_ps"], s + 1)
                    for t, n in enumerate(TILES):
                        choose(rk[0:n, t, ds(s + 1, 1)], t, n)
                for c in range(AHEAD, 11):
                    low_part(s, c)
                dve.wait_ge(S["g_low"], s + 1)
                v.tensor_tensor(g_sb[:], g_sb[:], ps[2][0:SLOTS, :], ALU.add).then_inc(S["g_sum"], 1)
                for c in range(11, 19):
                    low_part(s, c)
                dve.wait_ge(S["u_low"], s + 1)
                v.tensor_tensor(u_sb[:], u_sb[:], ps[3][0:SLOTS, :], ALU.add).then_inc(S["u_sum"], 1)
                dve.wait_ge(S["u_sum"], s + 1)
                dve.wait_ge(S["silu_done"], s + 1)
                v.tensor_tensor(g_sb[:], g_sb[:], u_sb[:], ALU.mult).then_inc(S["a_ready"], 1)
                low_part(s, 19)
                dve.wait_ge(S["aTh_done"], s + 1)
                v.tensor_tensor(aTx[:, :, SLOTS:], ps[2][:, 0:FT * SLOTS].rearrange("p (f n) -> p f n", f=FT),
                                aTx[:, :, 0:SLOTS].bitcast(F32), ALU.subtract).then_inc(S["aTl_done"], 1)
                low_part(s, 20)
                if nxt:
                    gathered(s + 1)
                low_part(s, 21)
                low_part(s, 22)
                if nxt:
                    tokens_low(s + 1)
                low_part(s, 23)
                if nxt:
                    for c in range(AHEAD):
                        low_part(s, CH + c)
                for q in range(4):
                    dve.wait_ge(S["y_act"], s * 4 + (q + 2))
                    y = y_sb[:, q * 512:(q + 1) * 512]
                    v.tensor_tensor(y, y, ps[4 + q][0:SLOTS, :], ALU.add).then_inc(S["y_dve"], 1)

            with dve.Fori(0, NE - 1) as e:
                expert(e, True)
            expert(NE - 1, False)
            dve.wait_ge(S["ints_ready"], 1)
            more = dve.value_load(ints[0:1, MAXOV:MAXOV + 1], min_val=0, max_val=MAXOV)
            with dve.If(more > 0):
                with dve.Fori(0, more) as i:
                    e = dve.value_load(ints[0:1, ds(i, 1)], min_val=0, max_val=NE - 1)
                    dve.wait_ge(S["hg_ps"], i + NE)
                    v.tensor_scalar(rko[:, 0:3].rearrange("p (k a) -> p k a", a=1), rk[:, :, ds(e, 1)],
                                    so[:, ds(i, 1)], None, ALU.subtract).then_inc(S["rko_done"], 1)
                    dve.wait_ge(S["rko_done"], i + 1)
                    for t, n in enumerate(TILES):
                        choose(rko[0:n, t:t + 1], t, n)
                    gathered(i + NE)
                    tokens_low(i + NE)
                    for c in range(AHEAD):
                        low_part(i + NE, c)
                    expert(i + NE, False)
            dve.wait_ge(S["gf_in"], 16)
            for t, n in enumerate(TILES):
                dve.wait_ge(S[f"y_in{t}"], 32)
                v.scalar_tensor_tensor(out=ya[t][0:n], in0=ya[t][0:n], scalar=wt[0:n, 0, t:t + 1], in1=x2[0:n, t, :],
                                       op0=ALU.mult, op1=ALU.add).then_inc(S["half_done"], 1)
                dve.wait_ge(S["half_done"], t + 1)
                v.scalar_tensor_tensor(out=ya[t][0:n], in0=yb[t][0:n], scalar=wt[0:n, 1, t:t + 1], in1=ya[t][0:n],
                                       op0=ALU.mult, op1=ALU.add).then_inc(S["sum_done"], 1)
            for t, n in enumerate(TILES):
                dve.wait_ge(S["ssq3"], t + 1)
                v.tensor_scalar(stat[0:n, 4 + t:5 + t], stat[0:n, t:t + 1], 1.0 / D, EPS, ALU.mult, ALU.add)\
                    .then_inc(S["rms"], 1)
                dve.wait_ge(S["rms"], 6 + 2 * t)
                inverse(n, t, t + 1)
                v.scalar_tensor_tensor(out=ya[t][0:n], in0=ya[t][0:n], scalar=stat[0:n, 8 + t:9 + t], in1=gfin[0:n],
                                       op0=ALU.mult, op1=ALU.mult).then_inc(S["fin"], 1)


_INS = """x_prompt x_sample cache_sb_k cache_sb_v cache_swa_k cache_swa_v w_in b_gate swa_sink w_sb_o w_swa_o w_out
g_mix g_ffn w_rg b_rg w_re b_re w_e_gate w_e_up w_e_down g_final""".split()
_OUTS = [(1, SEQ, D), (1, DEC, D), (4, SEQ, 512), (4, DEC, 512), (P, 512), (DEC, 512), (2, PAST - DEC, KV * HD)]


def kernel(**inputs):
    import concourse.bacc as bacc
    from concourse.bass_utils import run_bass_kernel_spmd

    nc = bacc.Bacc("TRN2", target_bir_lowering=False, num_devices=1)
    arrays, args = {}, []
    for name, a in [(n, inputs[n]) for n in _INS] + [("const", constants())]:
        a = np.ascontiguousarray(a)
        arrays[f"in_{name}"] = a
        args.append(nc.dram_tensor(f"in_{name}", a.shape, F32, kind="ExternalInput").ap())
    for i, shape in enumerate(_OUTS):
        args.append(nc.dram_tensor(f"out_{i}", shape, F32, kind="ExternalOutput").ap())
    build(nc, *args)
    r = run_bass_kernel_spmd(nc, [arrays], core_ids=[0])
    yp, ys, kvp, kvs, wp, wn, wk = (r.results[0][f"out_{i}"] for i in range(len(_OUTS)))

    def heads(a, n):
        return a.reshape(1, 1, a.shape[0], n, HD)

    halves = [np.concatenate([x[2 * n], x[2 * n + 1]], axis=1) for x in (kvp, kvs) for n in range(2)]
    w = KV * HD
    return (yp, ys, heads(halves[0], H), heads(halves[1], H), heads(wp[:, :w], KV), heads(wp[:, w:], KV),
            heads(halves[2], H), heads(halves[3], H),
            heads(np.concatenate([wk[0], wn[:, :w]]), KV), heads(np.concatenate([wk[1], wn[:, w:]]), KV))
```

```python
from contextlib import ExitStack

import concourse.bass as bass
import numpy as np
from concourse import mybir

F32 = mybir.dt.float32
F32R = mybir.dt.float32r
BF16 = mybir.dt.bfloat16
I32 = mybir.dt.int32
U32 = mybir.dt.uint32
ACT = mybir.ActivationFunctionType
ALU = mybir.AluOpType
AX = mybir.AxisListType.X

P = 128
D = 2048
KT = D // P
SEQ, DEC, PAST = 256, 32, 128
NT = SEQ + DEC
NTP = 3 * P
TILES = (P, P, DEC)
HD = 128
H = 8
KV = 2
GRP = H // KV
CHUNK = 64
SBW = H * HD
GATE0 = 3 * SBW + H * HD + 2 * KV * HD
INW = GATE0 + 2 * D
NG, EPG = 4, 4
NE = NG * EPG
DE = 512
FT = DE // P
EPS = 1e-6
SCALE = HD ** -0.5
NEG = -1e30
SLOTS = 64
MAXOV = 2 * NT // SLOTS
NL = NG + NE
SBUF0 = 16640
PAIR = 2 * P
PIECE = D // 2
CH = 24
BY_POOL = (1, 9, 18)
AHEAD = 3
FAR = 1000.0

IT_QSB, IT_KSB, IT_VSB, IT_QSW, IT_KVSW, IT_ATT, IT_PROJ, IT_OUT, IT_END = 0, 2, 4, 6, 8, 9, 13, 21, 25

C_ID, C_TRI, C_SU, C_ONE = 0, 128, 256, 384
C_MSB = 512
SBC = 448
C_MSW = C_MSB + SBC
SWC = 384
C_MSS = C_MSW + SWC
SSC = 160
C_COS = C_MSS + SSC
C_SIN = C_COS + NT
C_I64 = C_SIN + NT
C_I16 = C_I64 + SLOTS
C_GRP = C_I16 + NE
C_VAL = C_GRP + NE
NC_ = C_VAL + 4


def constants():
    c = np.zeros((P, NC_), np.float32)
    r = np.arange(P)
    c[:, C_ID:C_ID + P] = np.eye(P)
    c[:, C_TRI:C_TRI + P] = r[:, None] >= r[None]
    c[:, C_SU:C_SU + P] = r[:, None] < r[None]
    c[:, C_ONE:C_ONE + P] = 1
    tri = np.where(r[:, None] < r[None], 0, NEG)
    c[:, C_MSB:C_MSB + P] = tri
    c[:, C_MSB + SEQ:C_MSB + SEQ + P] = tri
    c[:, C_MSB + SEQ + P + DEC:C_MSB + SBC] = tri[:, :DEC]
    for j, (q0, n) in enumerate(((0, P), (P, SEQ))):
        d = (q0 + r)[:, None] // CHUNK - np.arange(n)[None] // CHUNK
        at = C_MSW + j * P
        c[:, at:at + n] = np.where((d >= 0) & (d < 2), 0, NEG)
    d = (PAST + r % DEC)[:, None] // CHUNK - np.arange(SSC)[None] // CHUNK
    c[:, C_MSS:C_MSS + SSC] = np.where((d >= 0) & (d < 2), 0, NEG)
    half = HD // 2
    inv = np.power(np.float32(10000.0), -np.arange(half, dtype=np.float32) * np.float32(2.0 / HD))
    pos = np.concatenate([np.arange(SEQ), PAST + np.arange(DEC)]).astype(np.float32)
    ang = (pos[None] * inv[:, None].astype(np.float32)).astype(np.float32)
    c[:, C_COS:C_COS + NT] = np.tile(np.cos(ang), (2, 1))
    c[:half, C_SIN:C_SIN + NT] = np.sin(ang)
    c[half:, C_SIN:C_SIN + NT] = -np.sin(ang)
    c[:, C_I64:C_I64 + SLOTS] = np.arange(SLOTS)
    c[:, C_I16:C_I16 + NE] = np.arange(NE)
    c[:, C_GRP:C_GRP + NE] = np.arange(NE) // EPG
    for t, n in enumerate(TILES):
        c[:n, C_VAL + t] = 1
    return c


RAISED = """z_sb o_sb h_turned pool_head m_done a_ready y_out nat_done zm_done e_done o_sb_ev nat_free
            rope_done ml_done y_act y_dve aT_ps aTl_done table_in ev_a ev_d""".split()


class Steps:

    def __init__(self, eng, sem):
        self.eng, self.sem, self.n, self.i, self.per, self.base = eng, sem, 0, None, 0, 0

    def at(self):
        return self.n if self.i is None else self.i * self.per + (self.base + self.n)

    def __call__(self, ins):
        ins.then_inc(self.sem, 1)
        self.n += 1

    def wait(self):
        if self.i is None and self.n == 0:
            return
        self.eng.wait_ge(self.sem, self.at())

    def enter(self, i, per):
        self.base, self.i, self.per, self.n = self.n, i, per, 0

    def leave(self, trips):
        assert self.n == self.per, (self.n, self.per)
        self.n, self.i = self.base + self.per * trips, None



def build(nc, x_prompt, x_sample, cache_sb_k, cache_sb_v, cache_swa_k, cache_swa_v, w_in, b_gate, swa_sink,
          w_sb_o, w_swa_o, w_out, g_mix, g_ffn, w_rg, b_rg, w_re, b_re, w_e_gate, w_e_up, w_e_down, g_final,
          const, y_prompt, y_sample, sb_kv_prompt, sb_kv_sample, swa_kv_prompt, swa_kv_new, swa_kv_kept):
    xT_spill = nc.dram_tensor("xT_spill", (P, KT * NT), F32, kind="Internal").ap()
    y_rows = nc.dram_tensor("y_rows", ((NE + MAXOV) * SLOTS, D), F32, kind="Internal").ap()

    def at(name, kb, shape, dt=F32):
        return nc.alloc_sbuf_tensor_at(name, shape, dt, offset=SBUF0 + int(kb * 1024))

    ring = at("ring", 0, [P, 2, KT, PAIR])
    wh = at("wh", 32, [P, 2, KT, P], F32R)
    wl = at("wl", 48, [P, 2, KT, P], F32R)
    xh = at("xh", 64, [P, KT, NT], F32R)
    xl = at("xl", 82, [P, KT, NT], F32R)
    kT_sb = at("kT_sb", 100, [P, H, NTP])
    v_sb = at("v_sb", 112, [P, 3, SBW])
    vc_sb = at("vc_sb", 124, [P, SBW])
    kcT_sb = at("kcT_sb", 128, [P, H, P])
    kT_sw = at("kT_sw", 132, [P, KV, NTP])
    v_sw = at("v_sw", 135, [P, 3, KV * HD])
    oh = at("oh", 100, [P, 2 * H, NT], F32R)
    ol = at("ol", 118, [P, 2 * H, NT], F32R)
    x_nat = at("x_nat", 138, [P, 3, D])
    squares = at("squares", 162, [P, D])
    kc_nat = at("kc_nat", 170, [P, SBW])
    headT = at("headT", 138, [P, 4, NTP])
    nat = at("nat", 144, [P, 3, 4 * P])
    gates = at("gates", 138, [P, KT, NT])
    qT = at("qT", 156, [P, 2 * H, NT])
    mh = at("mh", 138, [P, KT, NT], F32R)
    ml = at("ml", 156, [P, KT, NT], F32R)
    xT = at("xT", 174, [P, KT, NT])
    kcT_sw = at("kcT_sw", 174, [P, KV, P])
    vc_sw = at("vc_sw", 175, [P, KV * HD])
    kst = at("kst", 176, [P, 4, P])
    vst = at("vst", 178, [P, 4, P])
    qst = at("qst", 180, [P, SEQ])
    zm = at("zm", 181, [P, SBC])
    lg = at("lg", 182.75, [P, SBC])
    spb = at("spb", 184.5, [P, SBC])
    zw = at("zw", 186.25, [P, SWC])
    pT = at("pT", 187.75, [P, SWC])
    st = at("st", 189.25, [P, 16])
    kcw_nat = at("kcw_nat", 189.5, [P, KV * HD])
    rope_a = at("rope_a", 181, [P, NT])
    rope_b = at("rope_b", 182.25, [P, NT])
    zero = at("zero", 184, [P, 512])
    sg1 = at("sg1", 174, [P, NT])
    sg2 = at("sg2", 175.25, [P, NT])
    m1 = at("m1", 176.5, [P, NT])
    m2 = at("m2", 177.75, [P, NT])
    diag = at("diag", 112, [P, 3, P])
    rstd_b = at("rstd_b", 114, [P, NT])
    con = at("con", 192, [P, NC_])
    hbuf = at("hbuf", 201, [P, 2, NT])
    par = at("par", 203.5, [P, 64])
    par_nat = at("par_nat", 203.75, [64, P])
    wr = at("wr", 204.25, [P, KT, NL])
    sinks = at("sinks", 205.5, [P, H])
    sinks_s = at("sinks_s", 205.53125, [P, KV])
    br = at("br", 205.5625, [P, NL])
    stat = at("stat", 205.6875, [P, 32])
    slot_g = at("slot_g", 100, [P, KT, DE])
    slot_u = at("slot_u", 132, [P, KT, DE])
    slot_d = at("slot_d", 0, [P, FT, D])
    places = (164, 168, 172, 176, 180, 184, 188, 60)
    eh = [at(f"eh{j}", places[2 * j], [P, PIECE], F32R) for j in range(AHEAD + 1)]
    el = [at(f"el{j}", places[2 * j + 1], [P, PIECE], F32R) for j in range(AHEAD + 1)]
    x2 = [at(f"x2_{j}", 64 + 12 * j, [P, 3, D], BF16) for j in range(3)]
    x2r = [at(f"x2r{t}", 132 + 2 * t, [P, 512]) for t in range(3)]
    squares2 = at("squares2", 201, [P, 512])
    lgT = at("lgT", 58, [NL, NT])
    hgx = at("hgx", 32, [P, KT, 2 * SLOTS], F32R)
    hg = at("hg", 40, [P, KT, SLOTS])
    aTx = at("aTx", 44, [P, FT, 2 * SLOTS], F32R)
    pick = at("pick", 46, [P, 3, SLOTS], BF16)
    y_sb = at("y_sb", 50, [SLOTS, D])
    g_sb = at("g_sb", 58, [SLOTS, DE])
    u_sb = at("u_sb", 201, [SLOTS, DE])
    su_b = at("su_b", 206, [P, P], BF16)
    ones_b = at("ones_b", 206.25, [P, P], BF16)
    MMb = at("MMb", 206.5, [P, 3, NE], BF16)
    ident_b = at("ident_b", 203.25, [P, P], BF16)
    rparts = at("rparts", 205.8125, [P, 3, 4], BF16)
    sums2 = at("sums2", 205.84375, [P, 3, 4])
    rt = at("rt", 46.375, [P, 768])
    ri = at("ri", 49.375, [P, 64], U32)
    rows = at("rows", 49.625, [P, 8], U32)
    ints = at("ints", 49.65625, [1, 16], I32)
    rk = at("rk", 49.71875, [P, 3, NE + 1])
    rko = at("rko", 49.9375, [P, 4])
    gfin = at("gfin", 156, [P, D])
    ya = [at(f"ya{t}", 100 + 8 * t, [P, D]) for t in range(3)]
    yb = [at(f"yb{t}", 132 + 8 * t, [P, D]) for t in range(3)]

    c0 = [0]

    def cols(n, shape=None):
        a = c0[0]
        c0[0] += n
        v = rt[:, a:a + n]
        return v if shape is None else v.rearrange("p (a b) -> p a b", b=shape)
    lgt = cols(3 * NL, NL)
    gl8 = cols(24, 8)
    gm8 = cols(24, 8)
    em = cols(3 * NE, NE)
    em8 = cols(24, 8)
    gex = cols(3 * NG, NG)
    d21 = cols(3)
    gi = cols(3)
    gsum = cols(3)
    gp = cols(3)
    dn = cols(3)
    wt = cols(6, 3)
    ei = cols(6, 3)
    gmask = cols(3 * NE, NE)
    tmp = cols(3 * NE, NE)
    M1 = cols(3 * NE, NE)
    M2 = cols(3 * NE, NE)
    MM = cols(3 * NE, NE)
    rank = cols(3 * NE, NE)
    cnt = cols(NE)
    ov = cols(NE)
    ovc = cols(NE)
    ovx = cols(NE)
    sel = cols(MAXOV * NE, NE)
    se = cols(MAXOV)
    so = cols(MAXOV)
    rr = cols(6, 3)
    ro = cols(6, 3)
    assert c0[0] <= 768, c0[0]

    with ExitStack() as ctx:
        ps = [ctx.enter_context(nc.psum_tensor(f"bank{i}", [P, 512], F32)) for i in range(8)]
        names = """const_in x_in w_load0 w_load1 kc_in vc_in swc_in small_in xT_out act_own dve_own
                   rms diag_done rb_ps x_turned h_done xh_done xl_done xT_done par_ps par_sb kc_ps kc_sb pads
                   wh_ready wl_ready blk ev_a ev_d rope_done h_turned nat_done nat_out nat_free kept_out pool_head
                   kst_st vst_st qst_st z_sb z_sw zm_done zw_done l_done sp_done c_done e_done a_done
                   p_ready pT_ps pT_sb o_sb o_sw o_sb_ev o_sw_ev sums_done oh_done ol_done sig_done m_done mh_done
                   ml_done xT_in wr_scaled x2_ps x2_a x2_r x2_b x2_d lg_ps lgT_done lg_turned masks rk_ps rk_done
                   g_in u_in d_in picked hg_ps hg_sb hgh_done hgl_done eh_ready el_ready elp_ready ch_used g_low g_sum
                   silu_done u_low u_sum a_ready aT_ps aTh_done aTl_done y_act y_dve y_out
                   zero_set zero_out rows_ready ints_ready gf_in y_in0 y_in1 y_in2 sum_done fin out_done
                   ex_in ex_out half_done ssq3 rko_done ident_done rp_done x2_back all_rows table_in""".split()
        S = {n: ctx.enter_context(nc.semaphore(n)) for n in names}
        block = ctx.enter_context(nc.Block())
        ds = bass.ds
        v, a_ = nc.vector, nc.scalar

        def upto(it, j):
            return it * 4 + (j + 1)

        def tok(t):
            return slice(t * P, t * P + TILES[t])

        def x2_bank(q, t):
            return ps[2 + (3 * q + t) % 4]

        def piece(c):
            m, q = c % CH // 8, c % 8
            if m == 2:
                return "d_in", slot_d[:, q // 2, q % 2 * PIECE:(q % 2 + 1) * PIECE]
            w = (slot_g, slot_u)[m]
            return ("g_in", "u_in")[m], w[:, 2 * q:2 * q + 2, :].rearrange("p k n -> p (k n)")

        def low_part(eng, s, c):
            eng.wait_ge(S["eh_ready"], s * CH + (c + 1))
            (nc.gpsimd if eng.engine == mybir.EngineType.Pool else nc.vector).tensor_tensor(
                el[c % 4][:], piece(c)[1], eh[c % 4][:].bitcast(F32), ALU.subtract)\
                .then_inc(S["elp_ready" if c % CH in BY_POOL else "el_ready"], 1)

        def used(s, c):
            return s * CH + (c + 2 + AHEAD)

        def flat(ap):
            return ap.rearrange("p a n -> p (a n)")

        def main(j):
            return ps[j % 2][:, 0:NT]

        def raw(j):
            return ring[:, j // 2, :, (j % 2) * P:(j % 2 + 1) * P]

        EV_KVSW_A, EV_KVSW_D = 1 + 24, 1 + 8
        EV_ATT = EV_KVSW_A + 2
        EV_PROJ = EV_ATT + 16
        EV_OUT_D = EV_KVSW_D + 2

        @block.sync
        def _(sp):
            sp.dma_start(x_nat[:, 0:2, :], x_prompt[0].rearrange("(t p) d -> p t d", p=P)).then_inc(S["x_in"], 16)
            sp.dma_start(x_nat[0:DEC, 2, :], x_sample[0]).then_inc(S["x_in"], 16)

            def load_pair(j, src):
                sp.dma_start(ring[:, j], src.rearrange("(k p) n -> p k n", p=P)).then_inc(S[f"w_load{j}"], 16)

            def slot_free(j, it):
                sp.wait_ge(S["wl_ready"], (it - 1) * 4 + (2 * j + 2))

            sp.wait_ge(S["const_in"], 16 * 4)
            load_pair(0, w_in[0, :, 0:PAIR])
            load_pair(1, w_in[0, :, PAIR:2 * PAIR])
            with sp.Fori(1, IT_PROJ) as it:
                for j in range(2):
                    slot_free(j, it)
                    load_pair(j, w_in[0, :, ds(it * (2 * PAIR) + j * PAIR, PAIR)])
            with sp.Fori(IT_PROJ, IT_OUT) as it:
                slot_free(0, it)
                load_pair(0, w_in[0, :, ds(it * PAIR + (GATE0 + D - IT_PROJ * PAIR), PAIR)])
                slot_free(1, it)
                for k, w in enumerate((w_sb_o, w_swa_o)):
                    sp.dma_start(ring[:, 1, k * H:(k + 1) * H],
                                 w[0, :, ds((it - IT_PROJ) * PAIR, PAIR)].rearrange("(k p) n -> p k n", p=P))\
                        .then_inc(S["w_load1"], 16)
            with sp.Fori(IT_OUT, IT_END) as it:
                for j in range(2):
                    slot_free(j, it)
                    load_pair(j, w_out[0, :, ds((it - IT_OUT) * (2 * PAIR) + j * PAIR, PAIR)])

            def load(dst, w, e, sem):
                sp.dma_start(dst[:], w[0, ds(e, 1)].rearrange("a (k p) n -> p (a k) n", p=P)).then_inc(S[sem], 16)

            sp.wait_ge(S["blk"], upto(IT_OUT - 1, 3))
            load(slot_g, w_e_gate, 0, "g_in")
            sp.wait_ge(S["wl_ready"], upto(IT_END - 1, 3))
            load(slot_d, w_e_down, 0, "d_in")
            sp.wait_ge(S["x2_d"], 12)
            load(slot_u, w_e_up, 0, "u_in")

            def low_wait(s, c):
                assert not any(c - AHEAD <= p <= c for p in BY_POOL)
                sp.wait_ge(S["el_ready"], s * (CH - len(BY_POOL)) + (c + 1 - sum(p <= c for p in BY_POOL)))

            def next_matrices(e, s):
                low_wait(s - 1, 7)
                load(slot_g, w_e_gate, e, "g_in")
                low_wait(s - 1, 15)
                load(slot_u, w_e_up, e, "u_in")
                low_wait(s - 1, 23)
                load(slot_d, w_e_down, e, "d_in")

            def rows_out(s):
                sp.wait_ge(S["y_dve"], s * 4 + 5)
                sp.dma_start(y_rows[ds(s * SLOTS, SLOTS), :], y_sb[:]).then_inc(S["y_out"], 16)

            with sp.Fori(1, NE) as e:
                next_matrices(e, e)
                rows_out(e - 1)
            rows_out(NE - 1)
            sp.wait_ge(S["ints_ready"], 1)
            sp.wait_ge(S["zero_out"], 16 * 5)
            more = sp.value_load(ints[0:1, MAXOV:MAXOV + 1], min_val=0, max_val=MAXOV)
            with sp.If(more > 0):
                with sp.Fori(0, more) as i:
                    e = sp.value_load(ints[0:1, ds(i, 1)], min_val=0, max_val=NE - 1)
                    next_matrices(e, i + NE)
                    rows_out(i + NE)
            for t, n in enumerate(TILES):
                sp.wait_ge(S["fin"], t + 1)
                sp.dma_start(y_prompt[0, tok(t)] if t < 2 else y_sample[0], ya[t][0:n]).then_inc(S["out_done"], 16)
            sp.wait_ge(S["out_done"], 16 * 3)
            sp.wait_ge(S["nat_out"], 32 * 5)
            sp.wait_ge(S["kept_out"], 16 * 2)

        @block.gpsimd
        def _(pool):
            for name in RAISED:
                pool.sem_inc(S[name], 1)
            pool.dma_start(kc_nat[:], cache_sb_k[0, 0].rearrange("s h d -> s (h d)")).then_inc(S["kc_in"], 16)
            pool.dma_start(vc_sb[:], cache_sb_v[0, 0].rearrange("s h d -> s (h d)")).then_inc(S["vc_in"], 16)
            pool.dma_start(sinks[:], swa_sink[0:1, :].to_broadcast([P, H])).then_inc(S["small_in"], 16)
            with nc.allow_non_contiguous_dma(reason="8 sinks"):
                for g in range(GRP):
                    for kv in range(KV):
                        pool.dma_start(sinks_s[DEC * g:DEC * g + DEC, kv:kv + 1],
                                       swa_sink[0:1, GRP * kv + g:GRP * kv + g + 1].to_broadcast([DEC, 1]))\
                            .then_inc(S["small_in"], 16)
            pool.dma_start(wr[:, :, 0:NG], w_rg[0].rearrange("(k p) n -> p k n", p=P)).then_inc(S["small_in"], 16)
            pool.dma_start(wr[:, :, NG:], w_re[0].rearrange("(k p) n -> p k n", p=P)).then_inc(S["small_in"], 16)
            pool.dma_start(br[:, 0:NG], b_rg[0:1, :].to_broadcast([P, NG])).then_inc(S["small_in"], 16)
            pool.dma_start(br[:, NG:], b_re[0:1, :].to_broadcast([P, NE])).then_inc(S["small_in"], 16)
            for n, c in enumerate((cache_swa_k, cache_swa_v)):
                pool.dma_start(swa_kv_kept[n], c[0, 0, DEC:PAST].rearrange("s h d -> s (h d)"))\
                    .then_inc(S["kept_out"], 16)
            pool.wait_ge(S["xT_out"], 16)
            pool.dma_start(kcw_nat[:], cache_swa_k[0, 0].rearrange("s h d -> s (h d)")).then_inc(S["swc_in"], 16)
            pool.dma_start(vc_sw[:], cache_swa_v[0, 0].rearrange("s h d -> s (h d)")).then_inc(S["swc_in"], 16)
            pool.memset(zero[:], 0.0).then_inc(S["zero_set"], 1)
            pool.wait_ge(S["zero_set"], 1)
            for r0, k in ((NE * SLOTS, 4), (NE * SLOTS + 4 * P, 0)):
                n, m = (P, k) if k else (MAXOV * SLOTS - 4 * P, 1)
                for q in range(m):
                    pool.dma_start(y_rows[r0 + q * P:r0 + q * P + n, :].rearrange("p (b n) -> p b n", n=512),
                                   zero[0:n, :].rearrange("p (a n) -> p a n", a=1).to_broadcast([n, 4, 512]))\
                        .then_inc(S["zero_out"], 16)

            def nat_store(i, src, dst_prompt, dst_sample):
                pool.wait_ge(S["nat_done"], i * 4 + 5)
                pool.dma_start(dst_prompt, src).then_inc(S["nat_out"], 16)
                pool.dma_start(dst_sample, nat[0:DEC, 2, :]).then_inc(S["nat_out"], 16)
                pool.wait_ge(S["nat_out"], i * 32 + 32)
                pool.sem_inc(S["nat_free"], 1)

            for n in range(2):
                with pool.Fori(0, 2) as ii:
                    i = ii + 2 * n
                    for j in range(4):
                        if n == 0:
                            pool.wait_ge(S["ev_a"], i * 4 + (1 + 8 + j + 1 + 1))
                            pool.tensor_copy(kT_sb[:, ds(ii * 4 + j, 1), 0:NT], headT[:, j:j + 1, 0:NT])\
                                .then_inc(S["pool_head"], 1)
                        else:
                            pool.wait_ge(S["nat_done"], i * 4 + (j + 1 + 1))
                            pool.tensor_copy(v_sb[:, :, ds(ii * (4 * P) + j * P, P)], nat[:, :, j * P:(j + 1) * P])\
                                .then_inc(S["pool_head"], 1)
                    nat_store(i, nat[:, 0:2, :],
                              sb_kv_prompt[ds(i, 1)].rearrange("a (t p) n -> p (a t) n", p=P),
                              sb_kv_sample[ds(i, 1)].rearrange("a p n -> p (a n)"))
            pool.wait_ge(S["rope_done"], 11)
            for g in range(KV):
                pool.tensor_copy(qst[:, g * P:(g + 1) * P].rearrange("p (h n) -> p h n", h=GRP),
                                 qT[:, H + GRP * g:H + GRP * g + GRP, SEQ:NT]).then_inc(S["qst_st"], 1)
            pool.wait_ge(S["nat_done"], 21)
            pool.tensor_copy(v_sw[:], nat[:, :, KV * HD:]).then_inc(S["pool_head"], 1)
            nat_store(4, nat[:, 1, :], swa_kv_prompt, swa_kv_new)

            pool.wait_ge(S["pool_head"], 18)
            pool.wait_ge(S["vc_in"], 16)
            pool.wait_ge(S["kc_sb"], 2)
            with pool.Fori(0, IT_PROJ - IT_ATT) as i:
                for u in range(2):
                    hd = i * 2 + u
                    pool.wait_ge(S["z_sb"], hd + 1)
                    pool.tensor_copy(kst[:, 0:3, :], kT_sb[:, ds(hd, 1), :].rearrange("p a (t n) -> p (a t) n", n=P))\
                        .then_inc(S["kst_st"], 1)
                    pool.tensor_copy(kst[:, 3:4, :], kcT_sb[:, ds(hd, 1), :]).then_inc(S["kst_st"], 1)
                    pool.wait_ge(S["z_sw"], hd + KV)
                    pool.tensor_copy(qst[:].rearrange("p (a n) -> p a n", a=1),
                                     qT[:, ds(i + (H + GRP * u), 1), 0:SEQ]).then_inc(S["qst_st"], 1)
                    pool.wait_ge(S["o_sb"], hd + 1)
                    pool.tensor_copy(vst[:, 0:3, :], v_sb[:, :, ds(hd * P, P)]).then_inc(S["vst_st"], 1)
                    pool.tensor_copy(vst[:, 3:4, :], vc_sb[:, ds(hd * P, P)].rearrange("p (a n) -> p a n", a=1))\
                        .then_inc(S["vst_st"], 1)
            pool.wait_ge(S["ml_done"], KT + 1)
            pool.dma_start(xT[:], xT_spill.rearrange("p (k n) -> p k n", k=KT)).then_inc(S["xT_in"], 16)
            with pool.Fori(0, NE) as e:
                for c in BY_POOL:
                    low_part(pool, e, c)
            pool.wait_ge(S["ints_ready"], 1)
            more = pool.value_load(ints[0:1, MAXOV:MAXOV + 1], min_val=0, max_val=MAXOV)
            with pool.If(more > 0):
                with pool.Fori(0, more) as i:
                    for c in BY_POOL:
                        low_part(pool, i + NE, c)
            pool.wait_ge(S["y_out"], more * 16 + (16 * NE + 1))
            pool.sem_inc(S["all_rows"], 1)
            pool.wait_ge(S["all_rows"], 1)
            pool.wait_ge(S["rows_ready"], 1)
            for t, n in enumerate(TILES):
                for c, dst in enumerate((ya, yb)):
                    pool.indirect_dma_start(
                        dst[t][0:n, :], None, y_rows,
                        bass.IndirectOffsetOnAxis(ap=rows[0:n, 2 * t + c:2 * t + c + 1], axis=0))\
                        .then_inc(S[f"y_in{t}"], 16)
                if t == 0:
                    pool.dma_start(gfin[:], g_final.rearrange("(a n) -> a n", a=1).to_broadcast([P, D]))\
                        .then_inc(S["gf_in"], 16)

        @block.scalar
        def _(act):
            own = Steps(act, S["act_own"])
            for src, r0, r1 in ((b_gate, 0, 32), (g_mix, 32, 48), (g_ffn, 48, 64)):
                act.dma_start(par_nat[r0:r1, :], src[0].rearrange("(r p) -> r p", p=P)).then_inc(S["const_in"], 16)
            act.dma_start(con[:], const).then_inc(S["const_in"], 16)
            act.wait_ge(S["dve_own"], 2)
            act.wait_ge(S["x_in"], 32)
            for t, n in enumerate(TILES):
                own.wait()
                own(a_.activation(squares[0:n], x_nat[0:n, t, :], ACT.Square, accum_out=stat[0:n, t:t + 1]))
            act.wait_ge(S["rms"], 1)
            a_.activation(stat[:, 16:19], stat[:, 4:7], ACT.Sqrt).then_inc(S["rms"], 1)
            def split(j, loads):
                act.wait_ge(S[f"w_load{j // 2}"], loads)
                a_.activation(wh[:, j % 2], raw(j), ACT.Copy).then_inc(S["wh_ready"], 1)

            act.wait_ge(S["par_ps"], 1)
            a_.activation(par[:], ps[1][:, 0:64], ACT.Copy).then_inc(S["par_sb"], 1)
            split(0, 16)
            for k in range(KT):
                act.wait_ge(S["h_done"], k + 1)
                a_.activation(xh[:, k, :], hbuf[:, k % 2, :], ACT.Copy).then_inc(S["xh_done"], 1)
                if k == 5:
                    split(1, 16)
            for n in range(2):
                act.wait_ge(S["kc_ps"], n + 1)
                a_.activation(kcT_sb[:, 4 * n:4 * n + 4, :], ps[5 + n][:].rearrange("p (h n) -> p h n", h=4), ACT.Copy)\
                    .then_inc(S["kc_sb"], 1)
            act.wait_ge(S["xT_done"], KT)
            act.dma_start(xT_spill.rearrange("p (k n) -> p k n", k=KT), xT[:]).then_inc(S["xT_out"], 16)
            act.wait_ge(S["const_in"], 16 * 4)
            for dst, at_ in ((ident_b, C_ID), (su_b, C_SU), (ones_b, C_ONE)):
                a_.activation(dst[:], con[:, at_:at_ + P], ACT.Copy).then_inc(S["ident_done"], 1)
            act.sem_inc(S["ev_a"], 1)

            def step(it, j, evac, loads1=None):
                act.wait_ge(S["blk"], upto(it, j))
                if evac:
                    evac()
                if j < 2:
                    split(j + 2, it * 16 + 16 if loads1 is None else loads1)
                else:
                    split(j - 2, it * 16 + 32)

            with act.Fori(IT_QSB, IT_KSB) as it:
                for j in range(4):
                    step(it, j, lambda: a_.activation(flat(qT[:, ds(it * 4 + j, 1), :]), main(j), ACT.Copy)
                         .then_inc(S["ev_a"], 1))
            act.wait_ge(S["pads"], 1)
            with act.Fori(0, 4) as i:
                for j in range(4):
                    if j == 0:
                        act.wait_ge(S["h_turned"], i * 4 + 1)
                        act.wait_ge(S["pool_head"], i * 4 + 1)
                    step(i + IT_KSB, j, lambda: a_.activation(headT[:, j, 0:NT], main(j), ACT.Copy)
                         .then_inc(S["ev_a"], 1))
            with act.Fori(IT_QSW, IT_KVSW) as it:
                for j in range(4):
                    step(it, j, None)
            act.wait_ge(S["h_turned"], 17)
            act.wait_ge(S["pool_head"], 17)
            for j in range(4):
                step(IT_KVSW, j, None if j < 2 else lambda: a_.activation(
                    headT[:, j, 0:NT], main(j), ACT.Copy).then_inc(S["ev_a"], 1))
            act.wait_ge(S["kc_ps"], 3)
            a_.activation(kcT_sw[:], ps[6][:, 0:KV * P].rearrange("p (h n) -> p h n", h=KV), ACT.Copy)\
                .then_inc(S["kc_sb"], 1)

            def softmax(segments, sink, n):
                act.wait_ge(S["zw_done"], n)
                for c, (a, b) in enumerate(segments):
                    a_.activation(zw[:, a:b], zw[:, a:b], ACT.Exp, bias=st[:, 2 + c:3 + c],
                                  accum_out=st[:, 4 + c:5 + c]).then_inc(S["sums_done"], 1)
                c = len(segments)
                a_.activation(st[:, 6:6 + c], st[:, 2:2 + c], ACT.Exp, bias=sink).then_inc(S["sums_done"], 1)

            act.wait_ge(S["small_in"], 16 * 13)
            for g in range(KV):
                softmax([(0, SSC)], sinks_s[:, g:g + 1], g + 1)
                act.wait_ge(S["pT_ps"], g + 1)
                if g:
                    act.wait_ge(S["o_sw"], g)
                a_.activation(pT[:, 0:P], ps[5][:, 0:P], ACT.Copy).then_inc(S["pT_sb"], 1)
                a_.activation(pT[0:DEC, P:2 * P], ps[5][0:DEC, P:2 * P], ACT.Copy).then_inc(S["pT_sb"], 1)
                act.wait_ge(S["o_sw"], g + 1)
                a_.activation(qT[:, H + GRP * g:H + GRP * g + GRP, SEQ:NT],
                              ps[7][:, 0:P].rearrange("p (h n) -> p h n", h=GRP), ACT.Copy)\
                    .then_inc(S["o_sw_ev"], 1)
            act.wait_ge(S["nat_free"], 6)
            act.wait_ge(S["pool_head"], 18)
            with act.Fori(0, IT_PROJ - IT_ATT) as i:
                own.enter(i, 4)
                for u in range(2):
                    hd = i * 2 + u
                    act.wait_ge(S["zm_done"], hd + 2)
                    own(a_.activation(lg[:], zm[:], ACT.Abs))
                    own.wait()
                    own(a_.activation(lg[:], lg[:], ACT.Exp, scale=-1.0))
                    own.wait()
                    a_.activation(lg[:], lg[:], ACT.Ln, bias=1.0).then_inc(S["l_done"], 1)
                    softmax([(0, P), (P, SWC)], sinks[:, ds(i + GRP * u, 1)], hd + (KV + 1))

                    def gate(j):
                        return lambda: a_.activation(flat(gates[:, ds(i * 4 + j, 1), :]), main(j), ACT.Identity,
                                                     bias=par[:, ds(i * 4 + j, 1)]).then_inc(S["ev_a"], 1)
                    step(i + IT_ATT, 2 * u, gate(2 * u))
                    act.wait_ge(S["e_done"], hd + 2)
                    a_.activation(spb[:], lg[:], ACT.Exp).then_inc(S["a_done"], 1)
                    act.wait_ge(S["pT_ps"], hd + (KV + 1))
                    act.wait_ge(S["o_sw"], hd + KV)
                    a_.activation(pT[:], ps[5][:, 0:SWC], ACT.Copy).then_inc(S["pT_sb"], 1)
                    step(i + IT_ATT, 2 * u + 1, gate(2 * u + 1))
                    act.wait_ge(S["o_sb"], hd + 2)
                    a_.activation(flat(qT[:, ds(hd, 1), :]), ps[6][:, 0:NT], ACT.Copy).then_inc(S["o_sb_ev"], 1)
                own.leave(IT_PROJ - IT_ATT)
            act.wait_ge(S["o_sw"], KV + H)
            act.wait_ge(S["vst_st"], 2 * H)
            act.wait_ge(S["o_sb_ev"], H + 1)
            act.wait_ge(S["o_sw_ev"], KV + H)
            for h in range(2 * H):
                a_.activation(oh[:, h, :], qT[:, h, :], ACT.Copy).then_inc(S["oh_done"], 1)
            with act.Fori(0, IT_OUT - IT_PROJ) as i:
                it = i + IT_PROJ
                for j in range(2):
                    step(it, j, None, i * 32 + (16 * IT_PROJ + 32))
                for j in range(2):
                    m = i * 2 + j
                    act.wait_ge(S["m_done"], m + 1)
                    a_.activation(sg1[:], flat(gates[:, ds(m, 1), :]), ACT.Sigmoid).then_inc(S["sig_done"], 1)
                    a_.activation(sg2[:], main(j), ACT.Sigmoid, bias=par[:, ds(m + KT, 1)]).then_inc(S["ev_a"], 1)

                    def high():
                        act.wait_ge(S["m_done"], m + 2)
                        a_.activation(flat(mh[:, ds((i + 1) * 2 + (j - 2), 1), :]), m1[:], ACT.Copy).then_inc(S["mh_done"], 1)
                    step(it, 2 + j, high)
            slot1 = 16 * IT_PROJ + 32 * (IT_OUT - IT_PROJ)
            with act.Fori(0, IT_END - IT_OUT - 1) as i:
                for j in range(4):
                    step(i + IT_OUT, j, None, i * 16 + (slot1 + 16))
            for j in range(2):
                step(IT_END - 1, j, None, slot1 + 16 * (IT_END - IT_OUT))
            for q in range(4):
                for t, n in enumerate(TILES):
                    act.wait_ge(S["x2_ps"], 3 * q + t + 1)
                    a_.activation(x2[0][0:n, t, q * 512:(q + 1) * 512], x2_bank(q, t)[0:n], ACT.Copy)
                    if q or t:
                        act.wait_ge(S["x2_a"], 3 * q + t)
                    a_.activation(squares2[0:n], x2_bank(q, t)[0:n], ACT.Square, accum_out=sums2[0:n, t, q:q + 1])\
                        .then_inc(S["x2_a"], 1)
                for t, n in enumerate(TILES):
                    act.wait_ge(S["x2_r"], 3 * q + t + 1)
                    a_.activation(x2[1][0:n, t, q * 512:(q + 1) * 512], x2r[t][0:n], ACT.Copy).then_inc(S["x2_b"], 1)
            act.wait_ge(S["rms"], 3)
            a_.activation(stat[:, 16:19], stat[:, 4:7], ACT.Sqrt).then_inc(S["rms"], 1)
            act.wait_ge(S["ex_in"], 1)
            a_.activation(gex, gex, ACT.Exp).then_inc(S["ex_out"], 1)
            act.wait_ge(S["ex_in"], 2)
            a_.activation(d21, d21, ACT.Exp).then_inc(S["ex_out"], 1)

            def high(s, c):
                sem, w = piece(c)
                act.wait_ge(S[sem], s * 16 + 16 * (1 + c // CH))
                act.wait_ge(S["ch_used"], used(s, c - AHEAD - 1))
                a_.activation(eh[c % 4][:], w, ACT.Copy).then_inc(S["eh_ready"], 1)

            def tokens_high(s):
                act.wait_ge(S["hg_sb"], s * 2 + 2)
                if not isinstance(s, int) or s:
                    act.wait_ge(S["ch_used"], used(s, 15 - CH))
                a_.activation(hgx[:, :, 0:SLOTS], hg[:], ACT.Copy).then_inc(S["hgh_done"], 1)

            def expert(s, nxt):
                act.wait_ge(S["table_in"], s + 1)
                a_.activation(stat[0:1, 27:28], stat[0:1, 26:27], ACT.Silu).then_inc(S["table_in"], 1)
                for c in range(AHEAD, 11):
                    high(s, c)
                act.wait_ge(S["ch_used"], used(s, 7))
                act.wait_ge(S["a_ready"], s + 1)
                act.wait_ge(S["aT_ps"], s + 1)
                a_.activation(g_sb[:], ps[2][SLOTS:P, :], ACT.Copy).then_inc(S["g_low"], 1)
                high(s, 11)
                high(s, 12)
                act.wait_ge(S["g_sum"], s + 1)
                a_.activation(g_sb[:], g_sb[:], ACT.Silu, scale=stat[0:SLOTS, 24:25]).then_inc(S["silu_done"], 1)
                for c in range(13, 19):
                    high(s, c)
                act.wait_ge(S["ch_used"], used(s, 15))
                a_.activation(u_sb[:], ps[3][SLOTS:P, :], ACT.Copy).then_inc(S["u_low"], 1)
                high(s, 19)
                act.wait_ge(S["aT_ps"], s + 2)
                a_.activation(aTx[:, :, 0:SLOTS], ps[2][:, 0:FT * SLOTS].rearrange("p (f n) -> p f n", f=FT), ACT.Copy)\
                    .then_inc(S["aTh_done"], 1)
                if nxt:
                    tokens_high(s + 1)
                high(s, 20)
                high(s, 21)
                high(s, 22)
                high(s, 23)
                if nxt:
                    for c in range(AHEAD):
                        high(s, CH + c)
                act.wait_ge(S["ch_used"], used(s, CH - 1))
                act.wait_ge(S["y_out"], s * 16 + 1)
                for q in range(4):
                    a_.activation(y_sb[:, q * 512:(q + 1) * 512], ps[4 + q][SLOTS:P, :], ACT.Copy)\
                        .then_inc(S["y_act"], 1)

            for c in range(AHEAD):
                high(0, c)
            tokens_high(0)
            with act.Fori(0, NE - 1) as e:
                expert(e, True)
            expert(NE - 1, False)
            act.wait_ge(S["ints_ready"], 1)
            more = act.value_load(ints[0:1, MAXOV:MAXOV + 1], min_val=0, max_val=MAXOV)
            with act.If(more > 0):
                with act.Fori(0, more) as i:
                    tokens_high(i + NE)
                    for c in range(AHEAD):
                        high(i + NE, c)
                    expert(i + NE, False)
            for t, n in enumerate(TILES):
                act.wait_ge(S["sum_done"], t + 1)
                a_.activation(yb[t][0:n], ya[t][0:n], ACT.Square, accum_out=stat[0:n, t:t + 1])\
                    .then_inc(S["ssq3"], 1)
                act.wait_ge(S["rms"], 5 + 2 * t)
                a_.activation(stat[0:n, 16 + t:17 + t], stat[0:n, 4 + t:5 + t], ACT.Sqrt).then_inc(S["rms"], 1)

        @block.tensor
        def _(pe):
            mm_, tr = nc.tensor.matmul, nc.tensor.transpose
            ident = con[:, C_ID:C_ID + P]
            ones = con[:, C_ONE:C_ONE + P]
            pe.wait_ge(S["const_in"], 16 * 4)
            tr(ps[1][:, 0:64], par_nat[:], ident[0:64, 0:64]).then_inc(S["par_ps"], 1)
            pe.wait_ge(S["x_in"], 32)
            for k in range(KT):
                if k >= 3:
                    pe.wait_ge(S["xT_done"], k - 2)
                for t, n in enumerate(TILES):
                    mm = tr(ps[2 + k % 3][:, t * P:t * P + n], x_nat[0:n, t, k * P:(k + 1) * P], ident[0:n, 0:n])
                mm.then_inc(S["x_turned"], 1)
            pe.wait_ge(S["diag_done"], 3)
            for t, n in enumerate(TILES):
                mm = mm_(ps[7][:, 64 + t * P:64 + t * P + n], ones[0:n, :], diag[0:n, t, 0:n], start=True, stop=True)
            mm.then_inc(S["rb_ps"], 1)
            pe.wait_ge(S["kc_in"], 16)
            for n in range(2):
                for h in range(4):
                    k0 = (4 * n + h) * P
                    mm = tr(ps[5 + n][:, h * P:(h + 1) * P], kc_nat[:, k0:k0 + P], ident)
                mm.then_inc(S["kc_ps"], 1)

            def products(it, j, hi, lo, sums=None, first=False):
                pe.wait_ge(S["wl_ready"], upto(it, j))
                for dst, k0, k1 in sums or ((main(j), 0, KT),):
                    for k in range(k0, k1):
                        if first:
                            pe.wait_ge(S["xl_done"], k + 1)
                        mm_(dst, wh[:, j % 2, k, :], hi[:, k, :], start=(k == k0), stop=False)
                        mm_(dst, wh[:, j % 2, k, :], lo[:, k, :], start=False, stop=False)
                        mm = mm_(dst, wl[:, j % 2, k, :], hi[:, k, :], start=False, stop=(k == k1 - 1))
                mm.then_inc(S["blk"], 1)

            def turn(src, j):
                for t in range(3):
                    mm = tr(ps[5 + j % 2][:, t * P:(t + 1) * P], src[:, t * P:(t + 1) * P], ident)
                mm.then_inc(S["h_turned"], 1)

            for j in range(4):
                pe.wait_ge(S["ev_a"], j + 1)
                products(IT_QSB, j, xh, xl, first=(j == 0))
            with pe.Fori(IT_QSB + 1, IT_KSB) as it:
                for j in range(4):
                    pe.wait_ge(S["ev_a"], it * 4 + j + 1)
                    products(it, j, xh, xl)
            with pe.Fori(0, 4) as i:
                for j in range(4):
                    pe.wait_ge(S["ev_a"], i * 4 + (4 * IT_KSB + j + 1))
                    products(i + IT_KSB, j, xh, xl)
                    if j:
                        pe.wait_ge(S["ev_a"], i * 4 + (4 * IT_KSB + 1 + j + 1))
                        pe.wait_ge(S["nat_done"], i * 4 + max(j - 2, 0) + 1)
                        turn(headT[:, j - 1], j - 1)
                pe.wait_ge(S["ev_a"], i * 4 + (4 * IT_KSB + 5 + 1))
                pe.wait_ge(S["nat_done"], i * 4 + 3)
                turn(headT[:, 3], 3)
            with pe.Fori(0, 2) as i:
                for j in range(4):
                    if j < 2:
                        pe.wait_ge(S["ev_a"], 24 + j + 1)
                    pe.wait_ge(S["ev_d"], i * 4 + j + 1)
                    products(i + IT_QSW, j, xh, xl)
            for j in range(4):
                pe.wait_ge(S["ev_d"], EV_KVSW_D - 1 + j + 1)
                products(IT_KVSW, j, xh, xl)
                if j:
                    if j < 3:
                        pe.wait_ge(S["rope_done"], 8 + j + 1)
                    else:
                        pe.wait_ge(S["ev_a"], EV_KVSW_A + 1 + 1)
                    pe.wait_ge(S["nat_done"], 16 + max(j - 2, 0) + 1)
                    turn(kT_sw[:, j - 1] if j < 3 else headT[:, 2], j - 1)
            pe.wait_ge(S["ev_a"], EV_ATT + 1)
            pe.wait_ge(S["nat_done"], 19)
            turn(headT[:, 3], 3)
            pe.wait_ge(S["swc_in"], 32)
            pe.wait_ge(S["nat_done"], 21)
            for g in range(KV):
                mm = tr(ps[6][:, g * P:(g + 1) * P], kcw_nat[:, g * P:(g + 1) * P], ident)
            mm.then_inc(S["kc_ps"], 1)
            pe.wait_ge(S["kc_sb"], 3)
            pe.wait_ge(S["pool_head"], 18)
            for g in range(KV):
                pe.wait_ge(S["zw_done"], g)
                pe.wait_ge(S["qst_st"], g + 1)
                lhs = qst[:, g * P:(g + 1) * P]
                mm_(ps[4][:, 0:P], lhs, kcT_sw[:, g, :], start=True, stop=True)
                mm_(ps[4][:, P:SSC], lhs, kT_sw[:, g, SEQ:NT], start=True, stop=True).then_inc(S["z_sw"], 1)
                pe.wait_ge(S["p_ready"], g + 1)
                pe.wait_ge(S["pT_sb"], 2 * g)
                tr(ps[5][:, 0:P], zw[:, 0:P], ident)
                tr(ps[5][0:DEC, P:2 * P], zw[:, P:SSC], ident).then_inc(S["pT_ps"], 1)
                pe.wait_ge(S["pT_sb"], 2 * g + 2)
                pe.wait_ge(S["o_sw_ev"], g)
                mm_(ps[7][:, 0:P], vc_sw[:, g * P:(g + 1) * P], pT[:, 0:P], start=True, stop=False)
                mm_(ps[7][:, 0:P], v_sw[0:DEC, 2, g * P:(g + 1) * P], pT[0:DEC, P:2 * P], start=False, stop=True)\
                    .then_inc(S["o_sw"], 1)

            with pe.Fori(0, IT_PROJ - IT_ATT) as i:
                for u in range(2):
                    hd = i * 2 + u

                    def q(a, b):
                        return flat(qT[:, ds(hd, 1), a:b])

                    def gate_block(j):
                        pe.wait_ge(S["ev_a"], i * 4 + (EV_ATT - 1 + j + 1))
                        products(i + IT_ATT, j, xh, xl)

                    pe.wait_ge(S["kst_st"], hd * 2 + 2)
                    pe.wait_ge(S["zm_done"], hd + 1)
                    mm_(ps[2][:, 0:SEQ], kst[:, 0, :], q(0, SEQ), start=True, stop=True)
                    mm_(ps[2][:, SEQ:SEQ + P], kst[:, 1, :], q(P, SEQ), start=True, stop=True)
                    mm_(ps[2][:, SEQ + P:SEQ + P + DEC], kst[:, 3, :], q(SEQ, NT), start=True, stop=True)
                    mm_(ps[2][:, SEQ + P + DEC:SBC], kst[:, 2, :], q(SEQ, NT), start=True, stop=True)\
                        .then_inc(S["z_sb"], 1)
                    pe.wait_ge(S["qst_st"], hd + (KV + 1))
                    pe.wait_ge(S["zw_done"], hd + KV)
                    mm_(ps[4][:, 0:P], qst[:, 0:P], kT_sw[:, u, 0:P], start=True, stop=True)
                    mm_(ps[4][:, P:SWC], qst[:, P:SEQ], kT_sw[:, u, 0:SEQ], start=True, stop=True)\
                        .then_inc(S["z_sw"], 1)
                    gate_block(2 * u)
                    pe.wait_ge(S["sp_done"], hd + 1)
                    pe.wait_ge(S["e_done"], hd + 1)
                    mm_(ps[3][:, 0:SBC], con[:, C_TRI:C_TRI + P], spb[:], start=True, stop=False)
                    mm_(ps[3][:, P:SEQ], ones, spb[:, SEQ:SEQ + P], start=False, stop=False)
                    mm_(ps[3][:, SEQ + P:SEQ + P + DEC], ones, spb[:, SEQ + P + DEC:SBC], start=False, stop=True)\
                        .then_inc(S["c_done"], 1)
                    pe.wait_ge(S["p_ready"], hd + (KV + 1))
                    pe.wait_ge(S["pT_sb"], hd + 2 * KV)
                    for c in range(3):
                        mm = tr(ps[5][:, c * P:(c + 1) * P], zw[:, c * P:(c + 1) * P], ident)
                    mm.then_inc(S["pT_ps"], 1)
                    gate_block(2 * u + 1)
                    pe.wait_ge(S["a_done"], hd + 1)
                    pe.wait_ge(S["vst_st"], hd * 2 + 2)
                    pe.wait_ge(S["o_sb_ev"], hd + 1)
                    mm_(ps[6][:, 0:SEQ], vst[:, 0, :], spb[:, 0:SEQ], start=True, stop=False, skip_group_check=True)
                    mm_(ps[6][:, P:SEQ], vst[:, 1, :], spb[:, SEQ:SEQ + P], start=False, stop=False,
                        skip_group_check=True)
                    mm_(ps[6][:, SEQ:NT], vst[:, 3, :], spb[:, SEQ + P:SEQ + P + DEC], start=False, stop=False,
                        skip_group_check=True)
                    mm_(ps[6][:, SEQ:NT], vst[:, 2, :], spb[:, SEQ + P + DEC:SBC], start=False, stop=True,
                        skip_group_check=True).then_inc(S["o_sb"], 1)
                    pe.wait_ge(S["pT_sb"], hd + (2 * KV + 1))
                    pe.wait_ge(S["o_sw_ev"], hd + KV)
                    mm_(ps[7][:, 0:SEQ], v_sw[:, 0, u * P:(u + 1) * P], pT[:, 0:SEQ], start=True, stop=False)
                    mm_(ps[7][:, P:SEQ], v_sw[:, 1, u * P:(u + 1) * P], pT[:, SEQ:SWC], start=False, stop=True)\
                        .then_inc(S["o_sw"], 1)

            with pe.Fori(0, IT_OUT - IT_PROJ) as i:
                it = i + IT_PROJ
                for j in range(2):
                    pe.wait_ge(S["ev_a"], i * 2 + (EV_PROJ - 1 + j + 1))
                    products(it, j, xh, xl)
                pe.wait_ge(S["ol_done"], 2 * H)
                pe.wait_ge(S["m_done"], i * 2 + 1)
                for j in range(2):
                    products(it, 2 + j, oh, ol, ((ps[2 + j][:, 0:NT], 0, H), (ps[4 + j][:, 0:NT], H, 2 * H)))
            pe.wait_ge(S["ev_a"], EV_PROJ + 16 + 1)
            pe.wait_ge(S["ml_done"], KT + 1)
            with pe.Fori(0, IT_END - IT_OUT - 1) as i:
                for j in range(4):
                    pe.wait_ge(S["ev_d"], i * 4 + (EV_OUT_D + j))
                    products(i + IT_OUT, j, mh, ml)

            def token_major(q):
                for t in range(3):
                    if 3 * q + t >= 4:
                        pe.wait_ge(S["x2_r"], 3 * q + t - 3)
                    for k in range(4):
                        mm = tr(x2_bank(q, t)[0:TILES[t], k * P:(k + 1) * P], xT[:, 4 * q + k, tok(t)], ident)
                    mm.then_inc(S["x2_ps"], 1)

            def logits(k0, k1):
                for k in range(k0, k1):
                    mm = mm_(ps[7][0:NL, 0:NT], wr[:, k, :], xT[:, k, :], start=(k == 0), stop=(k == KT - 1))
                if k1 == KT:
                    mm.then_inc(S["lg_ps"], 1)

            for j in range(4):
                pe.wait_ge(S["ev_d"], EV_OUT_D + 12 + j)
                products(IT_END - 1, j, mh, ml)
                if j:
                    token_major(j - 1)
                if j == 1:
                    pe.wait_ge(S["wr_scaled"], 1)
                if j > 1:
                    logits(6 * j - 12, 6 * j - 6)
            pe.wait_ge(S["ev_d"], EV_OUT_D + KT + 1)
            logits(12, KT)
            token_major(3)
            pe.wait_ge(S["lgT_done"], 1)
            for t, n in enumerate(TILES):
                mm = mm_(ps[6][0:n, t * 32:t * 32 + NL], lgT[:, tok(t)], ident[0:NL, 0:NL], start=True, stop=True)
            mm.then_inc(S["lg_turned"], 1)
            pe.wait_ge(S["x2_ps"], 12)
            pe.sem_inc(S["ch_used"], AHEAD + 1)
            pe.wait_ge(S["masks"], 1)
            for t in range(3):
                for s in range(t + 1):
                    mm_(ps[6][:, t * NE:(t + 1) * NE], su_b[:] if s == t else ones_b[:], MMb[:, s, :],
                        start=(s == 0), stop=(s == t))
            for s in range(3):
                mm = mm_(ps[6][:, 3 * NE:4 * NE], ones_b[:], MMb[:, s, :], start=(s == 0), stop=(s == 2))
            mm.then_inc(S["rk_ps"], 1)

            def gather(s, k):
                if k == 0:
                    pe.wait_ge(S["picked"], s * 3 + 3)
                    if not isinstance(s, int) or s:
                        pe.wait_ge(S["hg_sb"], s * 2)
                for t, n in enumerate(TILES):
                    for j in range(3):
                        mm_(ps[k // 8][:, (k % 8) * SLOTS:(k % 8 + 1) * SLOTS],
                            x2[j][0:n, t, k * P:(k + 1) * P], pick[0:n, t, :],
                            start=(t == 0 and j == 0), stop=(t == 2 and j == 2))

            def slot_rms():
                for t, n in enumerate(TILES):
                    for j in range(3):
                        mm = mm_(ps[2][0:SLOTS, 256:257], pick[0:n, t, :], rparts[0:n, j, t:t + 1],
                                 start=(t == 0 and j == 0), stop=(t == 2 and j == 2))
                mm.then_inc(S["hg_ps"], 1)

            def low_ready(s, c):
                n = sum(p < c for p in BY_POOL)
                if c in BY_POOL:
                    pe.wait_ge(S["elp_ready"], s * len(BY_POOL) + (n + 1))
                else:
                    pe.wait_ge(S["el_ready"], s * (CH - len(BY_POOL)) + (c + 1 - n))

            def up_gate_piece(s, c):
                low_ready(s, c)
                for low, part in enumerate((eh[c % 4], el[c % 4])):
                    for k in range(2):
                        kt = c % 8 * 2 + k
                        mm = mm_(ps[2 + c // 8][:], hgx[:, kt, :], part[:, k * DE:(k + 1) * DE],
                                 start=(low == 0 and kt == 0), stop=(low == 1 and kt == KT - 1))
                mm.then_inc(S["ch_used"], 1)

            def expert(s, nxt):
                pe.wait_ge(S["hgl_done"], s + 1)
                pe.wait_ge(S["aTl_done"], s + 1)
                for c in range(16):
                    up_gate_piece(s, c)
                    if nxt and c > 2:
                        gather(s + 1, c - 3)
                if nxt:
                    for k in range(13, KT):
                        gather(s + 1, k)
                    pe.wait_ge(S["g_sum"], s + 1)
                    slot_rms()
                pe.wait_ge(S["a_ready"], s + 2)
                for f in range(FT):
                    mm = mm_(ps[2][:, f * SLOTS:(f + 1) * SLOTS], g_sb[:, f * P:(f + 1) * P],
                             ident[0:SLOTS, 0:SLOTS], start=True, stop=True)
                mm.then_inc(S["aT_ps"], 1)
                pe.wait_ge(S["aTl_done"], s + 2)
                pe.wait_ge(S["y_dve"], s * 4 + 1)
                for c in range(16, CH):
                    f, q0 = (c - 16) // 2, c % 2 * 2
                    low_ready(s, c)
                    for low, part in enumerate((eh[c % 4], el[c % 4])):
                        for q in range(2):
                            mm = mm_(ps[4 + q0 + q][:], aTx[:, f, :], part[:, q * 512:(q + 1) * 512],
                                     start=(low == 0 and f == 0), stop=(low == 1 and f == FT - 1))
                    mm.then_inc(S["ch_used"], 1)

            pe.wait_ge(S["rk_done"], 1)
            for k in range(KT):
                gather(0, k)
            pe.wait_ge(S["rp_done"], 1)
            slot_rms()
            with pe.Fori(0, NE - 1) as e:
                expert(e, True)
            expert(NE - 1, False)
            pe.wait_ge(S["ints_ready"], 1)
            more = pe.value_load(ints[0:1, MAXOV:MAXOV + 1], min_val=0, max_val=MAXOV)
            with pe.If(more > 0):
                with pe.Fori(0, more) as i:
                    for k in range(KT):
                        gather(i + NE, k)
                    pe.wait_ge(S["aTl_done"], i + (NE + 1))
                    slot_rms()
                    expert(i + NE, False)
            pe.wait_ge(S["ident_done"], 3)
            for t, n in enumerate(TILES):
                if t == 1:
                    pe.wait_ge(S["y_in0"], 32)
                if t == 2:
                    pe.wait_ge(S["half_done"], 4)
                for q in range(4):
                    for j in range(3):
                        mm = mm_(ps[4 * t % 8 + q][0:n, :], ident_b[0:n, 0:n], x2[j][0:n, t, q * 512:(q + 1) * 512],
                                 start=(j == 0), stop=(j == 2))
                mm.then_inc(S["x2_back"], 1)

        @block.vector
        def _(dve):
            own = Steps(dve, S["dve_own"])

            def then(ins):
                own(ins)
                own.wait()

            own(v.memset(sums2[:], 1.0))
            then(v.memset(stat[:], 1.0))

            def rms():
                v.tensor_scalar(stat[:, 4:7], stat[:, 0:3], 1.0 / D, EPS, ALU.mult, ALU.add).then_inc(S["rms"], 1)

            def inverse(n, a, b):
                m, inv, root, t = (stat[0:n, c + a:c + b] for c in (4, 8, 16, 20))
                then(v.reciprocal(inv, root))
                then(v.tensor_tensor(t, inv, inv, ALU.mult))
                then(v.tensor_tensor(t, t, m, ALU.mult))
                then(v.tensor_scalar(t, t, -0.5, 1.5, ALU.mult, ALU.add))
                then(v.tensor_tensor(inv, inv, t, ALU.mult))

            for k in range(KT):
                dve.wait_ge(S["x_turned"], k + 1)
                v.tensor_copy(xT[:, k, :], ps[2 + k % 3][:, 0:NT]).then_inc(S["xT_done"], 1)
                if k == 10:
                    dve.wait_ge(S["act_own"], 3)
                    rms()
            dve.wait_ge(S["rms"], 2)
            inverse(P, 0, 3)
            dve.wait_ge(S["const_in"], 16 * 4)
            for t in range(3):
                v.tensor_scalar(diag[:, t, :], con[:, C_ID:C_ID + P], stat[:, 8 + t:9 + t], None, ALU.mult)\
                    .then_inc(S["diag_done"], 1)
            dve.wait_ge(S["rb_ps"], 1)
            then(v.tensor_copy(rstd_b[:], ps[7][:, 64:64 + NT]))
            dve.wait_ge(S["par_sb"], 1)
            dve.wait_ge(S["xT_done"], KT)

            def normed(k):
                v.scalar_tensor_tensor(out=hbuf[:, k % 2, :], in0=xT[:, k, :], scalar=par[:, 32 + k:33 + k],
                                       in1=rstd_b[:], op0=ALU.mult, op1=ALU.mult).then_inc(S["h_done"], 1)

            def split(j, b):
                dve.wait_ge(S["wh_ready"], b)
                v.tensor_tensor(wl[:, j % 2], raw(j), wh[:, j % 2].bitcast(F32), ALU.subtract)\
                    .then_inc(S["wl_ready"], 1)

            normed(0)
            normed(1)
            split(0, 1)
            for k in range(KT):
                dve.wait_ge(S["xh_done"], k + 1)
                v.tensor_tensor(xl[:, k, :], hbuf[:, k % 2, :], xh[:, k, :].bitcast(F32), ALU.subtract)\
                    .then_inc(S["xl_done"], 1)
                if k < KT - 2:
                    dve.wait_ge(S["xl_done"], k + 1)
                    normed(k + 2)
                if k == 9:
                    split(1, 2)
            own(v.memset(headT[:, :, NT:], 0.0))
            v.memset(kT_sb[:, :, NT:], 0.0).then_inc(S["ev_d"], 1)
            v.memset(kT_sw[:, :, NT:], 0.0).then_inc(S["pads"], 1)
            with dve.Fori(IT_QSB, IT_KSB) as it:
                for j in range(4):
                    split((j + 2) % 4, it * 4 + (j + 3))

            def token_major(n, j):
                dve.wait_ge(S["h_turned"], n + 1)
                v.tensor_copy(nat[:, :, j * P:(j + 1) * P], ps[5 + j % 2][:, 0:3 * P].rearrange("p (t n) -> p t n", t=3))\
                    .then_inc(S["nat_done"], 1)

            with dve.Fori(0, 4) as i:
                for j in range(4):
                    if j == 1:
                        dve.wait_ge(S["nat_free"], i + 1)
                        dve.wait_ge(S["pool_head"], i * 4 + 1)
                    if j:
                        token_major(i * 4 + j, j - 1)
                    if j == 3:
                        token_major(i * 4 + 4, 3)
                    split((j + 2) % 4, i * 4 + (4 * IT_KSB + j + 3))

            def rotary(j):
                h = HD // 2
                src = main(j)
                own(v.tensor_tensor(rope_a[:], src, con[:, C_COS:C_COS + NT], ALU.mult))
                own(v.tensor_tensor(rope_b[0:h], src[h:P], con[h:P, C_SIN:C_SIN + NT], ALU.mult))
                v.tensor_tensor(rope_b[h:P], src[0:h], con[0:h, C_SIN:C_SIN + NT], ALU.mult).then_inc(S["ev_d"], 1)
                own.wait()

            dve.wait_ge(S["xT_out"], 16)
            with dve.Fori(0, 2) as i:
                own.enter(i, 8)
                for j in range(4):
                    dve.wait_ge(S["blk"], i * 4 + (4 * IT_QSW + j + 1))
                    dve.wait_ge(S["rope_done"], i * 4 + j + 1)
                    rotary(j)
                    dve.wait_ge(S["ev_d"], i * 4 + (j + 2 + 1))
                    v.tensor_tensor(flat(qT[:, ds(i * 4 + (H + j), 1), :]), rope_a[:], rope_b[:], ALU.add)\
                        .then_inc(S["rope_done"], 1)
                    split((j + 2) % 4, i * 4 + (4 * IT_QSW + j + 3))
                own.leave(2)
            for j in range(4):
                if j < 2:
                    dve.wait_ge(S["blk"], upto(IT_KVSW, j))
                    dve.wait_ge(S["rope_done"], 8 + j + 1)
                    rotary(j)
                    dve.wait_ge(S["ev_d"], EV_KVSW_D + 1 + j + 1)
                    v.tensor_tensor(kT_sw[:, j, 0:NT], rope_a[:], rope_b[:], ALU.add).then_inc(S["rope_done"], 1)
                if j == 1:
                    dve.wait_ge(S["nat_free"], 5)
                    dve.wait_ge(S["pool_head"], 17)
                if j:
                    token_major(16 + j, j - 1)
                if j == 3:
                    token_major(20, 3)
                split((j + 2) % 4, upto(IT_KVSW, j + 2))

            def scores(n, width, mask, segments, sinks_of):
                dve.wait_ge(S["z_sw"], n)
                if not isinstance(n, int) or n > 1:
                    dve.wait_ge(S["pT_ps"], n - 1)
                then(v.scalar_tensor_tensor(out=zw[:, 0:width], in0=ps[4][:, 0:width], scalar=SCALE,
                                            in1=con[:, mask:mask + width], op0=ALU.mult, op1=ALU.add))
                for c, (a, b) in enumerate(segments):
                    own(v.tensor_reduce(st[:, c:c + 1], zw[:, a:b], AX, ALU.max))
                own.wait()
                c = len(segments)
                v.tensor_scalar(st[:, 2:2 + c], st[:, 0:c], sinks_of, -1.0, ALU.max, ALU.mult).then_inc(S["zw_done"], 1)

            def divide(sums, segments):
                dve.wait_ge(S["sums_done"], sums)
                c = len(segments)
                then(v.tensor_tensor(st[:, 8:8 + c], st[:, 4:4 + c], st[:, 6:6 + c], ALU.add))
                then(v.reciprocal(st[:, 10:10 + c], st[:, 8:8 + c]))
                for n, (a, b) in enumerate(segments):
                    ins = v.tensor_scalar(zw[:, a:b], zw[:, a:b], st[:, 10 + n:11 + n], None, ALU.mult)
                    if n == c - 1:
                        ins.then_inc(S["p_ready"], 1)

            dve.wait_ge(S["small_in"], 16 * 13)
            for g in range(KV):
                scores(g + 1, SSC, C_MSS, [(0, SSC)], sinks_s[:, g:g + 1])
                divide(2 * g + 2, [(0, SSC)])
            heads = [(0, P), (P, SWC)]
            dve.wait_ge(S["zero_out"], 16 * 5)
            with dve.Fori(0, IT_PROJ - IT_ATT) as i:
                own.enter(i, 10)
                for u in range(2):
                    hd = i * 2 + u
                    dve.wait_ge(S["z_sb"], hd + 2)
                    v.scalar_tensor_tensor(out=zm[:], in0=ps[2][:, 0:SBC], scalar=SCALE, in1=con[:, C_MSB:C_MSB + SBC],
                                           op0=ALU.mult, op1=ALU.add).then_inc(S["zm_done"], 1)
                    scores(hd + (KV + 1), SWC, C_MSW, heads, sinks[:, ds(i + GRP * u, 1)])
                    dve.wait_ge(S["l_done"], hd + 1)
                    dve.wait_ge(S["o_sb"], hd + 1)
                    v.scalar_tensor_tensor(out=spb[:], in0=zm[:], scalar=0.0, in1=lg[:], op0=ALU.max, op1=ALU.add)\
                        .then_inc(S["sp_done"], 1)
                    divide(hd * 3 + (2 * KV + 3), heads)
                    split((2 * u + 2) % 4, i * 4 + (4 * IT_ATT + 2 * u + 3))
                    dve.wait_ge(S["c_done"], hd + 1)
                    v.tensor_tensor(lg[:], zm[:], ps[3][:, 0:SBC], ALU.subtract).then_inc(S["e_done"], 1)
                    split((2 * u + 3) % 4, i * 4 + (4 * IT_ATT + 2 * u + 4))
                    dve.wait_ge(S["o_sw"], hd + (KV + 1))
                    v.tensor_copy(flat(qT[:, ds(i + (H + GRP * u), 1), 0:SEQ]), ps[7][:, 0:SEQ])\
                        .then_inc(S["o_sw_ev"], 1)
                own.leave(IT_PROJ - IT_ATT)
            for h in range(2 * H):
                dve.wait_ge(S["oh_done"], h + 1)
                v.tensor_tensor(ol[:, h, :], qT[:, h, :], oh[:, h, :].bitcast(F32), ALU.subtract)\
                    .then_inc(S["ol_done"], 1)
            with dve.Fori(0, IT_OUT - IT_PROJ) as i:
                own.enter(i, 4)
                for j in range(2):
                    split(j + 2, i * 4 + (4 * IT_PROJ + j + 3))
                for j in range(2):
                    m = i * 2 + j
                    dve.wait_ge(S["sig_done"], m + 1)
                    dve.wait_ge(S["blk"], i * 4 + (4 * IT_PROJ + 3 + j))
                    dve.wait_ge(S["ml_done"], m + 1)
                    own(v.tensor_tensor(m1[:], sg1[:], ps[2 + j][:, 0:NT], ALU.mult))
                    dve.wait_ge(S["ev_a"], m + (EV_PROJ + 1 + 1))
                    own(v.tensor_tensor(m2[:], sg2[:], ps[4 + j][:, 0:NT], ALU.mult))
                    own.wait()
                    v.tensor_tensor(m1[:], m1[:], m2[:], ALU.add).then_inc(S["m_done"], 1)
                    dve.wait_ge(S["mh_done"], m + 1)
                    v.tensor_tensor(flat(ml[:, ds(m, 1), :]), m1[:], flat(mh[:, ds(m, 1), :]).bitcast(F32),
                                    ALU.subtract).then_inc(S["ml_done"], 1)
                    split(j, i * 4 + (4 * IT_PROJ + j + 5))
                own.leave(IT_OUT - IT_PROJ)
            dve.wait_ge(S["xT_in"], 16)

            def residual(it, j, m):
                dve.wait_ge(S["blk"], upto(it, j))
                v.tensor_tensor(m, m, main(j), ALU.add).then_inc(S["ev_d"], 1)

            with dve.Fori(0, IT_END - IT_OUT - 1) as i:
                for j in range(4):
                    residual(i + IT_OUT, j, flat(xT[:, ds(i * 4 + j, 1), :]))
                    split((j + 2) % 4, i * 4 + (4 * IT_OUT + j + 3))

            def parts(q):
                for t, n in enumerate(TILES):
                    dve.wait_ge(S["x2_a"], 3 * q + t + 1)
                    if q:
                        dve.wait_ge(S["x2_d"], 3 * q + t - 2)
                    v.tensor_tensor(x2r[t][0:n], x2_bank(q, t)[0:n], x2[0][0:n, t, q * 512:(q + 1) * 512],
                                    ALU.subtract).then_inc(S["x2_r"], 1)
                for t, n in enumerate(TILES):
                    dve.wait_ge(S["x2_b"], 3 * q + t + 1)
                    v.tensor_tensor(x2[2][0:n, t, q * 512:(q + 1) * 512], x2r[t][0:n],
                                    x2[1][0:n, t, q * 512:(q + 1) * 512], ALU.subtract).then_inc(S["x2_d"], 1)

            for j in range(4):
                residual(IT_END - 1, j, xT[:, KT - 4 + j, :])
                if j < 2:
                    split(j + 2, upto(IT_END - 1, j + 2))
                if j == 0:
                    v.tensor_tensor(wr[:], wr[:], par[:, 48:64].rearrange("p (k a) -> p k a", a=1)
                                    .to_broadcast([P, KT, NL]), ALU.mult).then_inc(S["wr_scaled"], 1)
                if j:
                    parts(j - 1)
            dve.wait_ge(S["lg_ps"], 1)
            v.tensor_copy(lgT[:], ps[7][0:NL, 0:NT]).then_inc(S["lgT_done"], 1)
            parts(3)
            own(v.memset(lgt, 0.0))
            own(v.memset(rk[:], -FAR))
            own(v.memset(gl8, NEG))
            dve.wait_ge(S["x2_a"], 12)
            then(v.tensor_reduce(stat[:, 0:3], sums2[:], AX, ALU.add))
            rms()
            dve.wait_ge(S["rms"], 4)
            inverse(P, 0, 3)
            dve.wait_ge(S["lg_turned"], 1)
            for t, n in enumerate(TILES):
                own(v.scalar_tensor_tensor(out=lgt[0:n, t, :], in0=ps[6][0:n, t * 32:t * 32 + NL],
                                           scalar=stat[0:n, 8 + t:9 + t], in1=br[0:n], op0=ALU.mult, op1=ALU.add))
            own.wait()
            then(v.tensor_copy(gl8[:, :, 0:NG], lgt[:, :, 0:NG]))

            def wide(ap, n):
                return ap.rearrange("p (k a) -> p k a", a=1).to_broadcast([P, ap.shape[1], n])

            def each(ap, k):
                return ap.rearrange("p (a n) -> p a n", a=1).to_broadcast([P, k, ap.shape[1]])

            for t in range(3):
                own(v.max(gm8[:, t, :], gl8[:, t, :]))
            own.wait()
            for t in range(3):
                own(v.max_index(ri[:, 8 * t:8 * t + 8], gm8[:, t, :], gl8[:, t, :]))
            v.tensor_tensor(gex, gl8[:, :, 0:NG], gm8[:, :, 0:1].to_broadcast([P, 3, NG]),
                            ALU.subtract).then_inc(S["ex_in"], 1)
            own.wait()
            then(v.tensor_copy(gi, ri[:, 0:24:8]))
            then(v.tensor_tensor(gmask, wide(gi, NE), each(con[:, C_GRP:C_GRP + NE], 3), ALU.is_equal))
            own(v.tensor_tensor(em, gmask, lgt[:, :, NG:], ALU.mult))
            own(v.tensor_scalar(tmp, gmask, -NEG, NEG, ALU.mult, ALU.add))
            own.wait()
            then(v.tensor_tensor(em, em, tmp, ALU.add))
            for t in range(3):
                own(v.max(em8[:, t, :], em[:, t, :]))
            own.wait()
            for t in range(3):
                own(v.max_index(ri[:, 24 + 8 * t:32 + 8 * t], em8[:, t, :], em[:, t, :]))
            v.tensor_tensor(d21.rearrange("p (k a) -> p k a", a=1), em8[:, :, 1:2], em8[:, :, 0:1], ALU.subtract)\
                .then_inc(S["ex_in"], 1)
            own.wait()
            for c in range(2):
                own(v.tensor_copy(ei[:, c, :], ri[:, 24 + c:48:8]))
            own.wait()
            for c, M in enumerate((M1, M2)):
                own(v.tensor_tensor(M, wide(ei[:, c, :], NE), each(con[:, C_I16:C_I16 + NE], 3), ALU.is_equal))
            own.wait()
            then(v.tensor_tensor(MM, M1, M2, ALU.add))
            then(v.tensor_tensor(MM, MM, wide(con[:, C_VAL:C_VAL + 3], NE), ALU.mult))
            v.tensor_copy(MMb[:], MM).then_inc(S["masks"], 1)

            def lows(s, *cs):
                for c in cs:
                    if c % CH not in BY_POOL:
                        low_part(dve, s, c)

            lows(0, 0)
            dve.wait_ge(S["masks"], 1)
            dve.wait_ge(S["rk_ps"], 1)
            own(v.tensor_copy(rank, ps[6][:, 0:3 * NE].rearrange("p (t n) -> p t n", t=3)))
            own(v.tensor_copy(cnt, ps[6][:, 3 * NE:4 * NE]))
            own.wait()
            then(v.scalar_tensor_tensor(out=tmp, in0=rank, scalar=FAR, in1=MM, op0=ALU.add, op1=ALU.mult))
            v.tensor_scalar(rk[:, :, 0:NE], tmp, -FAR, None, ALU.add).then_inc(S["rk_done"], 1)
            dve.wait_ge(S["rk_done"], 1)

            def choose(column, t, n):
                v.tensor_scalar(pick[0:n, t, :], con[0:n, C_I64:C_I64 + SLOTS], column, None, ALU.is_equal)\
                    .then_inc(S["picked"], 1)

            def gathered(s):
                dve.wait_ge(S["hg_ps"], s + 1)
                for n in range(2):
                    v.tensor_tensor(hg[:, 8 * n:8 * n + 8, :], ps[n][:].rearrange("p (k n) -> p k n", k=8),
                                    wide(par[:, 48 + 8 * n:56 + 8 * n], SLOTS), ALU.mult).then_inc(S["hg_sb"], 1)

            def tokens_low(s):
                dve.wait_ge(S["a_ready"], s + 1)
                v.tensor_copy(stat[0:SLOTS, 24:25], ps[2][0:SLOTS, 256:257])
                dve.wait_ge(S["hgh_done"], s + 1)
                v.tensor_tensor(hgx[:, :, SLOTS:], hg[:], hgx[:, :, 0:SLOTS].bitcast(F32), ALU.subtract)\
                    .then_inc(S["hgl_done"], 1)

            for t, n in enumerate(TILES):
                choose(rk[0:n, t, 0:1], t, n)
            rest = tmp[:, 0, 0:3]
            inv = stat[:, 8:11]
            then(v.tensor_copy(rparts[:, 0, 0:3], inv))
            then(v.tensor_tensor(rest, inv, rparts[:, 0, 0:3], ALU.subtract))
            then(v.tensor_copy(rparts[:, 1, 0:3], rest))
            v.tensor_tensor(rparts[:, 2, 0:3], rest, rparts[:, 1, 0:3], ALU.subtract).then_inc(S["rp_done"], 1)
            gathered(0)
            tokens_low(0)
            lows(0, *range(1, AHEAD))
            def further_steps():
                dve.wait_ge(S["ex_out"], 2)
                own(v.tensor_reduce(gsum, gex, AX, ALU.add))
                own(v.tensor_scalar(dn, d21, 1.0, None, ALU.add))
                own.wait()
                own(v.reciprocal(gp, gsum))
                own(v.reciprocal(gi, dn))
                own.wait()
                then(v.tensor_tensor(wt[:, 0, :], gp, gi, ALU.mult))
                own(v.tensor_tensor(wt[:, 1, :], wt[:, 0, :], d21, ALU.mult))
                then(v.tensor_scalar(ov, cnt, float(SLOTS), None, ALU.is_gt))
                for c in range(2, -(-NT // SLOTS)):
                    then(v.scalar_tensor_tensor(out=ov, in0=cnt, scalar=float(c * SLOTS), in1=ov, op0=ALU.is_gt,
                                                op1=ALU.add))
                then(v.tensor_tensor_scan(ovc, con[:, C_ONE:C_ONE + NE], ov, 0.0, ALU.mult, ALU.add))
                own(v.tensor_tensor(ovx, ovc, ov, ALU.subtract))
                own(v.tensor_tensor(sel, each(ovc, MAXOV), wide(con[:, C_I64:C_I64 + MAXOV], NE), ALU.is_le))
                own.wait()
                then(v.tensor_reduce(se, sel, AX, ALU.add))
                then(v.tensor_tensor(sel, sel, each(ov, MAXOV), ALU.mult))
                then(v.tensor_reduce(so, sel, AX, ALU.add))
                then(v.tensor_tensor(so, con[:, C_I64:C_I64 + MAXOV], so, ALU.subtract))
                own(v.tensor_scalar(so, so, 1.0, float(SLOTS), ALU.add, ALU.mult))
                own(v.tensor_scalar(se, se, float(NE - 1), None, ALU.min))
                own.wait()
                own(v.tensor_copy(ints[:, 0:MAXOV], se[0:1, :]))
                own.wait()
                v.tensor_copy(ints[:, MAXOV:MAXOV + 1], ovc[0:1, NE - 1:NE]).then_inc(S["ints_ready"], 1)

            def row_numbers():
                for c, M in enumerate((M1, M2)):
                    then(v.tensor_tensor(tmp, rank, M, ALU.mult))
                    own(v.tensor_reduce(rr[:, c, :], tmp, AX, ALU.add))
                    then(v.tensor_tensor(gmask, M, each(ovx, 3), ALU.mult))
                    then(v.tensor_reduce(ro[:, c, :], gmask, AX, ALU.add))
                then(v.tensor_tensor(ro, ro, ei, ALU.subtract))
                own(v.tensor_scalar(ro, ro, float(NE - 1), float(SLOTS), ALU.add, ALU.mult))
                own(v.tensor_scalar(tmp[:, 0:2, 0:3], rr, float(SLOTS), None, ALU.is_ge))
                own.wait()
                own(v.tensor_tensor(ro, ro, tmp[:, 0:2, 0:3], ALU.mult))
                then(v.scalar_tensor_tensor(out=rr, in0=ei, scalar=float(SLOTS), in1=rr, op0=ALU.mult, op1=ALU.add))
                then(v.tensor_tensor(rr, rr, ro, ALU.add))
                v.tensor_copy(rows[:, 0:6].rearrange("p (t c) -> p c t", c=2), rr).then_inc(S["rows_ready"], 1)

            def expert(s, nxt, last=False):
                if nxt:
                    dve.wait_ge(S["hg_ps"], s + 1)
                    for t, n in enumerate(TILES):
                        choose(rk[0:n, t, ds(s + 1, 1)], t, n)
                lows(s, *range(AHEAD, 11))
                dve.wait_ge(S["g_low"], s + 1)
                v.tensor_tensor(g_sb[:], g_sb[:], ps[2][0:SLOTS, :], ALU.add).then_inc(S["g_sum"], 1)
                lows(s, *range(11, 18))
                dve.wait_ge(S["u_low"], s + 1)
                v.tensor_tensor(u_sb[:], u_sb[:], ps[3][0:SLOTS, :], ALU.add).then_inc(S["u_sum"], 1)
                dve.wait_ge(S["u_sum"], s + 1)
                dve.wait_ge(S["silu_done"], s + 1)
                v.scalar_tensor_tensor(out=g_sb[:], in0=u_sb[:], scalar=stat[0:SLOTS, 24:25], in1=g_sb[:],
                                       op0=ALU.mult, op1=ALU.mult).then_inc(S["a_ready"], 1)
                lows(s, 18)
                if nxt:
                    gathered(s + 1)
                if last:
                    further_steps()
                dve.wait_ge(S["aTh_done"], s + 1)
                v.tensor_tensor(aTx[:, :, SLOTS:], ps[2][:, 0:FT * SLOTS].rearrange("p (f n) -> p f n", f=FT),
                                aTx[:, :, 0:SLOTS].bitcast(F32), ALU.subtract).then_inc(S["aTl_done"], 1)
                lows(s, 19)
                if nxt:
                    tokens_low(s + 1)
                lows(s, 20, 21, 22, 23)
                if nxt:
                    lows(s, *range(CH, CH + AHEAD))
                if last:
                    row_numbers()
                for q in range(4):
                    dve.wait_ge(S["y_act"], s * 4 + (q + 2))
                    y = y_sb[:, q * 512:(q + 1) * 512]
                    v.tensor_tensor(y, y, ps[4 + q][0:SLOTS, :], ALU.add).then_inc(S["y_dve"], 1)

            with dve.Fori(0, NE - 1) as e:
                expert(e, True)
            expert(NE - 1, False, True)
            dve.wait_ge(S["ints_ready"], 1)
            more = dve.value_load(ints[0:1, MAXOV:MAXOV + 1], min_val=0, max_val=MAXOV)
            with dve.If(more > 0):
                with dve.Fori(0, more) as i:
                    e = dve.value_load(ints[0:1, ds(i, 1)], min_val=0, max_val=NE - 1)
                    dve.wait_ge(S["hg_ps"], i + NE)
                    v.tensor_scalar(rko[:, 0:3].rearrange("p (k a) -> p k a", a=1), rk[:, :, ds(e, 1)],
                                    so[:, ds(i, 1)], None, ALU.subtract).then_inc(S["rko_done"], 1)
                    dve.wait_ge(S["rko_done"], i + 1)
                    for t, n in enumerate(TILES):
                        choose(rko[0:n, t:t + 1], t, n)
                    gathered(i + NE)
                    tokens_low(i + NE)
                    lows(i + NE, *range(AHEAD))
                    expert(i + NE, False)
            dve.wait_ge(S["gf_in"], 16)
            for t, n in enumerate(TILES):
                dve.wait_ge(S[f"y_in{t}"], 32)
                dve.wait_ge(S["x2_back"], t + 1)
                for q in range(4):
                    y = ya[t][0:n, q * 512:(q + 1) * 512]
                    v.scalar_tensor_tensor(out=y, in0=y, scalar=wt[0:n, 0, t:t + 1], in1=ps[4 * t % 8 + q][0:n, :],
                                           op0=ALU.mult, op1=ALU.add).then_inc(S["half_done"], 1)
                dve.wait_ge(S["half_done"], 4 * t + 4)
                v.scalar_tensor_tensor(out=ya[t][0:n], in0=yb[t][0:n], scalar=wt[0:n, 1, t:t + 1], in1=ya[t][0:n],
                                       op0=ALU.mult, op1=ALU.add).then_inc(S["sum_done"], 1)
            for t, n in enumerate(TILES):
                dve.wait_ge(S["ssq3"], t + 1)
                v.tensor_scalar(stat[0:n, 4 + t:5 + t], stat[0:n, t:t + 1], 1.0 / D, EPS, ALU.mult, ALU.add)\
                    .then_inc(S["rms"], 1)
                dve.wait_ge(S["rms"], 6 + 2 * t)
                inverse(n, t, t + 1)
                v.scalar_tensor_tensor(out=ya[t][0:n], in0=ya[t][0:n], scalar=stat[0:n, 8 + t:9 + t], in1=gfin[0:n],
                                       op0=ALU.mult, op1=ALU.mult).then_inc(S["fin"], 1)


_INS = """x_prompt x_sample cache_sb_k cache_sb_v cache_swa_k cache_swa_v w_in b_gate swa_sink w_sb_o w_swa_o w_out
g_mix g_ffn w_rg b_rg w_re b_re w_e_gate w_e_up w_e_down g_final""".split()
_OUTS = [(1, SEQ, D), (1, DEC, D), (4, SEQ, 512), (4, DEC, 512), (P, 512), (DEC, 512), (2, PAST - DEC, KV * HD)]


def kernel(**inputs):
    import concourse.bacc as bacc
    from concourse.bass_utils import run_bass_kernel_spmd

    nc = bacc.Bacc("TRN2", target_bir_lowering=False, num_devices=1)
    arrays, args = {}, []
    for name, a in [(n, inputs[n]) for n in _INS] + [("const", constants())]:
        a = np.ascontiguousarray(a)
        arrays[f"in_{name}"] = a
        args.append(nc.dram_tensor(f"in_{name}", a.shape, F32, kind="ExternalInput").ap())
    for i, shape in enumerate(_OUTS):
        args.append(nc.dram_tensor(f"out_{i}", shape, F32, kind="ExternalOutput").ap())
    build(nc, *args)
    r = run_bass_kernel_spmd(nc, [arrays], core_ids=[0])
    yp, ys, kvp, kvs, wp, wn, wk = (r.results[0][f"out_{i}"] for i in range(len(_OUTS)))

    def heads(a, n):
        return a.reshape(1, 1, a.shape[0], n, HD)

    halves = [np.concatenate([x[2 * n], x[2 * n + 1]], axis=1) for x in (kvp, kvs) for n in range(2)]
    w = KV * HD
    return (yp, ys, heads(halves[0], H), heads(halves[1], H), heads(wp[:, :w], KV), heads(wp[:, w:], KV),
            heads(halves[2], H), heads(halves[3], H),
            heads(np.concatenate([wk[0], wn[:, :w]]), KV), heads(np.concatenate([wk[1], wn[:, w:]]), KV))
```
